# Optimizing a Trainium2 kernel written in Bass

```python
import math
import jax, jax.numpy as jnp
from jax import lax
import numpy as np

D_MODEL = 1024
BATCH = 1
SEQ = 256
DEPTH = 2

N_MIXERS = 2
ROPE_THETA = 500000.0
ROT_DIM = 16
Q_BLOCK = 128
NORM_EPS = 1e-6
NEG_INF = -1e30

DA_HEAD_DIM = 64
DA_V_DIM = 2 * DA_HEAD_DIM
DA_HEADS = D_MODEL // DA_V_DIM

NSA_HEAD_DIM = 64
NSA_HEADS = D_MODEL // NSA_HEAD_DIM
NSA_KV_GROUPS = 2
NSA_HEADS_PER_GROUP = NSA_HEADS // NSA_KV_GROUPS
NSA_CMP_BLOCK = 32
NSA_CMP_STRIDE = 16
NSA_CMP_HIDDEN = 4 * NSA_HEAD_DIM
NSA_SEL_BLOCK = 64
NSA_TOP_N = 16
NSA_WINDOW = 512
NSA_FORCE = 1e4
NSA_IN_DIM = NSA_HEADS * NSA_HEAD_DIM + 6 * NSA_KV_GROUPS * NSA_HEAD_DIM + 3 * NSA_HEADS

MOE_GROUPS = 4
MOE_EXPERTS_PER_GROUP = 8
MOE_EXPERTS = MOE_GROUPS * MOE_EXPERTS_PER_GROUP
MOE_TOP_K = 2
MOE_HIDDEN = D_MODEL // 4


def _rmsnorm(x, g):
    xf = x.astype(jnp.float32)
    y = xf * lax.rsqrt(jnp.mean(xf * xf, axis=-1, keepdims=True) + NORM_EPS)
    return (y * g.astype(jnp.float32)).astype(x.dtype)

def _rope_tables(positions):
    inv_freq = ROPE_THETA ** (-jnp.arange(0, ROT_DIM, 2, dtype=jnp.float32) / ROT_DIM)
    ang = positions.astype(jnp.float32)[..., None] * inv_freq
    return jnp.cos(ang)[:, :, None, :], jnp.sin(ang)[:, :, None, :]

def _rotary(x, cos, sin):
    half = ROT_DIM // 2
    xr = x[..., :ROT_DIM].astype(jnp.float32)
    x1, x2 = xr[..., :half], xr[..., half:]
    rot = jnp.concatenate([x1 * cos - x2 * sin, x2 * cos + x1 * sin], axis=-1).astype(x.dtype)
    return jnp.concatenate([rot, x[..., ROT_DIM:]], axis=-1)

def _masked_softmax(s, mask):
    s = jnp.where(mask, s.astype(jnp.float32), NEG_INF)
    p = jnp.where(mask, jnp.exp(s - jnp.max(s, axis=-1, keepdims=True)), 0.0)
    return p / jnp.maximum(jnp.sum(p, axis=-1, keepdims=True), 1e-30)

def diff_attention(h, cos, sin, w_in, w_out, lam, subln_g, lambda_init):
    B, S, D = h.shape
    H, d = DA_HEADS, DA_HEAD_DIM
    q, k, v = jnp.split(h @ w_in, 3, axis=-1)
    q = _rotary(q.reshape(B, S, 2 * H, d), cos, sin).reshape(B, S, H, 2, d).transpose(3, 0, 2, 1, 4)
    k = _rotary(k.reshape(B, S, 2 * H, d), cos, sin).reshape(B, S, H, 2, d).transpose(3, 0, 2, 1, 4)
    v = v.reshape(B, S, H, DA_V_DIM).transpose(0, 2, 1, 3)
    lam = lam.astype(jnp.float32)
    lam_full = jnp.exp(jnp.sum(lam[0] * lam[1])) - jnp.exp(jnp.sum(lam[2] * lam[3])) + lambda_init
    scale = d ** -0.5
    k_pos = jnp.arange(S)

    def block(i):
        q0 = i * Q_BLOCK
        qb = lax.dynamic_slice_in_dim(q, q0, Q_BLOCK, axis=3)
        s = jnp.einsum('cbhqd,cbhkd->cbhqk', qb, k) * scale
        mask = k_pos[None, :] <= (q0 + jnp.arange(Q_BLOCK))[:, None]
        p = _masked_softmax(s, mask)
        a = p[0] - lam_full * p[1]
        return jnp.einsum('bhqk,bhkv->bhqv', a.astype(v.dtype), v)

    o = lax.map(block, jnp.arange(S // Q_BLOCK))
    o = o.transpose(1, 0, 3, 2, 4).reshape(B, S, H, DA_V_DIM)
    o = _rmsnorm(o, subln_g) * (1.0 - lambda_init)
    return o.reshape(B, S, D) @ w_out

def _nsa_compress(t, pos_emb, w1, b1, w2):
    B, G, S, d = t.shape
    ch = t.reshape(B, G, S // NSA_CMP_STRIDE, NSA_CMP_STRIDE, d)
    blk = jnp.concatenate([ch[:, :, :-1], ch[:, :, 1:]], axis=3) + pos_emb
    blk = blk.reshape(B, G, blk.shape[2], NSA_CMP_BLOCK * d)
    return jax.nn.gelu(blk @ w1 + b1) @ w2

def nsa_attention(h, cos, sin, w_in, w_out, cmp_pos, cmp_w1, cmp_b1, cmp_w2):
    B, S, D = h.shape
    H, G, Hg, d = NSA_HEADS, NSA_KV_GROUPS, NSA_HEADS_PER_GROUP, NSA_HEAD_DIM
    kvw = G * d
    proj = h @ w_in
    bounds = [H * d + j * kvw for j in range(7)]
    q, k_c, v_c, k_s, v_s, k_w, v_w, g_raw = jnp.split(proj, bounds, axis=-1)
    q = _rotary(q.reshape(B, S, H, d), cos, sin).reshape(B, S, G, Hg, d).transpose(0, 2, 3, 1, 4)

    def kv(t, rope):
        t = t.reshape(B, S, G, d)
        if rope:
            t = _rotary(t, cos, sin)
        return t.transpose(0, 2, 1, 3)

    k_c, v_c = kv(k_c, False), kv(v_c, False)
    k_s, v_s = kv(k_s, True), kv(v_s, True)
    k_w, v_w = kv(k_w, True), kv(v_w, True)
    gates = jax.nn.sigmoid(g_raw.astype(jnp.float32)).reshape(B, S, G, Hg, 3).transpose(0, 2, 3, 1, 4)

    k_cmp = _nsa_compress(k_c, cmp_pos[0], cmp_w1[0], cmp_b1[0], cmp_w2[0])
    v_cmp = _nsa_compress(v_c, cmp_pos[1], cmp_w1[1], cmp_b1[1], cmp_w2[1])
    n_cmp = k_cmp.shape[2]
    n_sel = S // NSA_SEL_BLOCK
    n_top = min(NSA_TOP_N, n_sel)
    cmp_start = jnp.arange(n_cmp) * NSA_CMP_STRIDE
    cmp_end = cmp_start + NSA_CMP_BLOCK - 1
    sel_start = jnp.arange(n_sel) * NSA_SEL_BLOCK
    cmp_to_sel = ((cmp_start[:, None] < sel_start[None, :] + NSA_SEL_BLOCK)
                  & (cmp_start[:, None] + NSA_CMP_BLOCK > sel_start[None, :])).astype(jnp.float32)
    k_blocks = k_s.reshape(B, G, n_sel, NSA_SEL_BLOCK, d)
    v_blocks = v_s.reshape(B, G, n_sel, NSA_SEL_BLOCK, d)
    pad = ((0, 0), (0, 0), (NSA_WINDOW, 0), (0, 0))
    k_w_pad, v_w_pad = jnp.pad(k_w, pad), jnp.pad(v_w, pad)
    b_ix = jnp.arange(B)[:, None, None, None]
    g_ix = jnp.arange(G)[None, :, None, None]
    blk_off = jnp.arange(NSA_SEL_BLOCK)
    sel_ids = jnp.arange(n_sel)
    scale = d ** -0.5

    def block(i):
        q0 = i * Q_BLOCK
        tq = q0 + jnp.arange(Q_BLOCK)
        qb = lax.dynamic_slice_in_dim(q, q0, Q_BLOCK, axis=3)
        s_c = jnp.einsum('bghqd,bgnd->bghqn', qb, k_cmp) * scale
        p_c = _masked_softmax(s_c, cmp_end[None, :] <= tq[:, None])
        o_c = jnp.einsum('bghqn,bgnd->bghqd', p_c.astype(v_cmp.dtype), v_cmp)
        imp = jnp.einsum('bgqn,ns->bgqs', p_c.sum(axis=2), cmp_to_sel)
        q_blk = tq // NSA_SEL_BLOCK
        forced = ((sel_ids[None, :] == 0) | (sel_ids[None, :] == q_blk[:, None])
                  | (sel_ids[None, :] == q_blk[:, None] - 1))
        causal = sel_ids[None, :] <= q_blk[:, None]
        imp = jnp.where(forced, NSA_FORCE, jnp.where(causal, imp, -NSA_FORCE))
        _, sel = lax.top_k(imp, n_top)
        k_sel = k_blocks[b_ix, g_ix, sel].reshape(B, G, Q_BLOCK, n_top * NSA_SEL_BLOCK, d)
        v_sel = v_blocks[b_ix, g_ix, sel].reshape(B, G, Q_BLOCK, n_top * NSA_SEL_BLOCK, d)
        tok = (sel[..., None] * NSA_SEL_BLOCK + blk_off).reshape(B, G, Q_BLOCK, n_top * NSA_SEL_BLOCK)
        s_s = jnp.einsum('bghqd,bgqkd->bghqk', qb, k_sel) * scale
        p_s = _masked_softmax(s_s, tok[:, :, None] <= tq[:, None])
        o_s = jnp.einsum('bghqk,bgqkd->bghqd', p_s.astype(v_sel.dtype), v_sel)
        k_win = lax.dynamic_slice_in_dim(k_w_pad, q0, Q_BLOCK + NSA_WINDOW, axis=2)
        v_win = lax.dynamic_slice_in_dim(v_w_pad, q0, Q_BLOCK + NSA_WINDOW, axis=2)
        tk = q0 - NSA_WINDOW + jnp.arange(Q_BLOCK + NSA_WINDOW)
        dist = tq[:, None] - tk[None, :]
        mask_w = (tk[None, :] >= 0) & (dist >= 0) & (dist < NSA_WINDOW)
        s_w = jnp.einsum('bghqd,bgkd->bghqk', qb, k_win) * scale
        p_w = _masked_softmax(s_w, mask_w)
        o_w = jnp.einsum('bghqk,bgkd->bghqd', p_w.astype(v_win.dtype), v_win)
        gb = lax.dynamic_slice_in_dim(gates, q0, Q_BLOCK, axis=3)
        o = gb[..., 0:1] * o_c + gb[..., 1:2] * o_s + gb[..., 2:3] * o_w
        return o.astype(h.dtype)

    o = lax.map(block, jnp.arange(S // Q_BLOCK))
    o = o.transpose(1, 0, 4, 2, 3, 5).reshape(B, S, D)
    return o @ w_out

def hier_moe(h, w_grp, b_grp, w_exp, b_exp, w_gate, w_up, w_down):
    B, S, D = h.shape
    t = h.reshape(B * S, D)
    T = t.shape[0]
    pg = jax.nn.softmax((t @ w_grp).astype(jnp.float32) + b_grp, axis=-1)
    p_top, grp = lax.top_k(pg, 1)
    le = jnp.einsum('td,gde->tge', t, w_exp).astype(jnp.float32) + b_exp
    le_sel = le[jnp.arange(T), grp[:, 0]]
    val, idx = lax.top_k(le_sel, MOE_TOP_K)
    wts = jax.nn.softmax(val, axis=-1) * p_top
    eid = grp * MOE_EXPERTS_PER_GROUP + idx
    combine = jnp.sum(jax.nn.one_hot(eid, MOE_EXPERTS, dtype=jnp.float32) * wts[..., None], axis=1)
    y = jnp.zeros_like(t)
    for gi in range(MOE_GROUPS):
        sl = slice(gi * MOE_EXPERTS_PER_GROUP, (gi + 1) * MOE_EXPERTS_PER_GROUP)
        a = jax.nn.silu(jnp.einsum('td,edh->teh', t, w_gate[sl])) * jnp.einsum('td,edh->teh', t, w_up[sl])
        a = a * combine[:, sl, None].astype(a.dtype)
        y = y + jnp.einsum('teh,ehd->td', a, w_down[sl]).astype(t.dtype)
    return y.reshape(B, S, D)

def first_inputs(seed: int = 0) -> dict:
    key = jax.random.key(seed)
    ks = iter(jax.random.split(key, 32))
    D = D_MODEL
    n_a = (DEPTH + N_MIXERS - 1) // N_MIXERS
    n_b = DEPTH // N_MIXERS

    def nrm(shape, scale):
        return jax.random.normal(next(ks), shape, jnp.float32) * scale

    return {
        'x': nrm((BATCH, SEQ, D), 1.0),
        'c': nrm((BATCH, D), 1.0),
        'positions': (jax.random.randint(next(ks), (BATCH, 1), 0, 4096) + jnp.arange(SEQ)[None, :]).astype(jnp.int32),
        'ada_w': nrm((DEPTH, D, 6 * D), 0.5 * D ** -0.5),
        'ada_b': nrm((DEPTH, 6 * D), 0.02),
        'norm_g': 1.0 + nrm((DEPTH, 2, D), 0.02),
        'final_g': 1.0 + nrm((D,), 0.02),
        'diff_w_in': nrm((n_a, D, 3 * D), D ** -0.5),
        'diff_w_out': nrm((n_a, D, D), D ** -0.5),
        'diff_lambda': nrm((n_a, 4, DA_HEAD_DIM), 0.1),
        'diff_subln_g': 1.0 + nrm((n_a, DA_V_DIM), 0.02),
        'nsa_w_in': nrm((n_b, D, NSA_IN_DIM), D ** -0.5),
        'nsa_w_out': nrm((n_b, D, D), D ** -0.5),
        'nsa_cmp_pos': nrm((n_b, 2, NSA_CMP_BLOCK, NSA_HEAD_DIM), 0.02),
        'nsa_cmp_w1': nrm((n_b, 2, NSA_CMP_BLOCK * NSA_HEAD_DIM, NSA_CMP_HIDDEN), (NSA_CMP_BLOCK * NSA_HEAD_DIM) ** -0.5),
        'nsa_cmp_b1': nrm((n_b, 2, NSA_CMP_HIDDEN), 0.02),
        'nsa_cmp_w2': nrm((n_b, 2, NSA_CMP_HIDDEN, NSA_HEAD_DIM), NSA_CMP_HIDDEN ** -0.5),
        'moe_w_group': nrm((DEPTH, D, MOE_GROUPS), D ** -0.5),
        'moe_b_group': nrm((DEPTH, MOE_GROUPS), 0.01),
        'moe_w_expert': nrm((DEPTH, MOE_GROUPS, D, MOE_EXPERTS_PER_GROUP), D ** -0.5),
        'moe_b_expert': nrm((DEPTH, MOE_GROUPS, MOE_EXPERTS_PER_GROUP), 0.01),
        'moe_w_gate': nrm((DEPTH, MOE_EXPERTS, D, MOE_HIDDEN), D ** -0.5),
        'moe_w_up': nrm((DEPTH, MOE_EXPERTS, D, MOE_HIDDEN), D ** -0.5),
        'moe_w_down': nrm((DEPTH, MOE_EXPERTS, MOE_HIDDEN, D), MOE_HIDDEN ** -0.5),
    }

def first_block(x, c, positions, ada_w, ada_b, norm_g, final_g,
              diff_w_in, diff_w_out, diff_lambda, diff_subln_g,
              nsa_w_in, nsa_w_out, nsa_cmp_pos, nsa_cmp_w1, nsa_cmp_b1, nsa_cmp_w2,
              moe_w_group, moe_b_group, moe_w_expert, moe_b_expert,
              moe_w_gate, moe_w_up, moe_w_down):
    cos, sin = _rope_tables(positions)
    c_act = jax.nn.silu(c)
    for i in range(DEPTH):
        mod = c_act @ ada_w[i] + ada_b[i]
        sh1, sc1, g1, sh2, sc2, g2 = jnp.split(mod[:, None, :], 6, axis=-1)
        h = _rmsnorm(x, norm_g[i, 0]) * (1.0 + sc1) + sh1
        j = i // N_MIXERS
        if i % N_MIXERS == 0:
            lambda_init = 0.8 - 0.6 * math.exp(-0.3 * i)
            mix = diff_attention(h, cos, sin, diff_w_in[j], diff_w_out[j], diff_lambda[j],
                                 diff_subln_g[j], lambda_init)
        else:
            mix = nsa_attention(h, cos, sin, nsa_w_in[j], nsa_w_out[j], nsa_cmp_pos[j],
                                nsa_cmp_w1[j], nsa_cmp_b1[j], nsa_cmp_w2[j])
        x = x + g1 * mix
        h = _rmsnorm(x, norm_g[i, 1]) * (1.0 + sc2) + sh2
        x = x + g2 * hier_moe(h, moe_w_group[i], moe_b_group[i], moe_w_expert[i], moe_b_expert[i],
                              moe_w_gate[i], moe_w_up[i], moe_w_down[i])
    return _rmsnorm(x, final_g)


GRID_W = 64
ROPE_THETA_2 = 10000.0
EPS = 1e-6
PLE_DIM = 256

MLA_HEADS = 8
MLA_Q_LORA = 256
MLA_KV_LORA = 128
MLA_NOPE = 64
MLA_ROPE = 32
MLA_V = 64

GLA_HEADS = 4
GLA_DK = 64
GLA_DV = 128
GLA_GATE_RANK = 16
GLA_GATE_NORM = 16.0
GLA_CHUNK = 64

GQA_HEADS = 16
GQA_KV_HEADS = 4
GQA_HEAD_DIM = 64

N_EXPERTS = 16
EC_CAPACITY_FACTOR = 2
EXPERT_FF = 1024

D_MIX = MLA_HEADS * MLA_V + GLA_HEADS * GLA_DV
EVEN_SPLITS = (MLA_Q_LORA, MLA_KV_LORA, MLA_ROPE,
               GLA_HEADS * GLA_DK, GLA_HEADS * GLA_DK, GLA_HEADS * GLA_DV,
               2 * GLA_GATE_RANK, GLA_HEADS * GLA_DV)
ODD_SPLITS = (GQA_HEADS * GQA_HEAD_DIM, GQA_KV_HEADS * GQA_HEAD_DIM, GQA_KV_HEADS * GQA_HEAD_DIM)
N_EVEN = (DEPTH + 1) // 2
N_ODD = DEPTH // 2
DEEPNORM_ALPHA = (2.0 * DEPTH) ** 0.25
DEEPNORM_BETA = (8.0 * DEPTH) ** -0.25


def _split(h, sizes):
    offs = np.cumsum(sizes)[:-1].tolist()
    return jnp.split(h, offs, axis=-1)

def rms_norm(x, g):
    x32 = x.astype(jnp.float32)
    y = x32 * lax.rsqrt(jnp.mean(x32 * x32, axis=-1, keepdims=True) + EPS)
    return (y * g.astype(jnp.float32)).astype(x.dtype)

def layer_norm(x, g, b):
    x32 = x.astype(jnp.float32)
    mu = jnp.mean(x32, axis=-1, keepdims=True)
    xc = x32 - mu
    var = jnp.mean(xc * xc, axis=-1, keepdims=True)
    y = xc * lax.rsqrt(var + EPS) * g.astype(jnp.float32) + b.astype(jnp.float32)
    return y.astype(x.dtype)

def axial_rope(seq, rot_dim):
    rows = seq // GRID_W
    row = jnp.repeat(jnp.arange(rows, dtype=jnp.float32), GRID_W)
    col = jnp.tile(jnp.arange(GRID_W, dtype=jnp.float32), rows)
    axis_dim = rot_dim // 2
    inv = ROPE_THETA_2 ** (-jnp.arange(0, axis_dim, 2, dtype=jnp.float32) / axis_dim)
    ang = jnp.concatenate([row[:, None] * inv, col[:, None] * inv], axis=-1)
    return jnp.cos(ang), jnp.sin(ang)

def apply_rope(x, cos, sin):
    half = x.shape[-1] // 2
    c = cos.astype(x.dtype)
    s = sin.astype(x.dtype)
    x1, x2 = x[..., :half], x[..., half:]
    return jnp.concatenate([x1 * c - x2 * s, x1 * s + x2 * c], axis=-1)

def _to_blocks(t):
    b, s = t.shape[:2]
    nb = s // Q_BLOCK
    return t.reshape((b, nb, Q_BLOCK) + t.shape[2:]).swapaxes(0, 1)

def _from_blocks(t):
    nb, b, qb = t.shape[:3]
    return t.swapaxes(0, 1).reshape((b, nb * qb) + t.shape[3:])

def mla_attention(q_nope, q_pe, k_nope, k_pe, v):
    scale = (MLA_NOPE + MLA_ROPE) ** -0.5

    def block(args):
        qn, qp = args
        s = (jnp.einsum('bqhd,bkhd->bhqk', qn, k_nope)
             + jnp.einsum('bqhd,bkd->bhqk', qp, k_pe)) * scale
        pr = jax.nn.softmax(s.astype(jnp.float32), axis=-1).astype(v.dtype)
        return jnp.einsum('bhqk,bkhd->bqhd', pr, v)

    o = lax.map(block, (_to_blocks(q_nope), _to_blocks(q_pe)))
    return _from_blocks(o)

def gla_chunked(q, k, v, log_a):
    b, s, h, dk = q.shape
    dv = v.shape[-1]
    n = s // GLA_CHUNK
    L = GLA_CHUNK

    def chunk(t):
        return t.astype(jnp.float32).reshape(b, n, L, h, t.shape[-1]).transpose(0, 3, 1, 2, 4)

    qc, kc, vc, lac = chunk(q), chunk(k), chunk(v), chunk(log_a)
    cum = jnp.cumsum(lac, axis=-2)
    qg = qc * jnp.exp(cum)
    kg = kc * jnp.exp(-cum)
    tri = jnp.tril(jnp.ones((L, L), dtype=bool))
    att = jnp.where(tri, jnp.einsum('bhnld,bhnmd->bhnlm', qg, kg), 0.0)
    o_intra = jnp.einsum('bhnlm,bhnme->bhnle', att, vc)
    last = cum[..., -1:, :]
    u = jnp.einsum('bhnld,bhnle->bhnde', kc * jnp.exp(last - cum), vc)
    decay = jnp.exp(last[..., 0, :])

    def step(state, inp):
        d, du = inp
        return d[..., None] * state + du, state

    init = jnp.zeros((b, h, dk, dv), jnp.float32)
    _, s_prev = lax.scan(step, init, (jnp.moveaxis(decay, 2, 0), jnp.moveaxis(u, 2, 0)))
    o_inter = jnp.einsum('bhnld,nbhde->bhnle', qg, s_prev)
    o = (o_intra + o_inter).transpose(0, 2, 3, 1, 4).reshape(b, s, h, dv)
    return o.astype(v.dtype)

def even_mixer(x, w_in, mla_q_norm, w_uq, mla_kv_norm, w_ukv,
               gla_gate_w_fwd, gla_gate_b_fwd, gla_gate_w_bwd, gla_gate_b_bwd, gla_norm,
               cos_a, sin_a):
    b, s, _ = x.shape
    h = x @ w_in
    c_q, c_kv, k_pe, gq, gk, gv, g_lr, gr = _split(h, EVEN_SPLITS)

    q = (rms_norm(c_q, mla_q_norm) @ w_uq).reshape(b, s, MLA_HEADS, MLA_NOPE + MLA_ROPE)
    q_nope = q[..., :MLA_NOPE]
    q_pe = apply_rope(q[..., MLA_NOPE:], cos_a[:, None, :], sin_a[:, None, :])
    kv = (rms_norm(c_kv, mla_kv_norm) @ w_ukv).reshape(b, s, MLA_HEADS, MLA_NOPE + MLA_V)
    k_nope, v_mla = kv[..., :MLA_NOPE], kv[..., MLA_NOPE:]
    k_pe = apply_rope(k_pe, cos_a, sin_a)
    o_mla = mla_attention(q_nope, q_pe, k_nope, k_pe, v_mla).reshape(b, s, MLA_HEADS * MLA_V)

    qh = (gq * (GLA_DK ** -0.5)).reshape(b, s, GLA_HEADS, GLA_DK)
    kh = gk.reshape(b, s, GLA_HEADS, GLA_DK)
    vh = gv.reshape(b, s, GLA_HEADS, GLA_DV)
    lr_f, lr_b = g_lr[..., :GLA_GATE_RANK], g_lr[..., GLA_GATE_RANK:]
    la_f = (jax.nn.log_sigmoid((lr_f @ gla_gate_w_fwd + gla_gate_b_fwd).astype(jnp.float32))
            / GLA_GATE_NORM).reshape(b, s, GLA_HEADS, GLA_DK)
    la_b = (jax.nn.log_sigmoid((lr_b @ gla_gate_w_bwd + gla_gate_b_bwd).astype(jnp.float32))
            / GLA_GATE_NORM).reshape(b, s, GLA_HEADS, GLA_DK)
    o_f = gla_chunked(qh, kh, vh, la_f)
    flip = lambda t: jnp.flip(t, axis=1)
    o_b = flip(gla_chunked(flip(qh), flip(kh), flip(vh), flip(la_b)))
    o_gla = rms_norm(o_f + o_b, gla_norm).reshape(b, s, GLA_HEADS * GLA_DV) * jax.nn.silu(gr)

    return jnp.concatenate([o_mla, o_gla], axis=-1)

def odd_mixer(x, w_in, gqa_q_norm, gqa_k_norm, cos_c, sin_c):
    b, s, _ = x.shape
    g = GQA_HEADS // GQA_KV_HEADS
    q, k, v = _split(x @ w_in, ODD_SPLITS)
    q = rms_norm(q.reshape(b, s, GQA_HEADS, GQA_HEAD_DIM), gqa_q_norm)
    k = rms_norm(k.reshape(b, s, GQA_KV_HEADS, GQA_HEAD_DIM), gqa_k_norm)
    v = v.reshape(b, s, GQA_KV_HEADS, GQA_HEAD_DIM)
    q = apply_rope(q, cos_c[:, None, :], sin_c[:, None, :]).reshape(b, s, GQA_KV_HEADS, g, GQA_HEAD_DIM)
    k = apply_rope(k, cos_c[:, None, :], sin_c[:, None, :])
    scale = GQA_HEAD_DIM ** -0.5

    def block(qb):
        sc = jnp.einsum('bqkgd,bskd->bkgqs', qb, k) * scale
        pr = jax.nn.softmax(sc.astype(jnp.float32), axis=-1).astype(v.dtype)
        return jnp.einsum('bkgqs,bskd->bqkgd', pr, v)

    o = _from_blocks(lax.map(block, _to_blocks(q)))
    return o.reshape(b, s, GQA_HEADS * GQA_HEAD_DIM)

def expert_choice_moe(x, router_w, w1, w3, w2):
    b, s, d = x.shape
    cap = EC_CAPACITY_FACTOR * s // N_EXPERTS
    aff = jax.nn.softmax(jnp.einsum('bsd,de->bse', x, router_w).astype(jnp.float32), axis=-1)
    gates, idx = lax.top_k(aff.transpose(0, 2, 1), cap)
    xg = jax.vmap(lambda xb, ib: xb[ib])(x, idx)
    hid = jax.nn.silu(jnp.einsum('becd,edf->becf', xg, w1)) * jnp.einsum('becd,edf->becf', xg, w3)
    ye = jnp.einsum('becf,efd->becd', hid, w2) * gates[..., None].astype(x.dtype)
    return jax.vmap(lambda yb, ib: jnp.zeros((s, d), x.dtype).at[ib.reshape(-1)].add(yb.reshape(-1, d)))(ye, idx)

def second_inputs(seed: int = 0) -> dict:
    key = jax.random.key(seed)
    ks = iter(jax.random.split(key, 40))
    f32 = jnp.float32

    def nrm(shape, scale):
        return jax.random.normal(next(ks), shape, f32) * scale

    def gain(shape):
        return 1.0 + 0.02 * jax.random.normal(next(ks), shape, f32)

    d_even_in = sum(EVEN_SPLITS)
    d_odd_in = sum(ODD_SPLITS)
    NE, NO = N_EVEN, N_ODD
    return {
        "x": nrm((BATCH, SEQ, D_MODEL), 1.0),
        "p": nrm((DEPTH, BATCH, SEQ, PLE_DIM), 1.0),
        "w_in_even": nrm((NE, D_MODEL, d_even_in), D_MODEL ** -0.5),
        "mla_q_norm": gain((NE, MLA_Q_LORA)),
        "w_uq": nrm((NE, MLA_Q_LORA, MLA_HEADS * (MLA_NOPE + MLA_ROPE)), MLA_Q_LORA ** -0.5),
        "mla_kv_norm": gain((NE, MLA_KV_LORA)),
        "w_ukv": nrm((NE, MLA_KV_LORA, MLA_HEADS * (MLA_NOPE + MLA_V)), MLA_KV_LORA ** -0.5),
        "gla_gate_w_fwd": nrm((NE, GLA_GATE_RANK, GLA_HEADS * GLA_DK), GLA_GATE_RANK ** -0.5),
        "gla_gate_b_fwd": nrm((NE, GLA_HEADS * GLA_DK), 0.1),
        "gla_gate_w_bwd": nrm((NE, GLA_GATE_RANK, GLA_HEADS * GLA_DK), GLA_GATE_RANK ** -0.5),
        "gla_gate_b_bwd": nrm((NE, GLA_HEADS * GLA_DK), 0.1),
        "gla_norm": gain((NE, GLA_DV)),
        "w_in_odd": nrm((NO, D_MODEL, d_odd_in), D_MODEL ** -0.5),
        "gqa_q_norm": gain((NO, GQA_HEAD_DIM)),
        "gqa_k_norm": gain((NO, GQA_HEAD_DIM)),
        "w_o": nrm((DEPTH, D_MIX, D_MODEL), D_MIX ** -0.5 * DEEPNORM_BETA),
        "ln1_g": gain((DEPTH, D_MODEL)),
        "ln1_b": nrm((DEPTH, D_MODEL), 0.02),
        "router_w": nrm((DEPTH, D_MODEL, N_EXPERTS), D_MODEL ** -0.5),
        "w1": nrm((DEPTH, N_EXPERTS, D_MODEL, EXPERT_FF), D_MODEL ** -0.5),
        "w3": nrm((DEPTH, N_EXPERTS, D_MODEL, EXPERT_FF), D_MODEL ** -0.5),
        "w2": nrm((DEPTH, N_EXPERTS, EXPERT_FF, D_MODEL), EXPERT_FF ** -0.5 * DEEPNORM_BETA),
        "ple_gate_w": nrm((DEPTH, D_MODEL, D_MODEL), D_MODEL ** -0.5),
        "ple_gate_b": nrm((DEPTH, D_MODEL), 0.02),
        "ple_w": nrm((DEPTH, PLE_DIM, D_MODEL), PLE_DIM ** -0.5 * DEEPNORM_BETA),
        "ln2_g": gain((DEPTH, D_MODEL)),
        "ln2_b": nrm((DEPTH, D_MODEL), 0.02),
    }

def second_block(x, p, w_in_even, mla_q_norm, w_uq, mla_kv_norm, w_ukv,
              gla_gate_w_fwd, gla_gate_b_fwd, gla_gate_w_bwd, gla_gate_b_bwd, gla_norm,
              w_in_odd, gqa_q_norm, gqa_k_norm,
              w_o, ln1_g, ln1_b, router_w, w1, w3, w2,
              ple_gate_w, ple_gate_b, ple_w, ln2_g, ln2_b):
    seq = x.shape[1]
    cos_a, sin_a = axial_rope(seq, MLA_ROPE)
    cos_c, sin_c = axial_rope(seq, GQA_HEAD_DIM)
    for i in range(DEPTH):
        if i % 2 == 0:
            j = i // 2
            mix = even_mixer(x, w_in_even[j], mla_q_norm[j], w_uq[j], mla_kv_norm[j], w_ukv[j],
                             gla_gate_w_fwd[j], gla_gate_b_fwd[j], gla_gate_w_bwd[j], gla_gate_b_bwd[j],
                             gla_norm[j], cos_a, sin_a)
        else:
            j = i // 2
            mix = odd_mixer(x, w_in_odd[j], gqa_q_norm[j], gqa_k_norm[j], cos_c, sin_c)
        x = layer_norm(DEEPNORM_ALPHA * x + mix @ w_o[i], ln1_g[i], ln1_b[i])
        ffn = expert_choice_moe(x, router_w[i], w1[i], w3[i], w2[i])
        ple = jax.nn.sigmoid(x @ ple_gate_w[i] + ple_gate_b[i]) * (p[i] @ ple_w[i])
        x = layer_norm(DEEPNORM_ALPHA * x + ffn + ple, ln2_g[i], ln2_b[i])
    return x


def setup_inputs(seed=0):
    out = dict(first_inputs(seed))
    for name, value in second_inputs(seed + 1).items():
        if name != "x":
            out[name + "_2"] = value
    return out


def reference(
    x, c, positions, ada_w, ada_b, norm_g, final_g, diff_w_in, diff_w_out, diff_lambda,
    diff_subln_g, nsa_w_in, nsa_w_out, nsa_cmp_pos, nsa_cmp_w1, nsa_cmp_b1, nsa_cmp_w2,
    moe_w_group, moe_b_group, moe_w_expert, moe_b_expert, moe_w_gate, moe_w_up, moe_w_down, p_2,
    w_in_even_2, mla_q_norm_2, w_uq_2, mla_kv_norm_2, w_ukv_2, gla_gate_w_fwd_2,
    gla_gate_b_fwd_2, gla_gate_w_bwd_2, gla_gate_b_bwd_2, gla_norm_2, w_in_odd_2, gqa_q_norm_2,
    gqa_k_norm_2, w_o_2, ln1_g_2, ln1_b_2, router_w_2, w1_2, w3_2, w2_2, ple_gate_w_2,
    ple_gate_b_2, ple_w_2, ln2_g_2, ln2_b_2,
):
    x = first_block(
        x, c, positions, ada_w, ada_b, norm_g, final_g, diff_w_in, diff_w_out, diff_lambda,
        diff_subln_g, nsa_w_in, nsa_w_out, nsa_cmp_pos, nsa_cmp_w1, nsa_cmp_b1, nsa_cmp_w2,
        moe_w_group, moe_b_group, moe_w_expert, moe_b_expert, moe_w_gate, moe_w_up, moe_w_down,
    )
    return second_block(
        x, p_2, w_in_even_2, mla_q_norm_2, w_uq_2, mla_kv_norm_2, w_ukv_2, gla_gate_w_fwd_2,
        gla_gate_b_fwd_2, gla_gate_w_bwd_2, gla_gate_b_bwd_2, gla_norm_2, w_in_odd_2,
        gqa_q_norm_2, gqa_k_norm_2, w_o_2, ln1_g_2, ln1_b_2, router_w_2, w1_2, w3_2, w2_2,
        ple_gate_w_2, ple_gate_b_2, ple_w_2, ln2_g_2, ln2_b_2,
    )


_drawn_inputs = setup_inputs


def setup_inputs(seed=0):
    import zlib

    import numpy as np

    out = dict(_drawn_inputs(seed))
    spreads = {}
    factors = {'diff_lambda': 6.576,
     'diff_subln_g': 3.99,
     'nsa_cmp_pos': 8.0,
     'nsa_cmp_b1': 8.0,
     'moe_b_group': 8.0,
     'moe_b_expert': 6.658,
     'mla_q_norm_2': 8.0,
     'mla_kv_norm_2': 8.0,
     'gla_gate_w_fwd_2': 4.258,
     'gla_gate_b_fwd_2': 8.0,
     'gla_gate_w_bwd_2': 4.289,
     'gla_gate_b_bwd_2': 8.0,
     'gla_norm_2': 8.0,
     'gqa_q_norm_2': 8.0,
     'gqa_k_norm_2': 8.0,
     'ple_gate_b_2': 8.0}
    for name, (base, spread) in spreads.items():
        noise = np.random.default_rng([zlib.crc32(name.encode()), seed]).standard_normal(out[name].shape)
        drawn = base * np.exp(spread * noise) if base else spread * noise
        out[name] = __import__('jax').numpy.asarray(drawn.astype(out[name].dtype))
    for name, factor in factors.items():
        out[name] = (out[name] * factor).astype(out[name].dtype)
    return out
```

```python
import math
from contextlib import ExitStack

import numpy as np

import concourse.bass as bass
from concourse import mybir

F32 = mybir.dt.float32
BF16 = mybir.dt.bfloat16
I32 = mybir.dt.int32
U32 = mybir.dt.uint32
ALU = mybir.AluOpType
ACT = mybir.ActivationFunctionType
AX = mybir.AxisListType.X

P = 128
T = 256
TT = T // P
D = 1024
C = D // P
EPS = 1e-6
NEG = 1e30
RING = 12
SLOT = 2048
ROT_DIM = 16
ALPHA = (2.0 * 2) ** 0.25
LAMBDA_INIT = 0.8 - 0.6 * math.exp(-0.3 * 0)
NSA_Q = 1024
NCMP = T // 16 - 1
E1, TOPK, E1_FF = 32, 2, 256
BLK = 32
E1_BLOCKS = (TOPK * T + E1 * (BLK - 1)) // BLK + 1
E1_GROUPS = E1_BLOCKS // 4
E2, E2_FF = 16, 1024
E2_GROUPS = E2 // 4
assert E1_BLOCKS % 4 == 0

CONST = {}


def _layout():
    at = 0
    for name, n in (("ident", P), ("ones", P), ("ones64", P), ("rot16", P), ("rot64", P), ("rot_mla", P),
                    ("before", P), ("tri_f", P), ("tri_b", P), ("iota", P), ("tri_neg", P),
                    ("cos_m", T), ("sin_m", T), ("cos_g", T), ("sin_g", T),
                    ("cmp_ok", TT * NCMP), ("inv_freq", 1)):
        CONST[name] = (at, n)
        at += n
    return at


N_CONST = _layout()
N_PARAMS = 41


def shape_constants():
    c = np.zeros((P, N_CONST), np.float32)

    def put(name, a):
        at, n = CONST[name]
        c[:a.shape[0], at:at + n] = a

    def rotation(size, base, half, parts):
        r = np.zeros((P, P), np.float32)
        for b in range(base, parts, size):
            for i in range(half):
                r[b + half + i, b + i] = -1.0
                r[b + i, b + half + i] = 1.0
        return r

    i = np.arange(P)
    put("ident", np.eye(P, dtype=np.float32))
    put("ones", np.ones((P, P), np.float32))
    put("ones64", (i[:, None] // 64 == i[None, :] // 64).astype(np.float32))
    put("rot16", rotation(64, 0, ROT_DIM // 2, P))
    put("rot64", rotation(64, 0, 32, P))
    put("rot_mla", rotation(64, 64, 16, P))
    put("before", (i[:, None] < i[None, :]).astype(np.float32))
    same = i[:, None] // 64 == i[None, :] // 64
    put("tri_f", (same & (i[:, None] <= i[None, :])).astype(np.float32))
    put("tri_b", (same & (i[:, None] >= i[None, :])).astype(np.float32))
    put("iota", np.broadcast_to(i.astype(np.float32), (P, P)))
    put("tri_neg", np.where(i[None, :] <= i[:, None], 0.0, -NEG).astype(np.float32))
    t = np.arange(T)

    def axial(rot_dim):
        row, col = (t // 64).astype(np.float32), (t % 64).astype(np.float32)
        axis = rot_dim // 2
        inv = (np.float32(10000.0) ** (-np.arange(0, axis, 2, dtype=np.float32) / np.float32(axis))).astype(np.float32)
        ang = np.concatenate([row[:, None] * inv, col[:, None] * inv], axis=-1)
        return np.cos(ang).astype(np.float32).T, np.sin(ang).astype(np.float32).T

    cos, sin = axial(32)
    cm, sm = np.ones((96, T), np.float32), np.zeros((96, T), np.float32)
    cm[64:96], sm[64:96] = np.tile(cos, (2, 1)), np.tile(sin, (2, 1))
    put("cos_m", cm)
    put("sin_m", sm)
    cos, sin = axial(64)
    put("cos_g", np.tile(cos, (4, 1)))
    put("sin_g", np.tile(sin, (4, 1)))
    end = np.arange(NCMP) * 16 + 31
    put("cmp_ok", np.concatenate([(end[None, :] <= (i + P * tt)[:, None]) for tt in range(TT)], 1).astype(np.float32))
    inv = (np.float32(500000.0) ** (-np.arange(0, ROT_DIM, 2, dtype=np.float32) / np.float32(ROT_DIM))).astype(np.float32)
    put("inv_freq", np.where(i % 64 < ROT_DIM, inv[i % 8], 0.0).astype(np.float32)[:, None])
    return c


def program(nc, A, out):
    ctx = ExitStack()
    with ctx:
        sems = {}

        def S(name):
            if name not in sems:
                sems[name] = ctx.enter_context(nc.semaphore(name))
            return sems[name]

        def sb(name, shape, dt=F32):
            return ctx.enter_context(nc.sbuf_tensor(name, shape, dt))

        ps = ctx.enter_context(nc.psum_tensor("ps", [P, 8, 512], F32))

        ring = sb("ring", [P, RING, SLOT])
        cst = sb("cst", [P, N_CONST])
        xT = sb("xT", [P, C, T])
        hT = sb("hT", [P, C, T])
        qT = sb("qT", [P, C, T])
        kT = sb("kT", [P, C, T])
        vt = sb("vt", [P, 2048])
        oT = sb("oT", [P, C, T])
        yT = sb("yT", [P, C, T])
        sqb = sb("sqb", [P, 1024])
        pb = sb("pb", [P, 2, 512])
        ptb = sb("ptb", [P, 2, 512])
        cosd = sb("cosd", [P, 2, T])
        identb = sb("identb", [P, P], BF16)
        trib = sb("trib", [P, P], BF16)
        colsA = sb("colsA", [P, 3, P])
        rows1 = sb("rows1", [1, 1100])
        wrb = sb("wr", [P, 2 * C * 52])
        gw = sb("gw", [16, 2, T])
        cpad = sb("cpad", [P, C, 32])
        mod = sb("mod", [P, 2, 48])
        modA = sb("modA", [P, 5, C])
        st = sb("st", [P, T])
        pn = sb("pn", [P, 512])
        rtmp = sb("rtmp", [P, 512])
        mx = sb("mx", [P, 2, 8])
        coef = sb("coef", [P, 8])
        gates = sb("gates", [P, TT, 48])
        rt = sb("rt", [P, 1100])
        ids = sb("ids", [1, 2, E1_BLOCKS], I32)
        Lw = sb("Lw", [P, 4, TT])
        affL = sb("affL", [P, 2, TT, E2])
        Dg = sb("Dg", [P, TT, P])
        DAg = sb("DAg", [P, TT, P])
        Cg = sb("Cg", [P, T])
        iog = sb("iog", [P, P])
        i8 = sb("i8", [P, 2, TT, 8], U32)
        misc = sb("misc", [P, 64])

        def K(name, parts=P):
            at, n = CONST[name]
            return cst[0:parts, at:at + n]

        ident = K("ident")
        iota = K("iota")

        h_tok = oT[:, :, :].rearrange("p c t -> p (c t)").rearrange("p (a d) -> p a d", a=TT)
        hid = kT[:, 0:4, :].rearrange("p c t -> p (c t)")
        hidT = kT[:, 4:8, :].rearrange("p c t -> p (c t)").rearrange("p (c s) -> p c s", s=P)
        Yg = qT[:, 0:4, :].rearrange("p c t -> p (c t)")
        xg = ptb[:, :, :].rearrange("p b n -> p (b n)").rearrange("p (k s) -> p k s", k=C)
        sg = pb[:, :, :].rearrange("p b n -> p (b n)")
        sq = kT[:, :, :].rearrange("p c t -> p (c t)")
        rowsA = qT[:, 0:2, :].rearrange("p c t -> p (c t)")[:, 0:3 * P].rearrange("p (a n) -> p a n", a=3)
        posi = yT[:, 2, :].bitcast(I32)
        wr = [wrb[:, C * 36 * m:C * 36 * m + C * 36].rearrange("p (k n) -> p k n", k=C) for m in range(2)]
        wr += [wrb[:, C * (72 + 16 * m):C * (88 + 16 * m)].rearrange("p (k n) -> p k n", k=C) for m in range(2)]
        vtok = vt[:, :].rearrange("p (a n) -> p a n", a=TT)

        def psf(b, n=1, rows=slice(0, P)):
            return ps[rows, b:b + n, :].rearrange("p b n -> p (b n)")

        R1, at = {}, 0
        for name, n in (("c", 8), ("final_g", 8), ("ln1_g_2", 16), ("ln1_b_2", 16), ("ln2_g_2", 16),
                        ("ln2_b_2", 16), ("ple_gate_b_2", 16), ("mla_q_norm_2", 2), ("mla_kv_norm_2", 1),
                        ("gla_norm_2", 1), ("diff_subln_g", 1), ("nsa_cmp_b1", 4), ("gqa_q_norm_2", 1),
                        ("gqa_k_norm_2", 1)):
            R1[name] = (at, n)
            at += n

        def col(name, k=0, parts=slice(0, P)):
            return colsA[parts, 1, R1[name][0] + k:R1[name][0] + k + 1]

        LAM0, GB0, RB0 = 0, 256, 768

        def slot_view(n, k, cols):
            return ring[:, n % RING, 0:k * cols].rearrange("p (k n) -> p k n", k=k)

        jobs = []
        n_slot = [48]

        def job(W, k, cols, mm, evac, new=True, last=True, need=None, eng="act"):
            if new:
                n_slot[0] += 1
            jobs.append(dict(W=W, k=k, cols=cols, mm=mm, evac=evac, new=new, last=last,
                             slot=n_slot[0] - 1, need=need, eng=eng, n=len(jobs)))
            return len(jobs) - 1

        def mm_T(src, k, pieces):
            def f(w, bank):
                return [[(ps[r0:r0 + m, bank, o0:o0 + T], w[:, kk, c0:c0 + m], src[:, kk, :]) for kk in range(k)]
                        for c0, m, r0, o0 in pieces]
            return f

        def mm_V(src, k, cols, c0=0, n=None):
            n = n or cols
            def f(w, bank):
                return [[(ps[:, bank, tt * n:(tt + 1) * n], src[:, kk, tt * P:(tt + 1) * P], w[:, kk, c0:c0 + n])
                         for kk in range(k)] for tt in range(TT)]
            return f

        def copy_to(*pairs, func=ACT.Copy):
            def f(bank):
                for src, dst in pairs:
                    last = nc.scalar.activation(dst, src(bank), func)
                return last
            return f

        def whole(bank):
            return ps[:, bank, :]

        def pair_dst(buf, s):
            return buf[:, 2 * s:2 * s + 2, :].rearrange("p c t -> p (c t)")

        def dense(W, src, dst, n, need):
            return [job(W[:, 256 * s:256 * s + 256], 8, 256,
                        mm_T(src, 8, [(0, P, 0, 0), (P, P, 0, T)]),
                        copy_to((whole, pair_dst(dst, s))), need=need) for s in range(n)]

        ropes = []

        ph = {}
        ph["diff"] = len(jobs)
        dj = dense(A["diff_w_in"][0], hT, qT, 4, ("h_ready", 1))
        dj += dense(A["diff_w_in"][0, :, D:2 * D], hT, kT, 4, None)
        for s in range(4):
            job(A["diff_w_in"][0, :, 2 * D + 256 * s:2 * D + 256 * s + 256], 8, 256, mm_V(hT, 8, 256),
                copy_to((lambda b: ps[:, b, :].rearrange("p (a n) -> p a n", a=TT),
                         vtok[:, :, 256 * s:256 * s + 256])))

        def out_jobs(W, need):
            return [job(W[:, 256 * s:256 * s + 256], 8, 256, mm_T(oT, 8, [(0, P, 0, 0), (P, P, 0, T)]),
                        s, need=need, eng="dve") for s in range(4)]

        ph["diff_out"] = len(jobs)
        out_jobs(A["diff_w_out"][0], "attention")
        slot_moe = {0: n_slot[0]}
        n_slot[0] += 12 * E1_GROUPS

        ph["nsa"] = len(jobs)
        nw = A["nsa_w_in"][0]
        dense(nw, hT, qT, 4, ("h_ready", 3))
        kdup = {"s": kT[:, 0:2, :], "w": kT[:, 2:4, :]}
        vTb = {"s": kT[:, 4, :], "w": kT[:, 5, :]}
        kcp = {0: sqb[:, 0:256].rearrange("p (g u) -> p g u", g=2), 1: sqb[:, 256:512].rearrange("p (g u) -> p g u", g=2)}
        dup_pieces = [(64 * g, 64, 64 * half, T * g) for g in range(2) for half in range(2)]
        nsa_src = {}
        for which, off in (("s", 256), ("w", 512)):
            nsa_src["k" + which] = job(nw[:, NSA_Q + off:NSA_Q + off + 128], 8, 128, mm_T(hT, 8, dup_pieces),
                                       copy_to((whole, kdup[which].rearrange("p c t -> p (c t)"))))
            nsa_src["v" + which] = job(nw[:, NSA_Q + off + 128:NSA_Q + off + 256], 8, 128,
                                       mm_T(hT, 8, [(0, P, 0, 0)]),
                                       copy_to((lambda b: ps[:, b, 0:T], vTb[which])))
        for t in range(2):
            def even(b):
                return ps[0:64, b, :].rearrange("p (g u e) -> p g u e", g=2, e=2)[:, :, :, 0]

            def odd(b):
                return ps[64:128, b, :].rearrange("p (g u e) -> p g u e", g=2, e=2)[:, :, :, 1]
            nsa_src["c" + str(t)] = job(nw[:, NSA_Q + 128 * t:NSA_Q + 128 * t + 128], 8, 128, mm_T(hT, 8, dup_pieces),
                                        copy_to((even, kcp[t][0:64]), (odd, kcp[t][64:128])))
        nsa_src["gate"] = job(nw[:, NSA_Q + 768:NSA_Q + 816], 8, 48, mm_V(hT, 8, 48),
                              copy_to((lambda b: ps[:, b, 0:96].rearrange("p (a n) -> p a n", a=TT), gates[:, :, :]),
                                      func=ACT.Sigmoid))
        blk = yT[:, 0:4, :].rearrange("p c t -> p (c t)")[:, 0:2 * 480].rearrange(
            "p (t j g n) -> p t j g n", t=2, j=16, g=2)
        gh = sqb[:, 512:632].rearrange("p (t m n) -> p t m n", t=2, m=2)
        kcmp = sqb[:, 640:670]
        vcmp = sqb[0:NCMP, 672:800]
        for t in range(2):
            for half in range(2):
                def f(w, bank, t=t, half=half):
                    return [[(ps[:, bank, 32 * m:32 * m + 30], w[:, j, P * m:P * m + P],
                              blk[:, t, 8 * half + j, :, :].rearrange("p g n -> p (g n)")) for j in range(8)]
                            for m in range(2)]
                job(A["nsa_cmp_w1"][0, t, 1024 * half:1024 * half + 1024, :], 8, 256, f,
                    copy_to((lambda b: ps[:, b, 0:64].rearrange("p (m n) -> p m n", m=2)[:, :, 0:30],
                             rt[:, 120 * half + 60 * t:120 * half + 60 * t + 60].rearrange("p (m n) -> p m n", m=2))),
                    need=("blk_ready", 1))

        def f(w, bank):
            gk = [[(ps[64 * half:64 * half + 64, bank, 0:30], w[:, m, 0:64], gh[:, 0, m, :]) for m in range(2)]
                  for half in range(2)]
            return gk
        job(A["nsa_cmp_w2"][0, 0], 2, 64, f, copy_to((lambda b: ps[:, b, 0:30], kcmp)), need=("gelu", 1))

        def f(w, bank):
            return [[(ps[0:NCMP, bank, 64 * g:64 * g + 64], gh[:, 1, m, NCMP * g:NCMP * g + NCMP], w[:, m, 0:64])
                     for m in range(2)] for g in range(2)]
        nsa_src["cmp"] = job(A["nsa_cmp_w2"][0, 1], 2, 64, f, copy_to((lambda b: ps[0:NCMP, b, 0:128], vcmp)))
        ph["nsa_out"] = len(jobs)
        out_jobs(A["nsa_w_out"][0], "attention")
        slot_moe[1] = n_slot[0]
        n_slot[0] += 12 * E1_GROUPS

        ph["even"] = len(jobs)
        ew = A["w_in_even_2"][0]
        scr = yT[:, :, :].rearrange("p c t -> p (c t)")
        cqT = scr[:, 0:512].rearrange("p (c t) -> p c t", c=2)
        ckvT = scr[:, 512:768].rearrange("p (c t) -> p c t", c=1)
        kpe = scr[:, 768:1024]
        gqT = scr[:, 1024:1536].rearrange("p (c t) -> p c t", c=2)
        gkT = scr[:, 1536:2048].rearrange("p (c t) -> p c t", c=2)
        hfl = hT[:, :, :].rearrange("p c t -> p (c t)")
        gv = hfl[:, 0:1024].rearrange("p (a n) -> p a n", a=TT)
        grT = hfl[:, 1024:2048].rearrange("p (c t) -> p c t", c=4)
        lrT = rt[0:16, 0:512].rearrange("p (a t) -> p a t", a=2)
        vm = vt[:, 0:1024].rearrange("p (a h n) -> p a h n", a=TT, h=8)
        job(ew[:, 0:256], 8, 256, mm_T(xT, 8, [(0, P, 0, 0), (P, P, 0, T)]),
            copy_to((whole, scr[:, 0:512])), need=("h_ready", 5))
        job(ew[:, 256:384], 8, 128, mm_T(xT, 8, [(0, P, 0, 0)]),
            copy_to((lambda b: ps[:, b, 0:T], ckvT[:, 0, :])))
        job(ew[:, 384:416], 8, 32, mm_T(xT, 8, [(0, 32, 64, 0)]),
            copy_to((lambda b: ps[64:96, b, 0:T], kpe[64:96, :])))
        ev_kpe = len(jobs) - 1
        job(ew[:, 416:672], 8, 256, mm_T(xT, 8, [(0, P, 0, 0), (P, P, 0, T)]), copy_to((whole, scr[:, 1024:1536])))
        job(ew[:, 672:928], 8, 256, mm_T(xT, 8, [(0, P, 0, 0), (P, P, 0, T)]), copy_to((whole, scr[:, 1536:2048])))
        for s in range(2):
            job(ew[:, 928 + 256 * s:1184 + 256 * s], 8, 256, mm_V(xT, 8, 256),
                copy_to((lambda b: ps[:, b, :].rearrange("p (a n) -> p a n", a=TT), gv[:, :, 256 * s:256 * s + 256])))
        job(ew[:, 1440:1472], 8, 32, mm_T(xT, 8, [(0, 16, 0, 0), (16, 16, 0, T)]),
            copy_to((lambda b: ps[0:16, b, :], rt[0:16, 0:512])))
        ev_lr = len(jobs) - 1
        for s in range(2):
            job(ew[:, 1472 + 256 * s:1728 + 256 * s], 8, 256, mm_T(xT, 8, [(0, P, 0, 0), (P, P, 0, T)]),
                copy_to((whole, hfl[:, 1024 + 512 * s:1536 + 512 * s]), func=ACT.Silu))
        ev_uq = len(jobs)
        for s in range(4):
            job(A["w_uq_2"][0], 2, 768, mm_T(cqT, 2, [(96 * (2 * s + a), 96, 0, T * a) for a in range(2)]),
                copy_to((lambda b: ps[0:96, b, :], qT[0:96, 2 * s:2 * s + 2, :].rearrange("p c t -> p (c t)"))),
                new=(s == 0), last=(s == 3), need=("pn_done", 6) if s == 0 else None)
        ev_kv = len(jobs)
        for s in range(4):
            job(A["w_ukv_2"][0], 1, 1024, mm_T(ckvT, 1, [(P * (2 * s + a), 64, 0, T * a) for a in range(2)]),
                copy_to((lambda b: ps[0:64, b, :], kT[0:64, 2 * s:2 * s + 2, :].rearrange("p c t -> p (c t)"))),
                new=(s == 0), last=False)
        for tt in range(TT):
            def f(w, bank, tt=tt):
                return [[(ps[:, bank, :], ckvT[:, 0, tt * P:tt * P + P],
                          w[:, 0, :].rearrange("p (h n) -> p h n", h=8)[:, :, 64:128])]]
            job(A["w_ukv_2"][0], 1, 1024, f,
                copy_to((whole, vt[:, 512 * tt:512 * tt + 512])), new=False, last=(tt == 1))
        ph["even_out"] = len(jobs)
        out_jobs(A["w_o_2"][0], "attention")

        def ple_jobs(layer, nh):
            first = len(jobs)
            for s in range(4):
                def ev(bank, s=s):
                    for a in range(2):
                        last = nc.scalar.activation(kT[:, 2 * s + a, :], ps[:, bank, T * a:T * a + T], ACT.Sigmoid,
                                                    bias=col("ple_gate_b_2", 8 * layer + 2 * s + a))
                    return last
                job(A["ple_gate_w_2"][layer][:, 256 * s:256 * s + 256], 8, 256,
                    mm_T(xT, 8, [(0, P, 0, 0), (P, P, 0, T)]), ev, need=("h_ready", nh) if s == 0 else None)
            for s in range(4):
                def ev(bank, s=s):
                    return nc.scalar.activation(pair_dst(qT, s), ps[:, bank, :], ACT.Copy)
                job(A["ple_w_2"][layer], 2, 1024, mm_T(pTb[layer], 2, [(256 * s, P, 0, 0), (256 * s + P, P, 0, T)]),
                    ev, new=(s == 0), last=(s == 3))
            return first
        pTall = sb("pT", [P, 2, 2, T])
        pTb = [pTall[:, 0], pTall[:, 1]]
        ph["ple0"] = ple_jobs(0, 6)
        slot_moe[2] = n_slot[0]
        n_slot[0] += 48 * E2_GROUPS

        ph["odd"] = len(jobs)
        ow = A["w_in_odd_2"][0]
        dense(ow, xT, qT, 4, ("h_ready", 7))
        for s in range(2):
            job(ow[:, D + 128 * s:D + 128 * s + 128], 8, 128, mm_T(xT, 8, dup_pieces),
                copy_to((whole, pair_dst(kT, s))))
        job(ow[:, D + 256:D + 512], 8, 256, mm_V(xT, 8, 256), copy_to((whole, vt[:, 0:512])))
        vo = vt[:, 0:512].rearrange("p (a n) -> p a n", a=TT)
        ph["odd_out"] = len(jobs)
        out_jobs(A["w_o_2"][1], "attention")
        ph["ple1"] = ple_jobs(1, 8)
        slot_moe[3] = n_slot[0]
        n_slot[0] += 48 * E2_GROUPS
        ph["end"] = len(jobs)
        phases = ["diff", "diff_out", "nsa", "nsa_out", "even", "even_out", "ple0", "odd", "odd_out", "ple1", "end"]
        span = {a: range(ph[a], ph[b]) for a, b in zip(phases, phases[1:])}
        acts_before, res_no, part_no = {}, {}, {}
        for j, jb in enumerate(jobs):
            acts_before[j] = sum(x["eng"] == "act" for x in jobs[:j])
            res_no[j] = j - acts_before[j]
            part_no[j] = sum(not x["last"] for x in jobs[:j])
        acts_before[len(jobs)] = sum(x["eng"] == "act" for x in jobs)

        def finished(j):
            return ("slot_used", jobs[j]["slot"] + 1) if jobs[j]["last"] else ("job_part", part_no[j] + 1)

        def evacuated(j):
            return ("proj_evac", acts_before[j] + 1) if jobs[j]["eng"] == "act" else ("res_evac", res_no[j] + 1)

        def await_need(eng, need):
            name, value = evacuated(need[1]) if need[0] == "job" else need
            eng.wait_ge(S(name), value)

        cd, sd = cosd[:, 0, :], cosd[:, 1, :]
        for s in range(8):
            buf = qT if s < 4 else kT
            ropes.append((pair_dst(buf, s % 4), 2, 0, P, K("rot16"), cd, sd, ("job", span["diff"][s])))
        r_nsa = len(ropes)
        for s in range(4):
            ropes.append((pair_dst(qT, s), 2, 0, P, K("rot16"), cd, sd, ("job", span["nsa"][s])))
        for i, w in enumerate("sw"):
            ropes.append((pair_dst(kT, i), 2, 0, P, K("rot16"), cd, sd, ("job", nsa_src["k" + w])))
            ropes.append((kT[:, 4 + i, :], 1, 0, P, K("rot16"), cd, sd, ("job", nsa_src["v" + w])))
        r_even = len(ropes)
        ropes.append((kpe, 1, 64, 32, K("rot_mla"), K("cos_m"), K("sin_m"), ("job", ev_kpe)))
        for s in range(4):
            ropes.append((pair_dst(qT, s), 2, 0, 96, K("rot_mla"), K("cos_m"), K("sin_m"), ("job", ev_uq + s)))
        r_odd = len(ropes)
        for s in range(6):
            ropes.append((pair_dst(qT if s < 4 else kT, s % 4), 2, 0, P, K("rot64"), K("cos_g"), K("sin_g"),
                          ("pn_done", 8 + s + 1)))
        r_end = len(ropes)

        pns = []
        for s in range(4):
            o = pair_dst(oT, s)
            pns.append(([o], K("ones"), 128, [(o, coef[:, 2:3], o, None)], ("o_evac", 2 * s + 2)))
        pns.append(([cqT[:, 0, :], cqT[:, 1, :]], K("ones"), 256,
                    [(cqT[:, a, :], col("mla_q_norm_2", a), cqT[:, a, :], None) for a in range(2)],
                    ("job", ph["even"])))
        pns.append(([ckvT[:, 0, :]], K("ones"), 128, [(ckvT[:, 0, :], col("mla_kv_norm_2"), ckvT[:, 0, :], None)],
                    ("job", ph["even"] + 1)))
        for s in range(2):
            o = oT[:, 4 + 2 * s:6 + 2 * s, :].rearrange("p c t -> p (c t)")
            gr_s = grT[:, 2 * s:2 * s + 2, :].rearrange("p c t -> p (c t)")
            pns.append(([o], K("ones"), 128, [(o, col("gla_norm_2"), o, gr_s)], ("gla_evac", 2)))
        for s in range(6):
            o = pair_dst(qT if s < 4 else kT, s % 4)
            pns.append(([o], K("ones64"), 64, [(o, col("gqa_q_norm_2" if s < 4 else "gqa_k_norm_2"), o, None)],
                        ("job", ph["odd"] + s)))

        units, obanks = [], []

        def unit(q, k, v, rows, obank, start, stop, causal=False, scale=64 ** -0.5, coef=None, cmp=None):
            units.append(dict(q=q, k=k, v=v, rows=rows, o=obank, start=start, stop=stop, causal=causal,
                              scale=scale, coef=coef, cmp=cmp, last=False))

        u_ph = {}
        u_ph["diff"] = 0
        for h in range(8):
            for c in range(2):
                r = slice(64 * c, 64 * c + 64)
                unit(qT[r, h, :], kT[r, h, :], [vtok[:, tt, P * h:P * h + P] for tt in range(TT)],
                     slice(0, P), len(obanks), c == 0, c == 1, causal=True, coef=coef[:, 0:2] if c else None)
            units[-1]["last"] = True
            obanks.append(oT[:, h, :])
        u_ph["nsa"] = len(units)
        vsw = {w: vt[:, 256 * i:256 * i + 256].rearrange("p (a n) -> p a n", a=TT) for i, w in enumerate("sw")}
        PC = vt[:, 512:992].rearrange("p (a h n) -> p a h n", a=TT, h=16)
        for h in range(16):
            g, r = h // 8, slice(64 * (h % 2), 64 * (h % 2) + 64)
            for i, w in enumerate("sw"):
                unit(qT[r, h // 2, :], kdup[w][r, g, :], [vsw[w][:, tt, 64 * g:64 * g + 64] for tt in range(TT)],
                     r, len(obanks), i == 0, False, causal=True, coef=gates[:, :, 3 * h + 1 + i])
            unit(None, None, vcmp[:, 64 * g:64 * g + 64], r, len(obanks), False, True, cmp=h)
            if h % 2:
                units[-1]["last"] = True
                obanks.append(oT[:, h // 2, :])
        u_ph["mla"] = len(units)
        for h in range(8):
            r = slice(64 * (h % 2), 64 * (h % 2) + 64)
            unit(qT[0:96, h, :], kT[0:96, h, :], [vm[:, tt, h, :] for tt in range(TT)], r, len(obanks), True, True,
                 scale=96 ** -0.5)
            if h % 2:
                units[-1]["last"] = True
                obanks.append(oT[:, h // 2, :])
        u_ph["gqa"] = len(units)
        for h in range(16):
            kv, r = h // 4, slice(64 * (h % 2), 64 * (h % 2) + 64)
            unit(qT[r, h // 2, :], kT[r, kv, :], [vo[:, tt, 64 * kv:64 * kv + 64] for tt in range(TT)],
                 r, len(obanks), True, True)
            if h % 2:
                units[-1]["last"] = True
                obanks.append(oT[:, h // 2, :])
        u_ph["end"] = len(units)
        soft = [u for u, un in enumerate(units) if un["cmp"] is None]
        s_no = [sum(x <= u for x in soft) for u in range(len(units))]
        u_span = {a: range(u_ph[a], u_ph[b]) for a, b in
                  zip(["diff", "nsa", "mla", "gqa"], ["nsa", "mla", "gqa", "end"])}
        o_after = {"diff": 8, "nsa": 16, "mla": 20, "gqa": 28}

        def flat(t):
            return t[:, :, :].rearrange("p c t -> p (c t)")
        at = [flat(qT)[:, 1024 * d:1024 * d + 1024].rearrange("p (a n) -> p a n", a=8) for d in range(2)]
        stt_ = [flat(kT)[:, 1024 * d:1024 * d + 1024].rearrange("p (c n v) -> p c n v", c=2, n=4) for d in range(2)]
        gE = vt[:, 0:1536].rearrange("p (a n) -> p a n", a=3)
        kd = vt[:, 1536:2048].rearrange("p (c t) -> p c t", c=2)
        lnb = [pn[:, :], sg[:, 512:1024]]
        la = [oT[:, 4 + 2 * d:6 + 2 * d, :].rearrange("p c t -> p (c t)").rearrange("p (a n) -> p a n", a=TT) for d in range(2)]
        qg = [sqb[:, 512 * d:512 * d + 512].rearrange("p (c t) -> p c t", c=2) for d in range(2)]
        kg = [ptb[:, :, :].rearrange("p b n -> p (b n)")[:, 512 * d:512 * d + 512].rearrange("p (c t) -> p c t", c=2) for d in range(2)]
        kdt = sg[:, 0:512].rearrange("p (a n) -> p a n", a=TT)
        gdec = misc[:, 16:32].rearrange("p (a n) -> p a n", a=2)

        def rtv(first, n, parts=P, **kw):
            v = rt[0:parts, first:first + n]
            return v.rearrange("p (a n) -> p a n", **kw) if kw else v
        rt_lg = rtv(0, 72, a=TT)
        rt_g8, rt_m8, rt_oh4 = rtv(72, 16, a=TT), rtv(88, 16, a=TT), rtv(104, 8, a=TT)
        rt_le, rt_L = rtv(112, 64, a=TT), rtv(304, 64, a=TT)
        rt_oh = rt[:, 176:304].rearrange("p (b a n) -> p b a n", b=2, a=TT)
        rt_c, rt_e, rt_t8 = rtv(432, 20), rtv(452, 8), rtv(460, 8, 32)
        rt_nblk, rt_nblkB, rt_base, rt_cmp = rtv(468, 1, 32), rtv(470, P, 32), rtv(600, 35), rtv(640, E1_BLOCKS, 32)
        rt_selT, rt_m8e = rtv(700, T, E2), rtv(960, 8, E2)

        def rt_sel(n):
            return rtv(368, TT * n, a=TT)

        moe_g0 = [0, E1_GROUPS, 2 * E1_GROUPS, 2 * E1_GROUPS + E2_GROUPS]

        block = ctx.enter_context(nc.Block())

        @block.sync
        def _(sp):
            n_par = [0]

            def param(dst, src):
                sp.dma_start(dst, src).then_inc(S("params"), 16)
                n_par[0] += 1

            sp.dma_start(cst[:, :], A["consts"]).then_inc(S("consts"), 16)
            sp.wait_ge(S("rows_zero"), 1)
            for tt in range(TT):
                sp.dma_start(sq[:, 1024 * tt:1024 * tt + 1024], A["x"][0, P * tt:P * tt + P, :]).then_inc(S("x_in"), 16)
            param(rowsA[0:96, 0, :], A["ada_b"].rearrange("l (r c) -> (l r) c", c=P))
            param(rowsA[96:128, 0, :], A["norm_g"].rearrange("l a (r c) -> (l a r) c", c=P))
            for name in ("c", "ln1_g_2", "ln1_b_2", "ln2_g_2", "ln2_b_2", "ple_gate_b_2", "mla_q_norm_2",
                         "mla_kv_norm_2", "gla_norm_2", "diff_subln_g"):
                a, n = R1[name]
                param(rowsA[a:a + n, 1, :], A[name].rearrange("l (r c) -> (l r) c", c=P))
            a, n = R1["final_g"]
            param(rowsA[a:a + n, 1, :], A["final_g"].rearrange("(r c) -> r c", c=P))
            a, n = R1["nsa_cmp_b1"]
            param(rowsA[a:a + n, 1, :], A["nsa_cmp_b1"].rearrange("l a (r c) -> (l a r) c", c=P))
            for name in ("gqa_q_norm_2", "gqa_k_norm_2"):
                a, _ = R1[name]
                for half in range(2):
                    param(rowsA[a:a + 1, 1, 64 * half:64 * half + 64], A[name])
            param(rowsA[0:32, 2, :], A["nsa_cmp_pos"].rearrange("l a (j e) d -> (l a j) (e d)", e=2))
            param(rows1[0:1, LAM0:LAM0 + 256], A["diff_lambda"].rearrange("l a d -> l (a d)"))
            param(rows1[0:1, GB0:GB0 + 256], A["gla_gate_b_fwd_2"])
            param(rows1[0:1, GB0 + 256:GB0 + 512], A["gla_gate_b_bwd_2"])
            for l in range(2):
                param(rows1[0:1, RB0 + 36 * l:RB0 + 36 * l + 4], A["moe_b_group"][l:l + 1, :])
                param(rows1[0:1, RB0 + 36 * l + 4:RB0 + 36 * l + 36],
                      A["moe_b_expert"][l:l + 1].rearrange("l g e -> l (g e)"))
                param(wr[l][:, :, 0:4], A["moe_w_group"][l].rearrange("(k p) n -> p k n", p=P))
                for g in range(4):
                    param(wr[l][:, :, 4 + 8 * g:12 + 8 * g], A["moe_w_expert"][l, g].rearrange("(k p) n -> p k n", p=P))
                param(wr[2 + l][:, :, :], A["router_w_2"][l].rearrange("(k p) n -> p k n", p=P))
            param(gw[:, 0, :], A["gla_gate_w_fwd_2"][0])
            param(gw[:, 1, :], A["gla_gate_w_bwd_2"][0])
            param(posi, A["positions"].to_broadcast([P, T]))
            assert n_par[0] == N_PARAMS, n_par[0]
            for l in range(2):
                sp.dma_start(yT[:, 4 * l:4 * l + 2, :], A["p_2"][l, 0].rearrange("(a p) n -> p a n", p=P))\
                    .then_inc(S("p_in"), 16)

            def load(n, dst, src, wait=True):
                if n >= RING:
                    sp.wait_ge(S("slot_used"), n - RING + 1)
                sp.dma_start(dst, src).then_inc(S(f"slot{n % RING}"), 16)

            for n in range(48):
                l, s = n // 24, n % 24
                load(n, slot_view(n, 8, 256), A["ada_w"][l][:, 256 * s:256 * s + 256].rearrange("(k p) n -> p k n", p=P))

            def load_jobs(name):
                for j in span[name]:
                    jb = jobs[j]
                    if jb["new"]:
                        load(jb["slot"], slot_view(jb["slot"], jb["k"], jb["cols"]),
                             jb["W"].rearrange("(k p) n -> p k n", p=P))

            def load_experts1(m):
                n0 = slot_moe[m]
                gate = A["moe_w_gate"].rearrange("l e (p k) n -> l e p (k n)", p=P)
                up = A["moe_w_up"].rearrange("l e (p k) n -> l e p (k n)", p=P)
                down = A["moe_w_down"].rearrange("l e (p k) n -> l e p (k n)", p=P)
                sp.wait_ge(S("ids_ready"), m + 1)
                with sp.Fori(0, E1_GROUPS) as i:
                    e = [sp.value_load(ids[0:1, 0, bass.ds(4 * i + j, 1)], min_val=0, max_val=E1 - 1) for j in range(4)]
                    on = [sp.value_load(ids[0:1, 1, bass.ds(4 * i + j, 1)], min_val=0, max_val=1) for j in range(4)]
                    order = [(w, j) for j in range(4) for w in (gate, up)] + [(down, j) for j in range(4)]
                    for s, (w, j) in enumerate(order):
                        sp.wait_ge(S("slot_used"), 12 * i + (n0 + s - RING + 1))
                        sp.dma_start(ring[:, (n0 + s) % RING, :], w[m, e[j]], cond=on[j] > 0)\
                            .then_inc(S(f"slot{(n0 + s) % RING}"), 16)

            def load_experts2(l, m):
                n0 = slot_moe[m]
                w1 = A["w1_2"].rearrange("l e (p k) n -> l e p (k n)", p=P)
                w3 = A["w3_2"].rearrange("l e (p k) n -> l e p (k n)", p=P)
                w2 = A["w2_2"].rearrange("l e (p k) n -> l e p (k n)", p=P)
                with sp.Fori(0, E2_GROUPS) as i:
                    order = [(w, j, kk) for kk in range(4) for j in range(4) for w in (w1, w3)]
                    order += [(w2, j, kk) for kk in range(4) for j in range(4)]
                    for s, (w, j, kk) in enumerate(order):
                        sp.wait_ge(S("slot_used"), 48 * i + (n0 + s - RING + 1))
                        sp.dma_start(ring[:, (n0 + s) % RING, :], w[l, 4 * i + j][:, SLOT * kk:SLOT * kk + SLOT])\
                            .then_inc(S(f"slot{(n0 + s) % RING}"), 16)

            load_jobs("diff")
            load_jobs("diff_out")
            load_experts1(0)
            load_jobs("nsa")
            load_jobs("nsa_out")
            load_experts1(1)
            load_jobs("even")
            load_jobs("even_out")
            load_jobs("ple0")
            load_experts2(0, 2)
            load_jobs("odd")
            load_jobs("odd_out")
            load_jobs("ple1")
            load_experts2(1, 3)
            for tt in range(TT):
                sp.wait_ge(S("out_ready"), tt + 1)
                sp.dma_start(out[0, P * tt:P * tt + P, :], h_tok[:, tt, :]).then_inc(S("stored"), 16)
            sp.wait_ge(S("stored"), 16 * TT)

        @block.tensor
        def _(pe):
            mmul = nc.tensor.matmul

            def slot_in(n):
                pe.wait_ge(S(f"slot{n % RING}"), 16 * (n // RING + 1))

            def tr(dst, src, k=P):
                return nc.tensor.transpose(dst, src, ident[0:k, 0:k])

            def project(js):
                for j in js:
                    jb = jobs[j]
                    if isinstance(jb["need"], tuple):
                        pe.wait_ge(S(jb["need"][0]), jb["need"][1])
                    if jb["new"]:
                        slot_in(jb["slot"])
                    if j >= 2:
                        await_need(pe, ("job", j - 2))
                    for grp in jb["mm"](slot_view(jb["slot"], jb["k"], jb["cols"]), j % 2):
                        for i, (o, l, r) in enumerate(grp):
                            last = mmul(o, l, r, start=(i == 0), stop=(i == len(grp) - 1))
                    last.then_inc(S(finished(j)[0]), 1)
                    after(j)

            rope_next = [0]

            def rope(i):
                buf, n, r0, rows, rot, _, _, need = ropes[i]
                await_need(pe, need)
                if i >= 2:
                    pe.wait_ge(S("rope_done"), i - 1)
                rr = slice(r0, r0 + rows)
                mmul(ps[rr, 2 + i % 2, 0:n * T], rot[rr, rr], buf[rr, :], start=True, stop=True)\
                    .then_inc(S("rope_mm"), 1)

            def after(j):
                while rope_next[0] < r_end and ropes[rope_next[0]][7][0] == "job" and \
                        ropes[rope_next[0]][7][1] < j and rope_next[0] < rope_limit[0]:
                    rope(rope_next[0])
                    rope_next[0] += 1

            rope_limit = [0]

            def ropes_until(end):
                while rope_next[0] < end:
                    rope(rope_next[0])
                    rope_next[0] += 1

            def partition_norm(i):
                srcs, ones, _, _, _ = pns[i]
                pe.wait_ge(S("pn_sq"), i + 1)
                if i:
                    pe.wait_ge(S("pn_var"), i)
                for a, s in enumerate(srcs):
                    n = s.shape[-1]
                    last = mmul(ps[:, 7, 0:n], ones, sqb[:, 512 * (i % 2) + n * a:512 * (i % 2) + n * a + n],
                                start=(a == 0), stop=(a == len(srcs) - 1))
                last.then_inc(S("pn_mm"), 1)

            def norm(n):
                if n >= 5:
                    pe.wait_ge(S("x_ready"), n + 1)
                    for c in range(C):
                        last = mmul(ps[:, 3, 0:T], K("ones"), xT[:, c, :], start=(c == 0), stop=(c == C - 1))
                    last.then_inc(S("mean_mm"), 1)
                pe.wait_ge(S("sq_ready"), n + 1)
                for c in range(C):
                    last = mmul(ps[:, 2, 0:T], K("ones"), sq[:, T * c:T * c + T], start=(c == 0), stop=(c == C - 1))
                last.then_inc(S("sq_mm"), 1)

            def attention(name):
                us = list(u_span[name])

                def scores(u):
                    un = units[u]
                    if un["cmp"] is not None:
                        return
                    b = 4 + s_no[u] % 2
                    if s_no[u] > 2:
                        pe.wait_ge(S("exp_done"), s_no[u] - 2)
                    q, k = un["q"], un["k"]
                    if un["causal"]:
                        mmul(ps[:, b, 0:P], q[:, 0:P], k[:, 0:P], start=True, stop=False, skip_group_check=True)
                        mmul(ps[:, b, 0:P], identb[:, :], trib[:, :], start=False, stop=True, skip_group_check=True)
                        mmul(ps[:, b, P:P + T], q[:, P:T], k, start=True, stop=False, skip_group_check=True)
                        last = mmul(ps[:, b, T:T + P], identb[:, :], trib[:, :], start=False, stop=True,
                                    skip_group_check=True)
                    else:
                        mmul(ps[:, b, 0:T], q[:, 0:P], k, start=True, stop=True)
                        last = mmul(ps[:, b, T:2 * T], q[:, P:T], k, start=True, stop=True)
                    last.then_inc(S("s_done"), 1)

                def transposes(u):
                    un = units[u]
                    b = 6 + u % 2
                    if u - 2 >= us[0]:
                        pe.wait_ge(S("pt_ready"), u - 1)
                    if un["cmp"] is not None:
                        for tt in range(TT):
                            last = tr(ps[0:NCMP, b, P * tt:P * tt + P], PC[:, tt, un["cmp"], :])
                    else:
                        pe.wait_ge(S("p_ready"), s_no[u])
                        p = pb[:, s_no[u] % 2, :]
                        order = [0, 1, 2] if un["causal"] else [0, 2, 1, 3]
                        for i, blk_ in enumerate(order):
                            last = tr(ps[:, b, P * i:P * i + P], p[:, P * blk_:P * blk_ + P])
                    last.then_inc(S("t_done"), 1)

                def values(u):
                    un = units[u]
                    b = 2 + un["o"] % 2
                    pe.wait_ge(S("pt_ready"), u + 1)
                    if un["start"] and un["o"] >= 2:
                        pe.wait_ge(S("o_evac"), un["o"] - 1)
                    o, pt, v = ps[un["rows"], b, 0:T], ptb[:, u % 2, :], un["v"]
                    if un["cmp"] is not None:
                        last = mmul(o, v, pt[0:NCMP, 0:T], start=False, stop=True, skip_group_check=True)
                    elif un["causal"]:
                        mmul(o, v[0], pt[:, 0:T], start=un["start"], stop=False, skip_group_check=True)
                        last = mmul(ps[un["rows"], b, P:T], v[1], pt[:, T:T + P], start=False, stop=un["stop"],
                                    skip_group_check=True)
                    else:
                        mmul(o, v[0], pt[:, 0:T], start=True, stop=False)
                        last = mmul(o, v[1], pt[:, T:2 * T], start=False, stop=True)
                    last.then_inc(S("v_done"), 1)

                pe.wait_ge(S("att_go"), {"diff": 1, "nsa": 2, "mla": 3, "gqa": 4}[name])
                for i, u in enumerate(us):
                    scores(u)
                    if i >= 1:
                        transposes(u - 1)
                    if i >= 2:
                        values(u - 2)
                transposes(us[-1])
                values(us[-2])
                values(us[-1])

            def to_tokens(src, count):
                for tt in range(TT):
                    for c in range(C):
                        last = tr(ps[:, 2 * tt + c // 4, P * (c % 4):P * (c % 4) + P], src[:, c, P * tt:P * tt + P])
                last.then_inc(S("tok_mm"), 1)

            def rank_of(sel, n, m):
                pe.wait_ge(S("sel_ready"), m + 1)
                mmul(ps[:, 5, 0:n], K("before"), sel[:, 0, :], start=True, stop=True)
                mmul(ps[:, 5, 64:64 + n], K("ones"), sel[:, 0, :], start=True, stop=False)
                return mmul(ps[:, 5, 64:64 + n], K("before"), sel[:, 1, :], start=False, stop=True)

            def router(m, src, n):
                for tt in range(TT):
                    for k in range(C):
                        last = mmul(ps[:, 4, 64 * tt:64 * tt + n], src[:, k, P * tt:P * tt + P], wr[m][:, k, 0:n],
                                    start=(k == 0), stop=(k == C - 1 and m >= 2))
                    if m < 2:
                        last = mmul(ps[:, 4, 64 * tt:64 * tt + n], K("ones", 1), rows1[0:1, RB0 + 36 * m:RB0 + 36 * m + n],
                                    start=False, stop=True)
                last.then_inc(S("logits"), 1)

            def route1(m):
                router(m, hT, 36)
                to_tokens(hT, m)
                sel = rt_sel(E1)
                rank_of(sel, E1, m)
                mmul(ps[0:32, 5, 128:129], sel[:, 0, :], K("ones")[:, 0:1], start=True, stop=False)
                mmul(ps[0:32, 5, 128:129], sel[:, 1, :], K("ones")[:, 0:1], start=False, stop=True)\
                    .then_inc(S("rank_mm"), 1)
                pe.wait_ge(S("nblk_ready"), m + 1)
                mmul(ps[:, 5, 192:224], rt_nblkB, K("before")[0:32, 0:32], start=True, stop=True)
                mmul(ps[:, 5, 224:225], rt_nblkB, K("ones")[0:32, 0:1], start=True, stop=True)
                mmul(ps[0:32, 5, 226:227], K("before")[0:32, 0:32], rt_nblk, start=True, stop=True)\
                    .then_inc(S("base_mm"), 1)
                pe.wait_ge(S("cmp_ready"), m + 1)
                mmul(ps[0:1, 6, 0:E1_BLOCKS], K("ones")[0:32, 0:1], rt_cmp, start=True, stop=True)\
                    .then_inc(S("count_mm"), 1)

            def route2(m):
                router(m, xT, 16)
                await_need(pe, ("job", ph["ple0" if m == 2 else "ple1"] + 7))
                to_tokens(xT, m)
                pe.wait_ge(S("aff_ready"), m - 1)
                for tt in range(TT):
                    last = tr(ps[0:E2, 6, P * tt:P * tt + P], affL[:, 0, tt, :])
                last.then_inc(S("affT_mm"), 1)
                pe.wait_ge(S("selT_ready"), m - 1)
                for tt in range(TT):
                    last = tr(ps[:, 6, 256 + 16 * tt:272 + 16 * tt], rt_selT[:, P * tt:P * tt + P], k=E2)
                last.then_inc(S("sel_mm"), 1)
                rank_of(rt_sel(E2), E2, m).then_inc(S("rank_mm"), 1)

            def experts(m, groups, ff):
                kpack = SLOT // ff
                halves = max(1, ff // 512)
                width = min(ff, 512)
                nup, ndn = 8 // kpack, ff // 256
                per = 12 * (ff // 256)
                n0, g0 = slot_moe[m], moe_g0[m]
                pe.wait_ge(S("tok_ready"), m + 1)
                with pe.Fori(0, groups) as i:
                    def slot_in_group(s):
                        n = n0 + s
                        pe.wait_ge(S(f"slot{n % RING}"), 16 * (per // RING) * i + 16 * (n // RING + 1))
                        return ring[:, n % RING, :]
                    pe.wait_ge(S("D_ready"), i + (g0 + 1))
                    for k in range(C):
                        for tt in range(TT):
                            last = mmul(ps[:, 4 + k // 4, P * (k % 4):P * (k % 4) + P],
                                        h_tok[:, tt, k::C], Dg[:, tt, :], start=(tt == 0), stop=(tt == 1))
                    last.then_inc(S("xg_mm"), 1)
                    for tt in range(TT):
                        last = tr(ps[:, 6, P * tt:P * tt + P], DAg[:, tt, :])
                    last.then_inc(S("C_mm"), 1)
                    pe.wait_ge(S("xg_ready"), i + (g0 + 1))
                    pe.wait_ge(S("y_added"), i + (g0 + m + 1))
                    s = 0
                    for kk in range(nup):
                        w = []
                        for j in range(4):
                            w.append([slot_in_group(s + 2 * j + a) for a in range(2)])
                        for k2 in range(kpack):
                            k = kpack * kk + k2
                            for h in range(halves):
                                for j in range(4):
                                    for a in range(2):
                                        last = mmul(ps[32 * j:32 * j + 32, 2 * a + h, 0:width],
                                                    xg[:, k, 32 * j:32 * j + 32],
                                                    w[j][a][:, ff * k2 + width * h:ff * k2 + width * h + width],
                                                    start=(k == 0), stop=(k == C - 1))
                                        if k2 == kpack - 1 and h == halves - 1:
                                            last.then_inc(S("slot_used"), 1)
                        s += 8
                    pe.wait_ge(S("hid_ready"), i + (g0 + 1))
                    nch = ff // P
                    for c in range(nch):
                        last = tr(ps[:, 4 + c // 4, P * (c % 4):P * (c % 4) + P], hid[:, c:ff:nch])
                    last.then_inc(S("hT_mm"), 1)
                    pe.wait_ge(S("hidT_ready"), i + (g0 + 1))
                    pe.wait_ge(S("C_ready"), i + (g0 + 1))
                    for kk in range(ndn):
                        w = [slot_in_group(s + j) for j in range(4)]
                        for c2 in range(2):
                            c = 2 * kk + c2
                            for h in range(2):
                                for j in range(4):
                                    last = mmul(ps[32 * j:32 * j + 32, 6 + h, :], hidT[:, c, 32 * j:32 * j + 32],
                                                w[j][:, D * c2 + 512 * h:D * c2 + 512 * h + 512],
                                                start=(c == 0), stop=(c == nch - 1))
                                    if c2 == 1 and h == 1:
                                        last.then_inc(S("slot_used"), 1)
                        s += 4
                    pe.wait_ge(S("Y_ready"), i + (g0 + 1))
                    for c in range(C):
                        last = mmul(ps[:, c // 2, T * (c % 2):T * (c % 2) + T], Yg[:, P * c:P * c + P], Cg[:, :],
                                    start=True, stop=True)
                    last.then_inc(S("y_mm"), 1)

            def gla_stage():
                pe.wait_ge(S("proj_evac"), acts_before[ev_lr] + 1)
                pe.wait_ge(S("o_evac"), o_after["mla"])
                for d in range(2):
                    for tt in range(TT):
                        mmul(ps[:, 4 + d, T * tt:T * tt + T], lrT[:, d, P * tt:P * tt + P], gw[:, d, :],
                             start=True, stop=False)
                        last = mmul(ps[:, 4 + d, T * tt:T * tt + T], K("ones", 1), rows1[0:1, GB0 + T * d:GB0 + T * d + T],
                                    start=False, stop=True)
                last.then_inc(S("gl_mm"), 1)
                for d in range(2):
                    pe.wait_ge(S("la_ready"), d + 1)
                    for c in range(2):
                        for tt in range(TT):
                            last = mmul(ps[:, 6, T * c + P * tt:T * c + P * tt + P],
                                        la[d][:, tt, P * c:P * c + P], K("tri_f" if d == 0 else "tri_b"),
                                        start=True, stop=True)
                    last.then_inc(S("cum_mm"), 1)
                    pe.wait_ge(S("qk_ready"), d + 1)
                    if d == 0:
                        pe.wait_ge(S("la_ready"), 2)
                    else:
                        pe.wait_ge(S("st_ready"), 1)
                    for h in range(4):
                        r = slice(64 * (h % 2), 64 * (h % 2) + 64)
                        for tt in range(TT):
                            tk = slice(P * tt, P * tt + P)
                            last = mmul(ps[:, 4 + h % 2, T * (h // 2) + P * tt:T * (h // 2) + P * tt + P],
                                        kg[d][r, h // 2, tk], qg[d][r, h // 2, tk], start=True, stop=True)
                    for c in range(2):
                        for tt in range(TT):
                            last = tr(ps[:, 2, T * tt + P * c:T * tt + P * c + P], kd[:, c, P * tt:P * tt + P])
                    last.then_inc(S("at_mm"), 1)
                    pe.wait_ge(S("at_ready"), d + 1)
                    for h in range(4):
                        c, half = h // 2, h % 2
                        for n in range(4):
                            tk = slice(64 * (n % 2), 64 * (n % 2) + 64)
                            last = mmul(ps[64 * half:64 * half + 64, 4 + n % 2, T * c + P * (n // 2):T * c + P * (n // 2) + P],
                                        kdt[tk, n // 2, 64 * h:64 * h + 64], gv[tk, n // 2, P * h:P * h + P],
                                        start=True, stop=True)
                    last.then_inc(S("u_mm"), 1)
                pe.wait_ge(S("st_ready"), 2)
                for h in range(4):
                    r, c = slice(64 * (h % 2), 64 * (h % 2) + 64), h // 2
                    for tt in range(TT):
                        o0 = T * (h // 2) + P * tt
                        for d in range(2):
                            mmul(ps[:, 4 + h % 2, o0:o0 + P], gv[:, tt, P * h:P * h + P],
                                 at[d][:, 4 * (h % 2) + 2 * (h // 2) + tt, :], start=(d == 0), stop=False, skip_group_check=True)
                        inter = [(d, n) for n in (2 * tt, 2 * tt + 1) for d in range(2)
                                 if not (d == 0 and n == 0) and not (d == 1 and n == 3)]
                        for x, (d, n) in enumerate(inter):
                            last = mmul(ps[:, 4 + h % 2, o0 + 64 * (n % 2):o0 + 64 * (n % 2) + 64],
                                        stt_[d][r, c, n, :], qg[d][r, c, 64 * n:64 * n + 64],
                                        start=False, stop=(x == len(inter) - 1), skip_group_check=True)
                    if h >= 2:
                        last.then_inc(S("go_mm"), 1)

            pe.wait_ge(S("consts"), 16)
            pe.wait_ge(S("x_in"), 16 * TT)
            for c in range(C):
                for tt in range(TT):
                    last = tr(ps[:, c // 2, T * (c % 2) + P * tt:T * (c % 2) + P * tt + P],
                              sq[:, 1024 * tt + P * c:1024 * tt + P * c + P])
            last.then_inc(S("xT_mm"), 1)
            pe.wait_ge(S("params"), 16 * N_PARAMS)
            for a in range(3):
                last = tr(ps[:, 4, P * a:P * a + P], rowsA[:, a, :])
            last.then_inc(S("cols_mm"), 1)
            pe.wait_ge(S("p_in"), 32)
            for l in range(2):
                for k in range(2):
                    for tt in range(TT):
                        last = tr(ps[:, 5 + l, T * k + P * tt:T * k + P * tt + P],
                                  yT[:, 4 * l + tt, P * k:P * k + P])
            last.then_inc(S("p_mm"), 1)
            pe.wait_ge(S("lam_ready"), 1)
            mmul(ps[:, 7, 0:1], K("ones", 1), misc[0:1, 8:9], start=True, stop=True).then_inc(S("lam_mm"), 1)
            pe.wait_ge(S("cpad_ready"), 1)
            pe.wait_ge(S("x_ready"), 1)
            for l in range(2):
                if l:
                    pe.wait_ge(S("modrow"), 1)
                for i in range(6):
                    for k in range(C):
                        for j in range(4):
                            n = 24 * l + 4 * i + j
                            if k == 0:
                                slot_in(n)
                            last = mmul(ps[32 * j:32 * j + 32, i // 2, T * (i % 2):T * (i % 2) + T],
                                        cpad[:, k, :], slot_view(n, 8, 256)[:, k, :], start=(k == 0), stop=(k == C - 1))
                            if k == C - 1:
                                last.then_inc(S("slot_used"), 1)
                pe.wait_ge(S("modrow"), l + 1)
                if l:
                    pe.wait_ge(S("mod_ready"), 1)
                for b in range(12):
                    last = tr(ps[:, 3 + b // 4, P * (b % 4):P * (b % 4) + P], sq[:, P * b:P * b + P])
                last.then_inc(S("modT_mm"), 1)
            norm(0)
            rope_limit[0] = r_nsa
            project(span["diff"])
            ropes_until(r_nsa)
            attention("diff")
            for i in range(4):
                partition_norm(i)
            pe.wait_ge(S("pn_done"), 4)
            project(span["diff_out"])
            norm(1)
            pe.wait_ge(S("h_ready"), 2)
            route1(0)
            experts(0, E1_GROUPS, E1_FF)
            norm(2)
            rope_limit[0] = r_even
            project(span["nsa"])
            ropes_until(r_even)
            pe.wait_ge(S("rope_done"), r_even)
            for i in range(2):
                for tt in range(TT):
                    last = tr(ps[:, 7, 256 * i + P * tt:256 * i + P * tt + P], kT[:, 4 + i, P * tt:P * tt + P])
            last.then_inc(S("vt_mm"), 1)
            pe.wait_ge(S("proj_evac"), acts_before[nsa_src["cmp"]] + 1)
            for tt in range(TT):
                for h in range(16):
                    r = slice(64 * (h % 2), 64 * (h % 2) + 64)
                    g = h // 8
                    o0 = NCMP * (8 * tt + h // 2)
                    last = mmul(ps[:, 4 + h % 2, o0:o0 + NCMP], qT[r, h // 2, P * tt:P * tt + P],
                                kcmp[r, NCMP * g:NCMP * g + NCMP], start=True, stop=True)
                last.then_inc(S("sc_mm"), 1)
            attention("nsa")
            pe.wait_ge(S("o_evac"), o_after["nsa"])
            project(span["nsa_out"])
            norm(3)
            pe.wait_ge(S("h_ready"), 4)
            route1(1)
            experts(1, E1_GROUPS, E1_FF)
            norm(4)
            rope_limit[0] = r_even
            project(range(ph["even"], ev_uq))
            partition_norm(4)
            partition_norm(5)
            rope_limit[0] = r_odd
            project(range(ev_uq, ph["even_out"]))
            ropes_until(r_odd)
            attention("mla")
            gla_stage()
            partition_norm(6)
            partition_norm(7)
            pe.wait_ge(S("pn_done"), 8)
            project(span["even_out"])
            norm(5)
            project(span["ple0"])
            route2(2)
            experts(2, E2_GROUPS, E2_FF)
            norm(6)
            rope_limit[0] = r_odd
            project(span["odd"])
            for s in range(6):
                partition_norm(8 + s)
                if s:
                    ropes_until(r_odd + s)
            ropes_until(r_end)
            attention("gqa")
            pe.wait_ge(S("o_evac"), o_after["gqa"])
            project(span["odd_out"])
            norm(7)
            project(span["ple1"])
            route2(3)
            experts(3, E2_GROUPS, E2_FF)
            norm(8)
            pe.wait_ge(S("h_ready"), 9)
            to_tokens(xT, 4)

        @block.scalar
        def _(act):
            func = nc.scalar.activation
            chain = [0]

            def link(ins):
                chain[0] += 1
                ins.then_inc(S("act_chain"), 1)
                act.wait_ge(S("act_chain"), chain[0])

            def evacuate(js):
                for j in js:
                    if jobs[j]["eng"] == "act":
                        act.wait_ge(S(finished(j)[0]), finished(j)[1])
                        jobs[j]["evac"](j % 2).then_inc(S("proj_evac"), 1)

            def norm(n):
                if n >= 5:
                    act.wait_ge(S("xc_ready"), n - 4)
                else:
                    act.wait_ge(S("x_ready"), n + 1)
                func(sq, xT[:, :, :].rearrange("p c t -> p (c t)"), ACT.Square).then_inc(S("sq_ready"), 1)
                act.wait_ge(S("var_ready"), n + 1)
                func(st[:, :], st[:, :], ACT.Sqrt).then_inc(S("std_ready"), 1)

            def partition_norm(i):
                srcs, _, _, _, need = pns[i]
                await_need(act, need)
                for a, s in enumerate(srcs):
                    n = s.shape[-1]
                    last = func(sqb[:, 512 * (i % 2) + n * a:512 * (i % 2) + n * a + n], s, ACT.Square)
                last.then_inc(S("pn_sq"), 1)
                act.wait_ge(S("pn_var"), i + 1)
                n = srcs[0].shape[-1]
                func(pn[:, 0:n], pn[:, 0:n], ACT.Sqrt).then_inc(S("pn_std"), 1)

            def attention(name):
                us = list(u_span[name])

                def exps(u):
                    un = units[u]
                    if un["cmp"] is None:
                        act.wait_ge(S("nm_ready"), s_no[u])
                        if s_no[u] > 2:
                            act.wait_ge(S("t_done"), soft[s_no[u] - 3] + 1)
                        n0 = P if un["causal"] else T
                        b, p, m = 4 + s_no[u] % 2, pb[:, s_no[u] % 2, :], mx[:, s_no[u] % 2, :]
                        func(p[:, 0:n0], ps[:, b, 0:n0], ACT.Exp, bias=m[:, 2:3], scale=un["scale"],
                             accum_out=m[:, 4:5])
                        func(p[:, n0:n0 + T], ps[:, b, n0:n0 + T], ACT.Exp, bias=m[:, 3:4], scale=un["scale"],
                             accum_out=m[:, 5:6]).then_inc(S("exp_done"), 1)

                def move(u):
                    un = units[u]
                    act.wait_ge(S("t_done"), u + 1)
                    if u - 2 >= us[0]:
                        act.wait_ge(S("v_done"), u - 1)
                    if un["cmp"] is not None:
                        src, dst = ps[0:NCMP, 6 + u % 2, 0:T], ptb[0:NCMP, u % 2, 0:T]
                    else:
                        n = 384 if un["causal"] else 512
                        src, dst = ps[:, 6 + u % 2, 0:n], ptb[:, u % 2, 0:n]
                    func(dst, src, ACT.Copy).then_inc(S("pt_ready"), 1)

                for i, u in enumerate(us):
                    exps(u)
                    if i >= 1:
                        move(u - 1)
                move(us[-1])

            def route1(m):
                act.wait_ge(S("gmax_ready"), m + 1)
                for tt in range(TT):
                    last = func(rt_e[:, 4 * tt:4 * tt + 4], rt_lg[:, tt, 0:4], ACT.Exp, bias=rt_c[:, tt:tt + 1],
                                accum_out=rt_c[:, 2 + tt:3 + tt])
                last.then_inc(S("gsum_ready"), 1)
                act.wait_ge(S("v10_ready"), m + 1)
                func(rt_c[:, 6:8], rt_c[:, 4:6], ACT.Exp).then_inc(S("e1_ready"), 1)

            def tokens(m):
                act.wait_ge(S("tok_mm"), m + 1)
                func(h_tok[:, :, :].rearrange("p a d -> p (a d)"), psf(0, 4), ACT.Copy).then_inc(S("tok_ready"), 1)

            def route2(m):
                act.wait_ge(S("amax_ready"), m - 1)
                for tt in range(TT):
                    last = func(affL[:, 0, tt, :], ps[:, 4, 64 * tt:64 * tt + E2], ACT.Exp, bias=rt_c[:, tt:tt + 1],
                                accum_out=rt_c[:, 2 + tt:3 + tt])
                last.then_inc(S("asum_ready"), 1)

            def experts(m, groups, ff):
                g0, n0, per = moe_g0[m], slot_moe[m], 12 * (ff // 256)
                width, halves = min(ff, 512), max(1, ff // 512)
                with act.Fori(0, groups) as i:
                    act.wait_ge(S("xg_mm"), i + (g0 + 1))
                    func(xg[:, :, :].rearrange("p k s -> p (k s)"), psf(4, 2), ACT.Copy).then_inc(S("xg_ready"), 1)
                    act.wait_ge(S("C_mm"), i + (g0 + 1))
                    func(Cg[:, :], ps[:, 6, 0:T], ACT.Copy).then_inc(S("C_ready"), 1)
                    act.wait_ge(S("slot_used"), per * i + (n0 + 2 * per // 3))
                    if halves == 2:
                        func(sg[:, :], psf(0, 2), ACT.Silu).then_inc(S("sg_ready"), 1)
                    else:
                        func(sg[:, 0:width], ps[:, 0, 0:width], ACT.Silu).then_inc(S("sg_ready"), 1)
                    act.wait_ge(S("slot_used"), per * i + (n0 + per))
                    func(Yg, psf(6, 2), ACT.Copy).then_inc(S("Y_ready"), 1)

            def gla_stage():
                act.wait_ge(S("gl_mm"), 1)
                for d in range(2):
                    z = psf(4 + d)
                    link(func(lnb[d], z, ACT.Abs))
                    link(func(lnb[d], lnb[d], ACT.Exp, scale=-1.0))
                    func(lnb[d], lnb[d], ACT.Ln, bias=1.0).then_inc(S("ln_ready"), 1)
                for d in range(2):
                    act.wait_ge(S("cum_mm"), d + 1)
                    func(gE[:, 0, :], ps[:, 6, :], ACT.Exp)
                    func(gE[:, 1, :], ps[:, 6, :], ACT.Exp, scale=-1.0).then_inc(S("e_ready"), 1)
                    act.wait_ge(S("diff_ready"), d + 1)
                    func(gE[:, 2, :], gE[:, 2, :], ACT.Exp).then_inc(S("el_ready"), 1)
                    if d == 0:
                        act.wait_ge(S("qk_ready"), 1)

            act.wait_ge(S("xT_mm"), 1)
            func(xT[:, :, :].rearrange("p c t -> p (c t)"), psf(0, 4), ACT.Copy).then_inc(S("x_ready"), 1)
            act.wait_ge(S("cols_mm"), 1)
            func(colsA[:, :, :].rearrange("p a n -> p (a n)"), ps[:, 4, 0:384], ACT.Copy).then_inc(S("cols_ready"), 1)
            act.wait_ge(S("p_mm"), 1)
            func(pTall[:, :, :, :].rearrange("p l k t -> p (l k t)"), psf(5, 2), ACT.Copy).then_inc(S("pT_ready"), 1)
            act.wait_ge(S("cols_ready"), 1)
            act.wait_ge(S("cpad_zero"), 1)
            func(cpad[:, :, 0], colsA[:, 1, 0:8], ACT.Silu).then_inc(S("cpad_ready"), 1)
            act.wait_ge(S("lam_sum"), 1)
            func(misc[0:1, 4:6], misc[0:1, 2:4], ACT.Exp).then_inc(S("lam_exp"), 1)
            act.wait_ge(S("ang_ready"), 1)
            func(cosd[:, :, :].rearrange("p a t -> p (a t)"), cosd[:, :, :].rearrange("p a t -> p (a t)"), ACT.Sin)\
                .then_inc(S("cos_ready"), 1)
            for l in range(2):
                act.wait_ge(S("slot_used"), 24 * (l + 1))
                if l:
                    act.wait_ge(S("mod_ready"), 1)
                func(sq[:, 0:1536], psf(0, 3), ACT.Copy).then_inc(S("modrow"), 1)
            act.wait_ge(S("mod_ready"), 2)
            norm(0)
            evacuate(span["diff"])
            attention("diff")
            for i in range(4):
                partition_norm(i)
            norm(1)
            tokens(0)
            route1(0)
            experts(0, E1_GROUPS, E1_FF)
            norm(2)
            nsa_mid = nsa_src["gate"] + 1
            evacuate(range(ph["nsa"], nsa_mid))
            evacuate(range(nsa_mid, nsa_mid + 4))
            act.wait_ge(S("hsum_ready"), 1)
            for t in range(2):
                for m in range(2):
                    last = func(gh[:, t, m, :], rt[:, 240 + 60 * t + 30 * m:270 + 60 * t + 30 * m], ACT.Gelu_apprx_tanh,
                                bias=col("nsa_cmp_b1", 2 * t + m))
            last.then_inc(S("gelu"), 1)
            evacuate(range(nsa_mid + 4, ph["nsa_out"]))
            act.wait_ge(S("vt_mm"), 1)
            func(vt[:, 0:512], ps[:, 7, :], ACT.Copy).then_inc(S("vt_ready"), 1)
            act.wait_ge(S("sc_sub"), 1)
            for tt in range(TT):
                last = func(PC[:, tt, :, :], PC[:, tt, :, :], ACT.Exp, scale=0.125)
            last.then_inc(S("sc_exp"), 1)
            attention("nsa")
            norm(3)
            tokens(1)
            route1(1)
            experts(1, E1_GROUPS, E1_FF)
            norm(4)
            evacuate(range(ph["even"], ev_uq))
            partition_norm(4)
            partition_norm(5)
            evacuate(range(ev_uq, ph["even_out"]))
            attention("mla")
            gla_stage()
            partition_norm(6)
            partition_norm(7)
            norm(5)
            evacuate(span["ple0"])
            tokens(2)
            route2(2)
            experts(2, E2_GROUPS, E2_FF)
            norm(6)
            evacuate(span["odd"])
            for s in range(6):
                partition_norm(8 + s)
            attention("gqa")
            norm(7)
            evacuate(span["ple1"])
            tokens(3)
            route2(3)
            experts(3, E2_GROUPS, E2_FF)
            norm(8)
            act.wait_ge(S("tok_mm"), 5)
            for tt in range(TT):
                func(h_tok[:, tt, :], psf(2 * tt, 2), ACT.Copy).then_inc(S("out_ready"), 1)

        @block.vector
        def _(dve):
            V = nc.vector
            chain = [0]

            def link(ins):
                chain[0] += 1
                ins.then_inc(S("dve_chain"), 1)
                dve.wait_ge(S("dve_chain"), chain[0])

            def norm(n):
                xf = xT[:, :, :].rearrange("p c t -> p (c t)")
                if n >= 5:
                    dve.wait_ge(S("mean_mm"), n - 4)
                    link(V.tensor_scalar(st[:, :], ps[:, 3, 0:T], 1.0 / D, None, ALU.mult))
                    V.tensor_tensor(xT[:, :, :], xT[:, :, :], st[:, :].rearrange("p (o t) -> p o t", o=1).to_broadcast([P, C, T]), ALU.subtract)\
                        .then_inc(S("xc_ready"), 1)
                    dve.wait_ge(S("xc_ready"), n - 4)
                dve.wait_ge(S("sq_mm"), n + 1)
                V.tensor_scalar(st[:, :], ps[:, 2, 0:T], 1.0 / D, EPS, ALU.mult, ALU.add).then_inc(S("var_ready"), 1)
                dve.wait_ge(S("std_ready"), n + 1)
                link(V.reciprocal(st[:, :], st[:, :]))
                dst = hT if n < 4 else xT
                link(V.tensor_tensor(dst[:, :, :], xT[:, :, :], st[:, :].rearrange("p (o t) -> p o t", o=1).to_broadcast([P, C, T]), ALU.mult))
                for c in range(C):
                    if n < 4:
                        l, a = n // 2, n % 2
                        last = V.tensor_scalar(dst[:, c, :], dst[:, c, :], modA[:, n, c:c + 1],
                                               mod[:, l, 24 * a + c:24 * a + c + 1], ALU.mult, ALU.add)
                    elif n == 4:
                        last = V.tensor_scalar(dst[:, c, :], dst[:, c, :], col("final_g", c), None, ALU.mult)
                    else:
                        l, which = (n - 5) // 2, "ln1" if n % 2 else "ln2"
                        last = V.tensor_scalar(dst[:, c, :], dst[:, c, :], col(which + "_g_2", 8 * l + c),
                                               col(which + "_b_2", 8 * l + c), ALU.mult, ALU.add)
                last.then_inc(S("h_ready"), 1)
                dve.wait_ge(S("h_ready"), n + 1)

            rope_at = [0]

            def ropes_until(end):
                while rope_at[0] < end:
                    i = rope_at[0]
                    buf, n, r0, rows, _, cos, sin, _ = ropes[i]
                    rr = slice(r0, r0 + rows)
                    b3 = buf[rr, :].rearrange("p (c t) -> p c t", c=n)
                    t3 = rtmp[rr, 0:n * T].rearrange("p (c t) -> p c t", c=n)
                    p3 = ps[rr, 2 + i % 2, 0:n * T].rearrange("p (c t) -> p c t", c=n)
                    cb = cos[rr, :].rearrange("p (o t) -> p o t", o=1).to_broadcast([rows, n, T])
                    sb_ = sin[rr, :].rearrange("p (o t) -> p o t", o=1).to_broadcast([rows, n, T])
                    dve.wait_ge(S("rope_mm"), i + 1)
                    V.tensor_tensor(t3, p3, sb_, ALU.mult)
                    link(V.tensor_tensor(b3, b3, cb, ALU.mult))
                    V.tensor_tensor(b3, b3, t3, ALU.add).then_inc(S("rope_done"), 1)
                    dve.wait_ge(S("rope_done"), i + 1)
                    rope_at[0] += 1

            def partition_norm(i):
                srcs, _, size, apply, _ = pns[i]
                n = srcs[0].shape[-1]
                dve.wait_ge(S("pn_mm"), i + 1)
                V.tensor_scalar(pn[:, 0:n], ps[:, 7, 0:n], 1.0 / size, EPS, ALU.mult, ALU.add)\
                    .then_inc(S("pn_var"), 1)
                dve.wait_ge(S("pn_std"), i + 1)
                link(V.reciprocal(pn[:, 0:n], pn[:, 0:n]))
                for src, c, dst, times in apply:
                    last = V.scalar_tensor_tensor(dst, src, c, pn[:, 0:n], ALU.mult, ALU.mult)
                    if times is not None:
                        link(last)
                        last = V.tensor_tensor(dst, dst, times, ALU.mult)
                last.then_inc(S("pn_done"), 1)
                dve.wait_ge(S("pn_done"), i + 1)

            def attention(name):
                us = list(u_span[name])

                def neg_max(u):
                    un = units[u]
                    if un["cmp"] is not None:
                        return
                    dve.wait_ge(S("s_done"), s_no[u])
                    b, m = 4 + s_no[u] % 2, mx[:, s_no[u] % 2, :]
                    if un["causal"]:
                        V.tensor_reduce(m[:, 0:1], ps[:, b, 0:P], AX, ALU.max)
                        link(V.tensor_reduce(m[:, 1:2], ps[:, b, P:P + T], AX, ALU.max))
                    else:
                        link(V.tensor_reduce(m[:, 0:2], ps[:, b, :].rearrange("p (a n) -> p a n", a=2), AX, ALU.max))
                    V.tensor_scalar(m[:, 2:4], m[:, 0:2], -un["scale"], None, ALU.mult).then_inc(S("nm_ready"), 1)

                def normalise(u):
                    un = units[u]
                    if un["cmp"] is not None:
                        return
                    dve.wait_ge(S("exp_done"), s_no[u])
                    m, p, n0 = mx[:, s_no[u] % 2, :], pb[:, s_no[u] % 2, :], P if un["causal"] else T
                    link(V.reciprocal(m[:, 6:8], m[:, 4:6]))
                    if un["coef"] is not None:
                        link(V.tensor_tensor(m[:, 6:8], m[:, 6:8], un["coef"], ALU.mult))
                    V.tensor_scalar(p[:, 0:n0], p[:, 0:n0], m[:, 6:7], None, ALU.mult)
                    V.tensor_scalar(p[:, n0:n0 + T], p[:, n0:n0 + T], m[:, 7:8], None, ALU.mult)\
                        .then_inc(S("p_ready"), 1)

                def outputs(u):
                    un = units[u]
                    if un["last"]:
                        dve.wait_ge(S("v_done"), u + 1)
                        V.tensor_copy(obanks[un["o"]], ps[:, 2 + un["o"] % 2, 0:T]).then_inc(S("o_evac"), 1)

                for i, u in enumerate(us):
                    neg_max(u)
                    if i >= 1:
                        normalise(u - 1)
                    if i >= 3:
                        outputs(u - 3)
                normalise(us[-1])
                for u in us[-3:]:
                    outputs(u)
                dve.wait_ge(S("o_evac"), o_after[name])

            def residual(name, gate=None):
                for j in span[name]:
                    s, r = jobs[j]["evac"], res_no[j]
                    dve.wait_ge(S(finished(j)[0]), finished(j)[1])
                    if gate is not None:
                        for a in range(2):
                            c = 2 * s + a
                            last = V.scalar_tensor_tensor(xT[:, c, :], ps[:, j % 2, T * a:T * a + T],
                                                          mod[:, gate, 16 + c:17 + c], xT[:, c, :], ALU.mult, ALU.add)
                    else:
                        last = V.scalar_tensor_tensor(pair_dst(xT, s), pair_dst(xT, s), ALPHA, ps[:, j % 2, :],
                                                      ALU.mult, ALU.add)
                    last.then_inc(S("res_evac"), 1)
                dve.wait_ge(S("res_evac"), r + 1)
                V.memset(misc[:, 60:61], 0.0).then_inc(S("x_ready"), 1)

            def route1(m):
                for_sel = rt_sel(E1)
                dve.wait_ge(S("logits"), m + 1)
                for tt in range(TT):
                    V.tensor_copy(rt_lg[:, tt, :], ps[:, 4, 64 * tt:64 * tt + 36])
                link(V.memset(rt_g8[:, :, :], -NEG))
                for tt in range(TT):
                    last = V.tensor_copy(rt_g8[:, tt, 0:4], rt_lg[:, tt, 0:4])
                link(last)
                for tt in range(TT):
                    link(V.max(rt_m8[:, tt, :], rt_g8[:, tt, :]))
                    last = V.max_index(i8[:, 0, tt, :], rt_m8[:, tt, :], rt_g8[:, tt, :])
                link(last)
                V.tensor_scalar(rt_c[:, 0:2], rt_m8[:, :, 0], -1.0, None, ALU.mult).then_inc(S("gmax_ready"), 1)
                link(V.tensor_copy(rt_c[:, 8:10], i8[:, 0, :, 0]))
                for tt in range(TT):
                    link(V.tensor_scalar(rt_oh4[:, tt, :], iota[:, 0:4], rt_c[:, 8 + tt:9 + tt], None, ALU.is_equal))
                    msk = rt_oh4[:, tt, :].rearrange("p (g o) -> p g o", o=1).to_broadcast([P, 4, 8])
                    le = rt_lg[:, tt, 4:36].rearrange("p (g e) -> p g e", g=4)
                    lm = rt_le[:, tt, :].rearrange("p (g e) -> p g e", g=4)
                    link(V.tensor_tensor(lm, le, msk, ALU.mult))
                    link(V.tensor_scalar(rt_oh4[:, tt, :], rt_oh4[:, tt, :], NEG, -NEG, ALU.mult, ALU.add))
                    link(V.tensor_tensor(lm, lm, msk, ALU.add))
                    link(V.max(rt_m8[:, tt, :], rt_le[:, tt, :]))
                    last = V.max_index(i8[:, 1, tt, :], rt_m8[:, tt, :], rt_le[:, tt, :])
                link(last)
                V.tensor_tensor(rt_c[:, 4:6], rt_m8[:, :, 1], rt_m8[:, :, 0], ALU.subtract).then_inc(S("v10_ready"), 1)
                V.tensor_copy(rt_c[:, 10:12], i8[:, 1, :, 0])
                link(V.tensor_copy(rt_c[:, 12:14], i8[:, 1, :, 1]))
                for tt in range(TT):
                    for a in range(2):
                        link(V.tensor_scalar(rt_oh[:, a, tt, :], iota[:, 0:E1], rt_c[:, 10 + 2 * a + tt:11 + 2 * a + tt],
                                             None, ALU.is_equal))
                V.tensor_tensor(for_sel, rt_oh[:, 0, :, :], rt_oh[:, 1, :, :], ALU.add).then_inc(S("sel_ready"), 1)
                dve.wait_ge(S("gsum_ready"), m + 1)
                dve.wait_ge(S("e1_ready"), m + 1)
                link(V.tensor_scalar(rt_c[:, 14:16], rt_c[:, 6:8], 1.0, None, ALU.add))
                link(V.tensor_tensor(rt_c[:, 14:16], rt_c[:, 14:16], rt_c[:, 2:4], ALU.mult))
                link(V.reciprocal(Lw[:, 2, :], rt_c[:, 14:16]))
                link(V.tensor_tensor(Lw[:, 3, :], Lw[:, 2, :], rt_c[:, 6:8], ALU.mult))
                dve.wait_ge(S("rank_mm"), m + 1)
                link(V.tensor_copy(rt_c[0:32, 16:17], ps[0:32, 5, 128:129]))
                link(V.tensor_scalar(rt_t8, iota[0:32, 0:8], float(BLK), rt_c[0:32, 16:17], ALU.mult, ALU.is_lt))
                link(V.tensor_reduce(rt_nblk, rt_t8, AX, ALU.add))
                V.tensor_scalar(rt_nblkB, K("ones")[0:32, :], rt_nblk, None, ALU.mult).then_inc(S("nblk_ready"), 1)
                dve.wait_ge(S("base_mm"), m + 1)
                link(V.tensor_copy(rt_base, ps[:, 5, 192:227]))
                V.tensor_scalar(rt_cmp, iota[0:32, 0:E1_BLOCKS], rt_base[0:32, 34:35], None, ALU.is_ge)\
                    .then_inc(S("cmp_ready"), 1)
                for tt in range(TT):
                    link(V.scalar_tensor_tensor(rt_L[:, tt, :], rt_base[:, 0:E1], float(BLK), ps[:, 5, 64 * tt:64 * tt + E1],
                                                ALU.mult, ALU.add))
                for a in range(2):
                    link(V.tensor_tensor(rt_oh[:, a, :, :], rt_oh[:, a, :, :], rt_L[:, :, :], ALU.mult))
                    link(V.tensor_reduce(Lw[:, a, :], rt_oh[:, a, :, :], AX, ALU.add))
                dve.wait_ge(S("count_mm"), m + 1)
                V.tensor_scalar(ids[0:1, 0, :], ps[0:1, 6, 0:E1_BLOCKS], -1.0, None, ALU.add)
                V.tensor_scalar(ids[0:1, 1, :], iota[0:1, 0:E1_BLOCKS], rt_base[0:1, 32:33], None, ALU.is_lt)\
                    .then_inc(S("ids_ready"), 1)
                V.memset(yT[:, :, :], 0.0).then_inc(S("y_added"), 1)
                link(V.tensor_copy(iog[:, :], iota))

            def route2(m):
                dve.wait_ge(S("logits"), m + 1)
                lg = ps[:, 4, 0:128].rearrange("p (a n) -> p a n", a=TT)[:, :, 0:E2]
                link(V.tensor_reduce(rt_c[:, 4:6], lg, AX, ALU.max))
                V.tensor_scalar(rt_c[:, 0:2], rt_c[:, 4:6], -1.0, None, ALU.mult).then_inc(S("amax_ready"), 1)
                dve.wait_ge(S("asum_ready"), m - 1)
                link(V.reciprocal(rt_c[:, 4:6], rt_c[:, 2:4]))
                for tt in range(TT):
                    last = V.tensor_scalar(affL[:, 0, tt, :], affL[:, 0, tt, :], rt_c[:, 4 + tt:5 + tt], None, ALU.mult)
                last.then_inc(S("aff_ready"), 1)
                dve.wait_ge(S("affT_mm"), m - 1)
                link(V.tensor_copy(rt_selT, ps[0:E2, 6, 0:T]))
                for r in range(2 * T // E2 // 8):
                    link(V.max(rt_m8e, rt_selT))
                    link(V.match_replace(rt_selT, rt_m8e, rt_selT, -1.0))
                V.tensor_scalar(rt_selT, rt_selT, 0.0, None, ALU.is_lt).then_inc(S("selT_ready"), 1)
                dve.wait_ge(S("sel_mm"), m - 1)
                sel = rt_sel(E2)
                V.tensor_copy(sel, ps[:, 6, 256:288].rearrange("p (a n) -> p a n", a=TT)).then_inc(S("sel_ready"), 1)
                dve.wait_ge(S("sel_ready"), m + 1)
                dve.wait_ge(S("rank_mm"), m + 1)
                rk = ps[:, 5, 0:128].rearrange("p (a n) -> p a n", a=TT)[:, :, 0:E2]
                link(V.scalar_tensor_tensor(affL[:, 1, :, :], rk, 1.0, sel, ALU.add, ALU.mult))
                link(V.tensor_scalar(affL[:, 1, :, :], affL[:, 1, :, :], -1.0, None, ALU.add))
                dve.wait_ge(S("proj_evac"), acts_before[ph["ple0" if m == 2 else "ple1"] + 7] + 1)
                V.tensor_tensor(yT[:, :, :], kT[:, :, :], qT[:, :, :], ALU.mult).then_inc(S("y_added"), 1)

            def experts(m, groups, ff):
                g0 = moe_g0[m]
                base = [chain[0]]
                steps = [0]

                with dve.Fori(0, groups) as i:
                    n_links = 7 if m < 2 else 2
                    at_link = [0]

                    def llink(ins):
                        at_link[0] += 1
                        ins.then_inc(S("dve_chain"), 1)
                        dve.wait_ge(S("dve_chain"), n_links * i + (base[0] + at_link[0]))

                    dve.wait_ge(S("y_added"), i + (g0 + m + 1))
                    if m < 2:
                        for tt in range(TT):
                            llink(V.tensor_scalar(Dg[:, tt, :], iog[:, :], Lw[:, 0, tt:tt + 1], None, ALU.is_equal))
                            V.scalar_tensor_tensor(Dg[:, tt, :], iog[:, :], Lw[:, 1, tt:tt + 1], Dg[:, tt, :],
                                                   ALU.is_equal, ALU.add)
                            V.tensor_scalar(DAg[:, tt, :], iog[:, :], Lw[:, 0, tt:tt + 1], Lw[:, 2, tt:tt + 1],
                                            ALU.is_equal, ALU.mult)
                            llink(V.tensor_scalar(rtmp[:, 0:P], iog[:, :], Lw[:, 1, tt:tt + 1], Lw[:, 3, tt:tt + 1],
                                                  ALU.is_equal, ALU.mult))
                            last = V.tensor_tensor(DAg[:, tt, :], DAg[:, tt, :], rtmp[:, 0:P], ALU.add)
                            if tt == 0:
                                llink(last)
                            else:
                                last.then_inc(S("D_ready"), 1)
                        dve.wait_ge(S("D_ready"), i + (g0 + 1))
                        llink(V.tensor_scalar(iog[:, :], iog[:, :], float(P), None, ALU.add))
                        llink(V.memset(misc[:, 61:62], 0.0))
                    else:
                        for tt in range(TT):
                            d3 = Dg[:, tt, :].rearrange("p (j s) -> p j s", j=4)
                            io = iota[:, 0:32].rearrange("p (o s) -> p o s", o=1).to_broadcast([P, 4, 32])
                            lp = affL[:, 1, tt, bass.ds(4 * i, 4)].rearrange("p (j o) -> p j o", o=1)\
                                .to_broadcast([P, 4, 32])
                            af = affL[:, 0, tt, bass.ds(4 * i, 4)].rearrange("p (j o) -> p j o", o=1)\
                                .to_broadcast([P, 4, 32])
                            llink(V.tensor_tensor(d3, io, lp, ALU.is_equal))
                            last = V.tensor_tensor(DAg[:, tt, :].rearrange("p (j s) -> p j s", j=4), d3, af, ALU.mult)
                        last.then_inc(S("D_ready"), 1)
                    dve.wait_ge(S("sg_ready"), i + (g0 + 1))
                    if ff == 1024:
                        V.tensor_tensor(hid, sg[:, :], psf(2, 2), ALU.mult).then_inc(S("hid_ready"), 1)
                    else:
                        V.tensor_tensor(hid[:, 0:ff], sg[:, 0:ff], ps[:, 2, 0:ff], ALU.mult)\
                            .then_inc(S("hid_ready"), 1)
                    dve.wait_ge(S("hT_mm"), i + (g0 + 1))
                    V.tensor_copy(hidT[:, 0:ff // P, :].rearrange("p c s -> p (c s)"),
                                  psf(4, 2)[:, 0:ff]).then_inc(S("hidT_ready"), 1)
                    dve.wait_ge(S("y_mm"), i + (g0 + 1))
                    V.tensor_tensor(yT[:, :, :].rearrange("p c t -> p (c t)"), yT[:, :, :].rearrange("p c t -> p (c t)"),
                                    psf(0, 4), ALU.add).then_inc(S("y_added"), 1)
                if m < 2:
                    assert at_link[0] == 7, at_link[0]
                else:
                    assert at_link[0] == 2, at_link[0]
                chain[0] += n_links * groups
                dve.wait_ge(S("y_added"), g0 + groups + m + 1)
                if m < 2:
                    for c in range(C):
                        last = V.scalar_tensor_tensor(xT[:, c, :], yT[:, c, :], mod[:, m, 40 + c:41 + c], xT[:, c, :],
                                                      ALU.mult, ALU.add)
                else:
                    last = V.scalar_tensor_tensor(xT[:, :, :], xT[:, :, :], ALPHA, yT[:, :, :], ALU.mult, ALU.add)
                last.then_inc(S("x_ready"), 1)
                dve.wait_ge(S("x_ready"), 2 * m + 3)

            def gla_stage():
                for d in range(2):
                    dve.wait_ge(S("ln_ready"), 2)
                    lf = la[d].rearrange("p a n -> p (a n)")
                    link(V.tensor_scalar(lf, psf(4 + d), 0.0, None, ALU.min))
                    link(V.tensor_tensor(lf, lf, lnb[d], ALU.subtract))
                    V.tensor_scalar(lf, lf, 1.0 / 16.0, None, ALU.mult).then_inc(S("la_ready"), 1)
                for d in range(2):
                    dve.wait_ge(S("e_ready"), d + 1)
                    last_tok = 63 if d == 0 else 0
                    cum = ps[:, 6, :].rearrange("p (n l) -> p n l", l=64)
                    link(V.tensor_copy(gdec[:, 0, :], cum[:, :, last_tok]))
                    lb = gdec[:, 0, :].rearrange("p (n o) -> p n o", o=1).to_broadcast([P, 8, 64])
                    V.tensor_copy(gdec[:, 1, :], gE[:, 0, :].rearrange("p (n l) -> p n l", l=64)[:, :, last_tok])
                    V.tensor_tensor(gE[:, 2, :].rearrange("p (n l) -> p n l", l=64), lb, cum, ALU.subtract)\
                        .then_inc(S("diff_ready"), 1)
                    qf, kf = gqT.rearrange("p c t -> p (c t)"), gkT.rearrange("p c t -> p (c t)")
                    V.scalar_tensor_tensor(qg[d].rearrange("p c t -> p (c t)"), qf, 0.125, gE[:, 0, :], ALU.mult, ALU.mult)
                    V.tensor_tensor(kg[d].rearrange("p c t -> p (c t)"), kf, gE[:, 1, :], ALU.mult)
                    dve.wait_ge(S("el_ready"), d + 1)
                    V.tensor_tensor(kd.rearrange("p c t -> p (c t)"), kf, gE[:, 2, :], ALU.mult)\
                        .then_inc(S("qk_ready"), 1)
                    dve.wait_ge(S("at_mm"), d + 1)
                    tri = K("tri_f" if d == 0 else "tri_b").rearrange("p (o n) -> p o n", o=1).to_broadcast([P, 8, P])
                    V.tensor_tensor(at[d], psf(4, 2).rearrange("p (a n) -> p a n", a=8), tri, ALU.mult)
                    V.tensor_copy(kdt.rearrange("p a n -> p (a n)"), ps[:, 2, :]).then_inc(S("at_ready"), 1)
                    dve.wait_ge(S("u_mm"), d + 1)
                    order = [1, 2, 3] if d == 0 else [2, 1, 0]
                    for c in range(2):
                        for x, n in enumerate(order):
                            prev = n - 1 if d == 0 else n + 1
                            u0 = T * c + P * (prev // 2)
                            u = ps[:, 4 + prev % 2, u0:u0 + P]
                            if x == 0:
                                link(V.tensor_copy(stt_[d][:, c, n, :], u))
                            else:
                                link(V.scalar_tensor_tensor(stt_[d][:, c, n, :], stt_[d][:, c, prev, :],
                                                            gdec[:, 1, 4 * c + prev:4 * c + prev + 1], u,
                                                            ALU.mult, ALU.add))
                    V.memset(misc[:, 62:63], 0.0).then_inc(S("st_ready"), 1)
                for s in range(2):
                    dve.wait_ge(S("go_mm"), 2)
                    V.tensor_copy(oT[:, 4 + s:8:2, :], ps[:, 4 + s, :].rearrange("p (c t) -> p c t", c=2))\
                        .then_inc(S("gla_evac"), 1)
                dve.wait_ge(S("gla_evac"), 2)

            V.memset(cpad[:, :, :], 0.0).then_inc(S("cpad_zero"), 1)
            dve.wait_ge(S("consts"), 16)
            V.tensor_copy(identb[:, :], ident)
            V.tensor_copy(trib[:, :], K("tri_neg"))
            dve.wait_ge(S("params"), 16 * N_PARAMS)
            pos = st[:, :]
            link(V.tensor_copy(pos, posi))
            link(V.tensor_scalar(pos, pos, K("inv_freq"), None, ALU.mult))
            two_pi = 2.0 * math.pi
            hi = 6.28125
            lo = two_pi - hi
            magic = 1.5 * 2.0 ** 23
            for a, (shift, add) in enumerate(((0.25, math.pi / 2), (0.0, 0.0))):
                n, r = pn[:, 0:T], cosd[:, a, :]
                link(V.tensor_scalar(n, pos, 1.0 / two_pi, shift, ALU.mult, ALU.add))
                link(V.tensor_scalar(n, n, magic, None, ALU.add))
                link(V.tensor_scalar(n, n, -magic, None, ALU.add))
                link(V.scalar_tensor_tensor(r, n, -hi, pos, ALU.mult, ALU.add))
                link(V.scalar_tensor_tensor(r, n, -lo, r, ALU.mult, ALU.add))
                link(V.tensor_scalar(r, r, add, 3.1415925, ALU.add, ALU.min))
                link(V.tensor_scalar(r, r, -3.1415925, None, ALU.max))
            V.memset(misc[:, 59:60], 0.0).then_inc(S("ang_ready"), 1)
            lam = rows1[0:1, LAM0:LAM0 + 256].rearrange("p (a b d) -> p a b d", a=2, b=2)
            pr = rows1[0:1, 840:968].rearrange("p (a d) -> p a d", a=2)
            link(V.tensor_tensor(pr, lam[:, :, 0, :], lam[:, :, 1, :], ALU.mult))
            V.tensor_reduce(misc[0:1, 2:4], pr, AX, ALU.add).then_inc(S("lam_sum"), 1)
            dve.wait_ge(S("lam_exp"), 1)
            link(V.tensor_tensor(misc[0:1, 8:9], misc[0:1, 5:6], misc[0:1, 4:5], ALU.subtract))
            V.tensor_scalar(misc[0:1, 8:9], misc[0:1, 8:9], -LAMBDA_INIT, None, ALU.add).then_inc(S("lam_ready"), 1)
            dve.wait_ge(S("lam_mm"), 1)
            V.tensor_copy(coef[:, 0:1], ps[:, 7, 0:1])
            V.tensor_copy(coef[:, 1:2], ps[:, 7, 0:1])
            dve.wait_ge(S("cols_ready"), 1)
            link(V.tensor_scalar(coef[:, 2:3], col("diff_subln_g"), 1.0 - LAMBDA_INIT, None, ALU.mult))
            for l in range(2):
                dve.wait_ge(S("modT_mm"), l + 1)
                for h in range(2):
                    src = psf(3, 3).rearrange("p (i h x) -> p i h x", h=2, x=P)[:, :, h, 0:P:32]
                    dst = mod[:, l, :].rearrange("p (i j h) -> p i j h", i=6, h=2)[:, :, :, h]
                    b_ = colsA[:, 0, 48 * l:48 * l + 48].rearrange("p (i j h) -> p i j h", i=6, h=2)[:, :, :, h]
                    last = V.tensor_tensor(dst, src, b_, ALU.add)
                last.then_inc(S("mod_ready"), 1)
                dve.wait_ge(S("mod_ready"), l + 1)
                for a in range(2):
                    link(V.scalar_tensor_tensor(modA[:, 2 * l + a, :], mod[:, l, 24 * a + 8:24 * a + 16], 1.0,
                                                colsA[:, 0, 96 + 16 * l + 8 * a:104 + 16 * l + 8 * a], ALU.add, ALU.mult))
            dve.wait_ge(S("cos_ready"), 1)
            dve.wait_ge(S("pT_ready"), 1)
            norm(0)
            ropes_until(r_nsa)
            dve.wait_ge(S("proj_evac"), acts_before[ph["diff_out"]])
            V.memset(misc[:, 58:59], 0.0).then_inc(S("att_go"), 1)
            attention("diff")
            for i in range(4):
                partition_norm(i)
            residual("diff_out", gate=0)
            norm(1)
            route1(0)
            experts(0, E1_GROUPS, E1_FF)
            norm(2)
            ropes_until(r_even)
            dve.wait_ge(S("proj_evac"), acts_before[nsa_src["c1"]] + 1)
            for t in range(2):
                for g in range(2):
                    kc = kcp[t][:, g, :]
                    win = bass.AP(kc.tensor, kc.offset, [list(kc.ap[0]), [1, 16], [8, NCMP]])
                    last = V.tensor_tensor(blk[:, t, :, g, :], win,
                                           colsA[:, 2, 16 * t:16 * t + 16].rearrange("p (j o) -> p j o", o=1)
                                           .to_broadcast([P, 16, NCMP]), ALU.add)
            last.then_inc(S("blk_ready"), 1)
            cmp_jobs = acts_before[nsa_src["gate"]] + 1 + 4
            dve.wait_ge(S("proj_evac"), cmp_jobs)
            V.tensor_tensor(rt[:, 240:360], rt[:, 0:120], rt[:, 120:240], ALU.add).then_inc(S("hsum_ready"), 1)
            ok = K("cmp_ok").rearrange("p (a n) -> p a n", a=TT)
            link(V.tensor_scalar(rt[:, 400:430], K("cmp_ok"), NEG, -NEG, ALU.mult, ALU.add))
            for tt in range(TT):
                dve.wait_ge(S("sc_mm"), TT)
                pc = PC[:, tt, :, :]
                neg = rt[:, 400 + NCMP * tt:400 + NCMP * tt + NCMP].rearrange("p (o n) -> p o n", o=1)\
                    .to_broadcast([P, 8, NCMP])
                for half in range(2):
                    s = ps[:, 4 + half, 8 * NCMP * tt:8 * NCMP * (tt + 1)].rearrange("p (h n) -> p h n", h=8)
                    link(V.tensor_tensor(PC[:, tt, half:16:2, :], s, neg, ALU.add))
                link(V.tensor_reduce(rt[:, 440:456], pc, AX, ALU.max))
                link(V.tensor_tensor(pc, pc, rt[:, 440:456].rearrange("p (h o) -> p h o", o=1)
                                     .to_broadcast([P, 16, NCMP]), ALU.subtract))
            V.memset(misc[:, 57:58], 0.0).then_inc(S("sc_sub"), 1)
            dve.wait_ge(S("sc_exp"), 1)
            for tt in range(TT):
                pc = PC[:, tt, :, :]
                okb = ok[:, tt:tt + 1, :].to_broadcast([P, 16, NCMP])
                link(V.tensor_tensor(pc, pc, okb, ALU.mult))
                link(V.tensor_reduce(rt[:, 440:456], pc, AX, ALU.add))
                link(V.tensor_scalar(rt[:, 440:456], rt[:, 440:456], 1e-30, None, ALU.max))
                link(V.reciprocal(rt[:, 460:476], rt[:, 440:456]))
                link(V.tensor_tensor(rt[:, 460:476], rt[:, 460:476], gates[:, tt, 0:48:3], ALU.mult))
                link(V.tensor_tensor(pc, pc, rt[:, 460:476].rearrange("p (h o) -> p h o", o=1)
                                     .to_broadcast([P, 16, NCMP]), ALU.mult))
            dve.wait_ge(S("vt_ready"), 1)
            V.memset(misc[:, 58:59], 0.0).then_inc(S("att_go"), 1)
            attention("nsa")
            residual("nsa_out", gate=1)
            norm(3)
            route1(1)
            experts(1, E1_GROUPS, E1_FF)
            norm(4)
            partition_norm(4)
            partition_norm(5)
            ropes_until(r_odd)
            dve.wait_ge(S("proj_evac"), acts_before[ph["even_out"]])
            V.tensor_copy(kT[64:96, :, :], kpe[64:96, :].rearrange("p (o t) -> p o t", o=1).to_broadcast([32, C, T]))\
                .then_inc(S("att_go"), 1)
            attention("mla")
            gla_stage()
            partition_norm(6)
            partition_norm(7)
            residual("even_out")
            norm(5)
            route2(2)
            experts(2, E2_GROUPS, E2_FF)
            norm(6)
            for s in range(6):
                partition_norm(8 + s)
                if s:
                    ropes_until(r_odd + s)
            ropes_until(r_end)
            dve.wait_ge(S("proj_evac"), acts_before[ph["odd_out"]])
            V.memset(misc[:, 58:59], 0.0).then_inc(S("att_go"), 1)
            attention("gqa")
            residual("odd_out")
            norm(7)
            route2(3)
            experts(3, E2_GROUPS, E2_FF)
            norm(8)

        @block.gpsimd
        def _(pool):
            nc.gpsimd.memset(rowsA[:, :, :], 0.0).then_inc(S("rows_zero"), 1)


_INS = ["x", "c", "positions", "ada_w", "ada_b", "norm_g", "final_g", "diff_w_in", "diff_w_out", "diff_lambda",
        "diff_subln_g", "nsa_w_in", "nsa_w_out", "nsa_cmp_pos", "nsa_cmp_w1", "nsa_cmp_b1", "nsa_cmp_w2",
        "moe_w_group", "moe_b_group", "moe_w_expert", "moe_b_expert", "moe_w_gate", "moe_w_up", "moe_w_down",
        "p_2", "w_in_even_2", "mla_q_norm_2", "w_uq_2", "mla_kv_norm_2", "w_ukv_2", "gla_gate_w_fwd_2",
        "gla_gate_b_fwd_2", "gla_gate_w_bwd_2", "gla_gate_b_bwd_2", "gla_norm_2", "w_in_odd_2", "gqa_q_norm_2",
        "gqa_k_norm_2", "w_o_2", "ln1_g_2", "ln1_b_2", "router_w_2", "w1_2", "w3_2", "w2_2", "ple_gate_w_2",
        "ple_gate_b_2", "ple_w_2", "ln2_g_2", "ln2_b_2"]


def kernel(**inputs):
    import concourse.bacc as _bacc
    from concourse.bass_utils import run_bass_kernel_spmd as _run

    nc = _bacc.Bacc("TRN2", target_bir_lowering=False, num_devices=1)
    arrays, args = {}, {}
    for name in _INS + ["consts"]:
        a = np.ascontiguousarray(inputs[name] if name != "consts" else shape_constants())
        arrays[f"in_{name}"] = a
        args[name] = nc.dram_tensor(f"in_{name}", a.shape, mybir.dt.from_np(a.dtype), kind="ExternalInput").ap()
    out = nc.dram_tensor("out_0", (1, T, D), F32, kind="ExternalOutput").ap()
    program(nc, args, out)
    r = _run(nc, [arrays], core_ids=[0])
    return r.results[0]["out_0"]
```

```python
import math
from contextlib import ExitStack

import numpy as np

import concourse.bass as bass
from concourse import mybir

F32 = mybir.dt.float32
BF16 = mybir.dt.bfloat16
I32 = mybir.dt.int32
U32 = mybir.dt.uint32
ALU = mybir.AluOpType
ACT = mybir.ActivationFunctionType
AX = mybir.AxisListType.X

P = 128
T = 256
TT = T // P
D = 1024
C = D // P
EPS = 1e-6
NEG = 1e30
RING = 12
SLOT = 2048
ROT_DIM = 16
ALPHA = (2.0 * 2) ** 0.25
LAMBDA_INIT = 0.8 - 0.6 * math.exp(-0.3 * 0)
NSA_Q = 1024
NCMP = T // 16 - 1
E1, TOPK, E1_FF = 32, 2, 256
BLK = 32
E1_BLOCKS = (TOPK * T + E1 * (BLK - 1)) // BLK + 1
E1_GROUPS = E1_BLOCKS // 4
E2, E2_FF = 16, 1024
E2_GROUPS = E2 // 4
assert E1_BLOCKS % 4 == 0 and RING == 12

CONST = {}


def _layout():
    at = 0
    for name, n in (("ident", P), ("ones", P), ("ones64", P), ("rot16", P), ("rot64", P), ("rot_mla", P),
                    ("before", P), ("tri_f", P), ("tri_b", P), ("iota", P), ("slots", P), ("tri_neg", P),
                    ("cos_m", T), ("sin_m", T), ("cos_g", T), ("sin_g", T),
                    ("fold", 2 * NCMP), ("cmp_ok", TT * NCMP), ("inv_freq", 1)):
        CONST[name] = (at, n)
        at += n
    return at


N_CONST = _layout()
N_PARAMS, N_LATE = 21, 20
ADA_FIRST = 2
ADA_JOB = (4, 7, 9, 11)
ADA_STEP = (0, 2, 4, 7, 10, 13)


def shape_constants():
    c = np.zeros((P, N_CONST), np.float32)

    def put(name, a):
        at, n = CONST[name]
        c[:a.shape[0], at:at + n] = a

    def rotation(size, base, half, parts):
        r = np.zeros((P, P), np.float32)
        for b in range(base, parts, size):
            for i in range(half):
                r[b + half + i, b + i] = -1.0
                r[b + i, b + half + i] = 1.0
        return r

    i = np.arange(P)
    put("ident", np.eye(P, dtype=np.float32))
    put("ones", np.ones((P, P), np.float32))
    put("ones64", (i[:, None] // 64 == i[None, :] // 64).astype(np.float32))
    put("rot16", rotation(64, 0, ROT_DIM // 2, P))
    put("rot64", rotation(64, 0, 32, P))
    put("rot_mla", rotation(64, 64, 16, P))
    put("before", (i[:, None] < i[None, :]).astype(np.float32))
    same = i[:, None] // 64 == i[None, :] // 64
    put("tri_f", (same & (i[:, None] <= i[None, :])).astype(np.float32))
    put("tri_b", (same & (i[:, None] >= i[None, :])).astype(np.float32))
    put("iota", np.broadcast_to(i.astype(np.float32), (P, P)))
    put("slots", np.broadcast_to((BLK * E1_GROUPS * (i // BLK) + i % BLK).astype(np.float32), (P, P)))
    put("tri_neg", np.where(i[None, :] <= i[:, None], 0.0, -NEG).astype(np.float32))
    t = np.arange(T)

    def axial(rot_dim):
        row, col = (t // 64).astype(np.float32), (t % 64).astype(np.float32)
        axis = rot_dim // 2
        inv = (np.float32(10000.0) ** (-np.arange(0, axis, 2, dtype=np.float32) / np.float32(axis))).astype(np.float32)
        ang = np.concatenate([row[:, None] * inv, col[:, None] * inv], axis=-1)
        return np.cos(ang).astype(np.float32).T, np.sin(ang).astype(np.float32).T

    cos, sin = axial(32)
    cm, sm = np.ones((96, T), np.float32), np.zeros((96, T), np.float32)
    cm[64:96], sm[64:96] = np.tile(cos, (2, 1)), np.tile(sin, (2, 1))
    put("cos_m", cm)
    put("sin_m", sm)
    cos, sin = axial(64)
    put("cos_g", np.tile(cos, (4, 1)))
    put("sin_g", np.tile(sin, (4, 1)))
    put("fold", (i[:, None] % 32 == np.arange(2 * NCMP)[None, :]).astype(np.float32))
    end = np.arange(NCMP) * 16 + 31
    put("cmp_ok", np.concatenate([(end[None, :] <= (i + P * tt)[:, None]) for tt in range(TT)], 1).astype(np.float32))
    inv = (np.float32(500000.0) ** (-np.arange(0, ROT_DIM, 2, dtype=np.float32) / np.float32(ROT_DIM))).astype(np.float32)
    put("inv_freq", np.where(i % 64 < ROT_DIM, inv[i % 8], 0.0).astype(np.float32)[:, None])
    return c


def program(nc, A, out):
    ctx = ExitStack()
    with ctx:
        sems = {}

        def S(name):
            if name not in sems:
                sems[name] = ctx.enter_context(nc.semaphore(name))
            return sems[name]

        def sb(name, shape, dt=F32):
            return ctx.enter_context(nc.sbuf_tensor(name, shape, dt))

        ps = ctx.enter_context(nc.psum_tensor("ps", [P, 8, 512], F32))

        ring = sb("ring", [P, RING, SLOT])
        cst = sb("cst", [P, N_CONST])
        xT = sb("xT", [P, C, T])
        hT = sb("hT", [P, C, T])
        qT = sb("qT", [P, C, T])
        kT = sb("kT", [P, C, T])
        vt = sb("vt", [P, 2048])
        oT = sb("oT", [P, C, T])
        yT = sb("yT", [P, C, T])
        sqb = sb("sqb", [P, 1024])
        pb = sb("pb", [P, 2, 512])
        ptb = sb("ptb", [P, 2, 512])
        cosd = sb("cosd", [P, 2, T])
        identb = sb("identb", [P, P], BF16)
        trib = sb("trib", [P, P], BF16)
        colsA = sb("colsA", [P, 3, P])
        rows1 = sb("rows1", [1, 1100])
        wrb = sb("wr", [P, 2 * C * 52])
        gw = sb("gw", [16, 2, T])
        cpad = sb("cpad", [P, C, 32])
        mod = sb("mod", [P, 2, 48])
        modA = sb("modA", [P, 5, C])
        st = sb("st", [P, T])
        pn = sb("pn", [P, 512])
        rtmp = sb("rtmp", [P, 512])
        mx = sb("mx", [P, 2, 8])
        coef = sb("coef", [P, 8])
        gates = sb("gates", [P, TT, 48])
        rt = sb("rt", [P, 1100])
        ids = sb("ids", [1, 2, E1_BLOCKS], I32)
        Lw = sb("Lw", [P, 4, TT])
        affL = sb("affL", [P, 2, TT, E2 + 4])
        Dg = sb("Dg", [P, TT, P])
        DAg = sb("DAg", [P, TT, P])
        Cg = sb("Cg", [P, T])
        iog = sb("iog", [P, P])
        i8 = sb("i8", [P, 2, TT, 8], U32)
        misc = sb("misc", [P, 64])
        eps_col = misc[:, 63:64]

        def K(name, parts=P):
            at, n = CONST[name]
            return cst[0:parts, at:at + n]

        ident = K("ident")
        iota = K("iota")

        h_tok = oT[:, :, :].rearrange("p c t -> p (c t)").rearrange("p (a d) -> p a d", a=TT)
        hid = kT[:, 0:4, :].rearrange("p c t -> p (c t)")
        hidT = kT[:, 4:8, :].rearrange("p c t -> p (c t)").rearrange("p (c s) -> p c s", s=P)
        Yg = qT[:, 0:4, :].rearrange("p c t -> p (c t)")
        xg = ptb[:, :, :].rearrange("p b n -> p (b n)").rearrange("p (k s) -> p k s", k=C)
        sg = pb[:, :, :].rearrange("p b n -> p (b n)")
        sq = kT[:, :, :].rearrange("p c t -> p (c t)")
        rowsA = qT[:, 0:2, :].rearrange("p c t -> p (c t)")[:, 0:3 * P].rearrange("p (a n) -> p a n", a=3)
        posi = yT[:, 2, :].bitcast(I32)
        wr = [wrb[:, C * 36 * m:C * 36 * m + C * 36].rearrange("p (k n) -> p k n", k=C) for m in range(2)]
        wr += [wrb[:, C * (72 + 16 * m):C * (88 + 16 * m)].rearrange("p (k n) -> p k n", k=C) for m in range(2)]
        vtok = vt[:, :].rearrange("p (a n) -> p a n", a=TT)

        ada_rows01 = ptb[:, 0, :]
        ada_rows = [yT[:, p, :] for p in range(8)] + [hT[:, p, :] for p in range(2)]

        def psf(b, n=1, rows=slice(0, P)):
            return ps[rows, b:b + n, :].rearrange("p b n -> p (b n)")

        R1, at = {}, 0
        for name, n in (("c", 8), ("final_g", 8), ("ln1_g_2", 16), ("ln1_b_2", 16), ("ln2_g_2", 16),
                        ("ln2_b_2", 16), ("ple_gate_b_2", 16), ("mla_q_norm_2", 2), ("mla_kv_norm_2", 1),
                        ("gla_norm_2", 1), ("diff_subln_g", 1), ("nsa_cmp_b1", 4), ("gqa_q_norm_2", 1),
                        ("gqa_k_norm_2", 1)):
            R1[name] = (at, n)
            at += n

        def col(name, k=0, parts=slice(0, P)):
            return colsA[parts, 1, R1[name][0] + k:R1[name][0] + k + 1]

        LAM0, GB0, RB0 = 0, 256, 768

        def slot_view(n, k, cols):
            return ring[:, n % RING, 0:k * cols].rearrange("p (k n) -> p k n", k=k)

        jobs = []
        n_slot = [4 * ADA_FIRST]

        ada_slots = [4 * p for p in range(ADA_FIRST)]

        def ada_reserve():
            ada_slots.append(n_slot[0])
            n_slot[0] += 4

        def ada_slot(p, j):
            return ada_slots[p] + j

        def ada_bank(x):
            return 4 + x % 2 if x < len(ADA_JOB) else x % 2

        def job(W, k, cols, mm, evac, new=True, last=True, need=None, eng="act"):
            if len(jobs) in ADA_JOB:
                ada_reserve()
            if new:
                n_slot[0] += 1
            jobs.append(dict(W=W, k=k, cols=cols, mm=mm, evac=evac, new=new, last=last,
                             slot=n_slot[0] - 1, need=need, eng=eng, n=len(jobs)))
            return len(jobs) - 1

        def mm_T(src, k, pieces):
            def f(w, bank):
                return [[(ps[r0:r0 + m, bank, o0:o0 + T], w[:, kk, c0:c0 + m], src[:, kk, :]) for kk in range(k)]
                        for c0, m, r0, o0 in pieces]
            return f

        def mm_V(src, k, cols, c0=0, n=None):
            n = n or cols
            def f(w, bank):
                return [[(ps[:, bank, tt * n:(tt + 1) * n], src[:, kk, tt * P:(tt + 1) * P], w[:, kk, c0:c0 + n])
                         for kk in range(k)] for tt in range(TT)]
            return f

        def copy_to(*pairs, func=ACT.Copy):
            def f(bank):
                for src, dst in pairs:
                    last = nc.scalar.activation(dst, src(bank), func)
                return last
            return f

        def whole(bank):
            return ps[:, bank, :]

        def pair_dst(buf, s):
            return buf[:, 2 * s:2 * s + 2, :].rearrange("p c t -> p (c t)")

        def dense(W, src, dst, n, need):
            return [job(W[:, 256 * s:256 * s + 256], 8, 256,
                        mm_T(src, 8, [(0, P, 0, 0), (P, P, 0, T)]),
                        copy_to((whole, pair_dst(dst, s))), need=need) for s in range(n)]

        ropes = []

        ph = {}
        ph["diff"] = len(jobs)
        dj = dense(A["diff_w_in"][0], hT, qT, 4, ("h_ready", 1))
        dj += dense(A["diff_w_in"][0, :, D:2 * D], hT, kT, 4, None)
        for s in range(4):
            job(A["diff_w_in"][0, :, 2 * D + 256 * s:2 * D + 256 * s + 256], 8, 256, mm_V(hT, 8, 256),
                copy_to((lambda b: ps[:, b, :].rearrange("p (a n) -> p a n", a=TT),
                         vtok[:, :, 256 * s:256 * s + 256])))

        def out_jobs(W, need):
            return [job(W[:, 256 * s:256 * s + 256], 8, 256, mm_T(oT, 8, [(0, P, 0, 0), (P, P, 0, T)]),
                        s, need=need, eng="dve") for s in range(4)]

        for _ in ADA_STEP:
            ada_reserve()
        ph["diff_out"] = len(jobs)
        out_jobs(A["diff_w_out"][0], "attention")
        slot_moe = {0: n_slot[0]}
        n_slot[0] += 12 * E1_GROUPS

        ph["nsa"] = len(jobs)
        nw = A["nsa_w_in"][0]
        dense(nw, hT, qT, 4, ("h_ready", 3))
        kdup = {"s": kT[:, 0:2, :], "w": kT[:, 2:4, :]}
        vTb = {"s": kT[:, 4, :], "w": kT[:, 5, :]}
        kcp = {0: sqb[:, 0:256].rearrange("p (g u) -> p g u", g=2), 1: sqb[:, 256:512].rearrange("p (g u) -> p g u", g=2)}

        def twice(dst):
            return [(lambda b, g=g: ps[64 * g:64 * g + 64, b, 0:T], dst[64 * half:64 * half + 64, g, :])
                    for g in range(2) for half in range(2)]
        nsa_src = {}
        for which, off in (("s", 256), ("w", 512)):
            nsa_src["k" + which] = job(nw[:, NSA_Q + off:NSA_Q + off + 128], 8, 128,
                                       mm_T(hT, 8, [(0, P, 0, 0)]), copy_to(*twice(kdup[which])))
            nsa_src["v" + which] = job(nw[:, NSA_Q + off + 128:NSA_Q + off + 256], 8, 128,
                                       mm_T(hT, 8, [(0, P, 0, 0)]),
                                       copy_to((lambda b: ps[:, b, 0:T], vTb[which])))
        for t in range(2):
            pairs = [(lambda b, g=g, e=e: ps[64 * g:64 * g + 64, b, 0:T].rearrange("p (u e) -> p u e", e=2)[:, :, e],
                      kcp[t][64 * e:64 * e + 64, g, :]) for g in range(2) for e in range(2)]
            nsa_src["c" + str(t)] = job(nw[:, NSA_Q + 128 * t:NSA_Q + 128 * t + 128], 8, 128,
                                        mm_T(hT, 8, [(0, P, 0, 0)]), copy_to(*pairs))
        nsa_src["gate"] = job(nw[:, NSA_Q + 768:NSA_Q + 816], 8, 48, mm_V(hT, 8, 48),
                              copy_to((lambda b: ps[:, b, 0:96].rearrange("p (a n) -> p a n", a=TT), gates[:, :, :]),
                                      func=ACT.Sigmoid))
        yfl = yT[:, :, :].rearrange("p c t -> p (c t)")
        blk = yfl[:, 0:1024].rearrange("p (t j n) -> p t j n", t=2, j=16)
        hpart = yfl[:, 1024:2048].rearrange("p (t a n) -> p t a n", t=2, a=2)
        gh = sqb[:, 512:632].rearrange("p (t m n) -> p t m n", t=2, m=2)
        kcmp = sqb[:, 640:640 + 4 * NCMP].rearrange("p (g e n) -> p g e n", g=2, e=2)
        vcmp = sqb[0:NCMP, 704:832]
        for t in range(2):
            for half in range(2):
                def f(w, bank, t=t, half=half):
                    return [[(ps[32 * (j % 4):32 * (j % 4) + 32, bank, 0:256], blk[:, t, 8 * half + j, :], w[:, j, :],
                              j < 4, j >= 4) for j in range(8)]]
                job(A["nsa_cmp_w1"][0, t, 1024 * half:1024 * half + 1024, :], 8, 256, f,
                    copy_to((lambda b: ps[:, b, 0:256], hpart[:, t, half, :])), need=("blk_ready", 1))

        def f(w, bank):
            gk = [[(ps[64 * half:64 * half + 64, bank, 0:30], w[:, m, 0:64], gh[:, 0, m, :]) for m in range(2)]
                  for half in range(2)]
            return gk
        job(A["nsa_cmp_w2"][0, 0], 2, 64, f,
            copy_to((lambda b: ps[0:64, b, 0:2 * NCMP].rearrange("p (g n) -> p g n", g=2), kcmp[0:64, :, 0, :]),
                    (lambda b: ps[64:P, b, 0:2 * NCMP].rearrange("p (g n) -> p g n", g=2), kcmp[64:P, :, 1, :])),
            need=("gelu", 1))

        def f(w, bank):
            return [[(ps[0:NCMP, bank, 64 * g:64 * g + 64], gh[:, 1, m, NCMP * g:NCMP * g + NCMP], w[:, m, 0:64])
                     for m in range(2)] for g in range(2)]
        nsa_src["cmp"] = job(A["nsa_cmp_w2"][0, 1], 2, 64, f, copy_to((lambda b: ps[0:NCMP, b, 0:128], vcmp)))
        nsa_w2 = len(jobs) - 2
        ph["nsa_out"] = len(jobs)
        out_jobs(A["nsa_w_out"][0], "attention")
        slot_moe[1] = n_slot[0]
        n_slot[0] += 12 * E1_GROUPS

        ph["even"] = len(jobs)
        ew = A["w_in_even_2"][0]
        scr = yT[:, :, :].rearrange("p c t -> p (c t)")
        cqT = scr[:, 0:512].rearrange("p (c t) -> p c t", c=2)
        ckvT = scr[:, 512:768].rearrange("p (c t) -> p c t", c=1)
        kpe = scr[:, 768:1024]
        gqT = scr[:, 1024:1536].rearrange("p (c t) -> p c t", c=2)
        gkT = scr[:, 1536:2048].rearrange("p (c t) -> p c t", c=2)
        hfl = hT[:, :, :].rearrange("p c t -> p (c t)")
        gv = hfl[:, 0:1024].rearrange("p (a n) -> p a n", a=TT)
        grT = hfl[:, 1024:2048].rearrange("p (c t) -> p c t", c=4)
        lrT = rt[0:16, 0:512].rearrange("p (a t) -> p a t", a=2)
        vm = vt[:, 0:1024].rearrange("p (a h n) -> p a h n", a=TT, h=8)
        job(ew[:, 0:256], 8, 256, mm_T(xT, 8, [(0, P, 0, 0), (P, P, 0, T)]),
            copy_to((whole, scr[:, 0:512])), need=("h_ready", 5))
        job(ew[:, 256:384], 8, 128, mm_T(xT, 8, [(0, P, 0, 0)]),
            copy_to((lambda b: ps[:, b, 0:T], ckvT[:, 0, :])))
        job(ew[:, 384:416], 8, 32, mm_T(xT, 8, [(0, 32, 64, 0)]),
            copy_to((lambda b: ps[64:96, b, 0:T], kpe[64:96, :])))
        ev_kpe = len(jobs) - 1
        job(ew[:, 416:672], 8, 256, mm_T(xT, 8, [(0, P, 0, 0), (P, P, 0, T)]), copy_to((whole, scr[:, 1024:1536])))
        job(ew[:, 672:928], 8, 256, mm_T(xT, 8, [(0, P, 0, 0), (P, P, 0, T)]), copy_to((whole, scr[:, 1536:2048])))
        for s in range(2):
            job(ew[:, 928 + 256 * s:1184 + 256 * s], 8, 256, mm_V(xT, 8, 256),
                copy_to((lambda b: ps[:, b, :].rearrange("p (a n) -> p a n", a=TT), gv[:, :, 256 * s:256 * s + 256])))
        job(ew[:, 1440:1472], 8, 32, mm_T(xT, 8, [(0, 16, 0, 0), (16, 16, 0, T)]),
            copy_to((lambda b: ps[0:16, b, :], rt[0:16, 0:512])))
        ev_lr = len(jobs) - 1
        for s in range(2):
            job(ew[:, 1472 + 256 * s:1728 + 256 * s], 8, 256, mm_T(xT, 8, [(0, P, 0, 0), (P, P, 0, T)]),
                copy_to((whole, hfl[:, 1024 + 512 * s:1536 + 512 * s]), func=ACT.Silu))
        ev_uq = len(jobs)
        for s in range(4):
            job(A["w_uq_2"][0], 2, 768, mm_T(cqT, 2, [(96 * (2 * s + a), 96, 0, T * a) for a in range(2)]),
                copy_to((lambda b: ps[0:96, b, :], qT[0:96, 2 * s:2 * s + 2, :].rearrange("p c t -> p (c t)"))),
                new=(s == 0), last=(s == 3), need=("pn_done", 6) if s == 0 else None)
        ev_kv = len(jobs)
        for s in range(4):
            job(A["w_ukv_2"][0], 1, 1024, mm_T(ckvT, 1, [(P * (2 * s + a), 64, 0, T * a) for a in range(2)]),
                copy_to((lambda b: ps[0:64, b, :], kT[0:64, 2 * s:2 * s + 2, :].rearrange("p c t -> p (c t)"))),
                new=(s == 0), last=False)
        for tt in range(TT):
            def f(w, bank, tt=tt):
                return [[(ps[:, bank, :], ckvT[:, 0, tt * P:tt * P + P],
                          w[:, 0, :].rearrange("p (h n) -> p h n", h=8)[:, :, 64:128])]]
            job(A["w_ukv_2"][0], 1, 1024, f,
                copy_to((whole, vt[:, 512 * tt:512 * tt + 512])), new=False, last=(tt == 1))
        ph["even_out"] = len(jobs)
        out_jobs(A["w_o_2"][0], "attention")

        def ple_value_jobs(layer):
            for s in range(4):
                job(A["ple_w_2"][layer], 2, 1024, mm_T(pTb[layer], 2, [(256 * s, P, 0, 0), (256 * s + P, P, 0, T)]),
                    copy_to((whole, pair_dst(hT, s))), new=(s == 0), last=(s == 3))

        def ple_gate_jobs(layer, pairs):
            for s in pairs:
                def ev(bank, s=s):
                    for a in range(2):
                        last = nc.scalar.activation(kT[:, 2 * s + a, :], ps[:, bank, T * a:T * a + T], ACT.Sigmoid,
                                                    bias=col("ple_gate_b_2", 8 * layer + 2 * s + a))
                    return last
                job(A["ple_gate_w_2"][layer][:, 256 * s:256 * s + 256], 8, 256,
                    mm_T(xT, 8, [(0, P, 0, 0), (P, P, 0, T)]), ev)

        E2_PARTS = [range(0, 1), range(1, 2), range(2, E2_GROUPS)]
        GATE_PARTS = [range(0, 2), range(2, 4)]
        slot_part = {}

        def moe2_slots(layer):
            ph[f"value{layer}"] = len(jobs)
            ple_value_jobs(layer)
            ph[f"gate{layer}"] = len(jobs)
            for part, groups in enumerate(E2_PARTS):
                slot_part[2 + layer, part] = n_slot[0]
                n_slot[0] += 48 * len(groups)
                if part < len(GATE_PARTS):
                    ple_gate_jobs(layer, GATE_PARTS[part])

        def gate_jobs(layer, part):
            return [ph[f"gate{layer}"] + a for a in GATE_PARTS[part]]

        pTall = sb("pT", [P, 2, 2, T])
        pTb = [pTall[:, 0], pTall[:, 1]]
        moe2_slots(0)

        ph["odd"] = len(jobs)
        ow = A["w_in_odd_2"][0]
        dense(ow, xT, qT, 4, ("h_ready", 7))
        for s in range(2):
            job(ow[:, D + 128 * s:D + 128 * s + 128], 8, 128, mm_T(xT, 8, [(0, P, 0, 0)]),
                copy_to(*twice(kT[:, 2 * s:2 * s + 2, :])))
        job(ow[:, D + 256:D + 512], 8, 256, mm_V(xT, 8, 256), copy_to((whole, vt[:, 0:512])))
        vo = vt[:, 0:512].rearrange("p (a n) -> p a n", a=TT)
        ph["odd_out"] = len(jobs)
        out_jobs(A["w_o_2"][1], "attention")
        moe2_slots(1)
        ph["end"] = len(jobs)
        phases = ["diff", "diff_out", "nsa", "nsa_out", "even", "even_out", "value0", "gate0", "odd", "odd_out",
                  "value1", "gate1", "end"]
        span = {a: range(ph[a], ph[b]) for a, b in zip(phases, phases[1:])}
        acts_before, res_no, part_no = {}, {}, {}
        for j, jb in enumerate(jobs):
            acts_before[j] = sum(x["eng"] == "act" for x in jobs[:j])
            res_no[j] = j - acts_before[j]
            part_no[j] = sum(not x["last"] for x in jobs[:j])
        acts_before[len(jobs)] = sum(x["eng"] == "act" for x in jobs)

        def finished(j):
            return ("slot_used", jobs[j]["slot"] + 1) if jobs[j]["last"] else ("job_part", part_no[j] + 1)

        def evacuated(j):
            return ("proj_evac", acts_before[j] + 1) if jobs[j]["eng"] == "act" else ("res_evac", res_no[j] + 1)

        def await_need(eng, need):
            name, value = evacuated(need[1]) if need[0] == "job" else need
            eng.wait_ge(S(name), value)

        cd, sd = cosd[:, 0, :], cosd[:, 1, :]
        for s in range(8):
            buf = qT if s < 4 else kT
            ropes.append((pair_dst(buf, s % 4), 2, 0, P, K("rot16"), cd, sd, ("job", span["diff"][s])))
        r_nsa = len(ropes)
        for s in range(4):
            ropes.append((pair_dst(qT, s), 2, 0, P, K("rot16"), cd, sd, ("job", span["nsa"][s])))
        for i, w in enumerate("sw"):
            ropes.append((pair_dst(kT, i), 2, 0, P, K("rot16"), cd, sd, ("job", nsa_src["k" + w])))
            ropes.append((kT[:, 4 + i, :], 1, 0, P, K("rot16"), cd, sd, ("job", nsa_src["v" + w])))
        r_even = len(ropes)
        ropes.append((kpe, 1, 64, 32, K("rot_mla"), K("cos_m"), K("sin_m"), ("job", ev_kpe)))
        for s in range(4):
            ropes.append((pair_dst(qT, s), 2, 0, 96, K("rot_mla"), K("cos_m"), K("sin_m"), ("job", ev_uq + s)))
        r_odd = len(ropes)
        for s in range(6):
            ropes.append((pair_dst(qT if s < 4 else kT, s % 4), 2, 0, P, K("rot64"), K("cos_g"), K("sin_g"),
                          ("pn_done", 8 + s + 1)))
        r_end = len(ropes)

        pns = []
        for s in range(4):
            o = pair_dst(oT, s)
            pns.append(([o], K("ones")[:, 0:1], 128, [(o, coef[:, 2:3], o, None)], ("o_evac", 2 * s + 2)))
        pns.append(([cqT[:, 0, :], cqT[:, 1, :]], K("ones")[:, 0:1], 256,
                    [(cqT[:, a, :], col("mla_q_norm_2", a), cqT[:, a, :], None) for a in range(2)],
                    ("job", ph["even"])))
        pns.append(([ckvT[:, 0, :]], K("ones")[:, 0:1], 128, [(ckvT[:, 0, :], col("mla_kv_norm_2"), ckvT[:, 0, :], None)],
                    ("job", ph["even"] + 1)))
        for s in range(2):
            o = oT[:, 4 + 2 * s:6 + 2 * s, :].rearrange("p c t -> p (c t)")
            gr_s = grT[:, 2 * s:2 * s + 2, :].rearrange("p c t -> p (c t)")
            pns.append(([o], K("ones")[:, 0:1], 128, [(o, col("gla_norm_2"), o, gr_s)], ("gla_evac", 2)))
        for s in range(6):
            o = pair_dst(qT if s < 4 else kT, s % 4)
            pns.append(([o], K("ones64")[:, 0:P:64], 64, [(o, col("gqa_q_norm_2" if s < 4 else "gqa_k_norm_2"), o, None)],
                        ("job", ph["odd"] + s)))

        pn_batch = [range(0, 4), range(4, 6), range(6, 8), range(8, 14)]

        def pn_columns(i, c, tt):
            batch = next(b for b in pn_batch if i in b)
            at = 0
            for x in range(batch[0], i):
                at += pns[x][0][0].shape[-1] // T * TT * pns[x][1].shape[-1]
            w = pns[i][1].shape[-1]
            return slice(at + (TT * c + tt) * w, at + (TT * c + tt + 1) * w)

        def pn_width(batch):
            last = batch[-1]
            return pn_columns(last, pns[last][0][0].shape[-1] // T - 1, TT - 1).stop

        units, obanks = [], []

        def unit(q, k, v, rows, obank, start, stop, causal=False, scale=64 ** -0.5, coef=None, cmp=None):
            units.append(dict(q=q, k=k, v=v, rows=rows, o=obank, start=start, stop=stop, causal=causal,
                              scale=scale, coef=coef, cmp=cmp, last=False))

        u_ph = {}
        u_ph["diff"] = 0
        for h in range(8):
            for c in range(2):
                r = slice(64 * c, 64 * c + 64)
                unit(qT[r, h, :], kT[r, h, :], [vtok[:, tt, P * h:P * h + P] for tt in range(TT)],
                     slice(0, P), len(obanks), c == 0, c == 1, causal=True, coef=coef[:, 0:2] if c else None)
            units[-1]["last"] = True
            obanks.append(oT[:, h, :])
        u_ph["nsa"] = len(units)
        vsw = {w: vt[:, 256 * i:256 * i + 256].rearrange("p (a n) -> p a n", a=TT) for i, w in enumerate("sw")}
        PC = vt[:, 512:992].rearrange("p (a h n) -> p a h n", a=TT, h=16)
        for h in range(16):
            g, r = h // 8, slice(64 * (h % 2), 64 * (h % 2) + 64)
            for i, w in enumerate("sw"):
                unit(qT[r, h // 2, :], kdup[w][r, g, :], [vsw[w][:, tt, 64 * g:64 * g + 64] for tt in range(TT)],
                     r, len(obanks), i == 0, False, causal=True, coef=gates[:, :, 3 * h + 1 + i])
            unit(None, None, vcmp[:, 64 * g:64 * g + 64], r, len(obanks), False, True, cmp=h)
            if h % 2:
                units[-1]["last"] = True
                obanks.append(oT[:, h // 2, :])
        u_ph["mla"] = len(units)
        for h in range(8):
            r = slice(64 * (h % 2), 64 * (h % 2) + 64)
            unit(qT[0:96, h, :], kT[0:96, h, :], [vm[:, tt, h, :] for tt in range(TT)], r, len(obanks), True, True,
                 scale=96 ** -0.5)
            if h % 2:
                units[-1]["last"] = True
                obanks.append(oT[:, h // 2, :])
        u_ph["gqa"] = len(units)
        for h in range(16):
            kv, r = h // 4, slice(64 * (h % 2), 64 * (h % 2) + 64)
            unit(qT[r, h // 2, :], kT[r, kv, :], [vo[:, tt, 64 * kv:64 * kv + 64] for tt in range(TT)],
                 r, len(obanks), True, True)
            if h % 2:
                units[-1]["last"] = True
                obanks.append(oT[:, h // 2, :])
        u_ph["end"] = len(units)
        soft = [u for u, un in enumerate(units) if un["cmp"] is None]
        s_no = [sum(x <= u for x in soft) for u in range(len(units))]
        u_span = {a: range(u_ph[a], u_ph[b]) for a, b in
                  zip(["diff", "nsa", "mla", "gqa"], ["nsa", "mla", "gqa", "end"])}
        o_after = {"diff": 8, "nsa": 16, "mla": 20, "gqa": 28}

        def flat(t):
            return t[:, :, :].rearrange("p c t -> p (c t)")
        at = [flat(qT)[:, 1024 * d:1024 * d + 1024].rearrange("p (a n) -> p a n", a=8) for d in range(2)]
        stt_ = [flat(kT)[:, 1024 * d:1024 * d + 1024].rearrange("p (c n v) -> p c n v", c=2, n=4) for d in range(2)]
        gE = [[vt[:, 0:512], vt[:, 512:1024], vt[:, 1024:1536]], [rt[:, 0:512], rt[:, 512:1024], scr[:, 0:512]]]
        kd = [v.rearrange("p (c t) -> p c t", c=2) for v in (vt[:, 1536:2048], scr[:, 512:1024])]
        lnb = [pn[:, :], sg[:, 512:1024]]
        la = [oT[:, 4 + 2 * d:6 + 2 * d, :].rearrange("p c t -> p (c t)").rearrange("p (a n) -> p a n", a=TT) for d in range(2)]
        qg = [sqb[:, 512 * d:512 * d + 512].rearrange("p (c t) -> p c t", c=2) for d in range(2)]
        kg = [ptb[:, :, :].rearrange("p b n -> p (b n)")[:, 512 * d:512 * d + 512].rearrange("p (c t) -> p c t", c=2) for d in range(2)]
        kdt = [sg[:, 512 * d:512 * d + 512].rearrange("p (a n) -> p a n", a=TT) for d in range(2)]
        gdec = [misc[:, 16 + 16 * d:32 + 16 * d].rearrange("p (a n) -> p a n", a=2) for d in range(2)]

        def rtv(first, n, parts=P, **kw):
            v = rt[0:parts, first:first + n]
            return v.rearrange("p (a n) -> p a n", **kw) if kw else v
        rt_lg = rtv(0, 72, a=TT)
        rt_g8, rt_m8, rt_oh4 = rtv(72, 16, a=TT), rtv(88, 16, a=TT), rtv(104, 8, a=TT)
        rt_le, rt_L = rtv(112, 64, a=TT), rtv(304, 64, a=TT)
        rt_oh = rt[:, 176:304].rearrange("p (b a n) -> p b a n", b=2, a=TT)
        rt_c, rt_e, rt_t8 = rtv(432, 20), rtv(452, 8), rtv(460, 8, 32)
        rt_nblk, rt_nblkB, rt_base, rt_cmp = rtv(468, 1, 32), rtv(470, P, 32), rtv(600, 35), rtv(640, E1_BLOCKS, 32)
        rt_selT, rt_m8e = rtv(700, T, E2), rtv(960, 8, E2)

        rt_new, rt_count = rtv(740, E1_BLOCKS, 1), rtv(800, E1_BLOCKS, 1)

        def rt_sel(n):
            return rtv(368, TT * n, a=TT)

        moe_g0 = [0, E1_GROUPS, 2 * E1_GROUPS, 2 * E1_GROUPS + E2_GROUPS]

        gather_g0 = [g + m for m, g in enumerate(moe_g0)]

        block = ctx.enter_context(nc.Block())

        @block.sync
        def _(sp):
            n_par = {"params": 0, "late_params": 0}

            def param(dst, src, signal="params"):
                sp.dma_start(dst, src).then_inc(S(signal), 16)
                n_par[signal] += 1

            sp.dma_start(cst[:, :], A["consts"]).then_inc(S("consts"), 16)
            sp.wait_ge(S("rows_zero"), 1)
            for tt in range(TT):
                sp.dma_start(sq[:, 1024 * tt:1024 * tt + 1024], A["x"][0, P * tt:P * tt + P, :]).then_inc(S("x_in"), 16)
            param(rowsA[0:96, 0, :], A["ada_b"].rearrange("l (r c) -> (l r) c", c=P))
            param(rowsA[96:128, 0, :], A["norm_g"].rearrange("l a (r c) -> (l a r) c", c=P))
            for name in ("c", "ln1_g_2", "ln1_b_2", "ln2_g_2", "ln2_b_2", "ple_gate_b_2", "mla_q_norm_2",
                         "mla_kv_norm_2", "gla_norm_2", "diff_subln_g"):
                a, n = R1[name]
                param(rowsA[a:a + n, 1, :], A[name].rearrange("l (r c) -> (l r) c", c=P))
            a, n = R1["final_g"]
            param(rowsA[a:a + n, 1, :], A["final_g"].rearrange("(r c) -> r c", c=P))
            a, n = R1["nsa_cmp_b1"]
            param(rowsA[a:a + n, 1, :], A["nsa_cmp_b1"].rearrange("l a (r c) -> (l a r) c", c=P))
            for name in ("gqa_q_norm_2", "gqa_k_norm_2"):
                a, _ = R1[name]
                for half in range(2):
                    param(rowsA[a:a + 1, 1, 64 * half:64 * half + 64], A[name])
            param(rowsA[0:32, 2, :], A["nsa_cmp_pos"].rearrange("l a (j e) d -> (l a j) (e d)", e=2))
            param(rows1[0:1, LAM0:LAM0 + 256], A["diff_lambda"].rearrange("l a d -> l (a d)"))
            param(posi, A["positions"].to_broadcast([P, T]))
            def load(n, dst, src, wait=True):
                if n >= RING:
                    sp.wait_ge(S("slot_used"), n - RING + 1)
                sp.dma_start(dst, src).then_inc(S(f"slot{n % RING}"), 16)

            def load_ada(parts):
                for p in parts:
                    for j in range(4):
                        n, s = ada_slot(p, j), 4 * (p % 6) + j
                        load(n, slot_view(n, 8, 256),
                             A["ada_w"][p // 6][:, 256 * s:256 * s + 256].rearrange("(k p) n -> p k n", p=P))

            load_ada(range(ADA_FIRST))
            param(rows1[0:1, GB0:GB0 + 256], A["gla_gate_b_fwd_2"], "late_params")
            param(rows1[0:1, GB0 + 256:GB0 + 512], A["gla_gate_b_bwd_2"], "late_params")
            for l in range(2):
                param(rows1[0:1, RB0 + 36 * l:RB0 + 36 * l + 4], A["moe_b_group"][l:l + 1, :], "late_params")
                param(rows1[0:1, RB0 + 36 * l + 4:RB0 + 36 * l + 36],
                      A["moe_b_expert"][l:l + 1].rearrange("l g e -> l (g e)"), "late_params")
                param(wr[l][:, :, 0:4], A["moe_w_group"][l].rearrange("(k p) n -> p k n", p=P), "late_params")
                for g in range(4):
                    param(wr[l][:, :, 4 + 8 * g:12 + 8 * g], A["moe_w_expert"][l, g].rearrange("(k p) n -> p k n", p=P), "late_params")
                param(wr[2 + l][:, :, :], A["router_w_2"][l].rearrange("(k p) n -> p k n", p=P), "late_params")
            param(gw[:, 0, :], A["gla_gate_w_fwd_2"][0], "late_params")
            param(gw[:, 1, :], A["gla_gate_w_bwd_2"][0], "late_params")
            for l in range(2):
                sp.dma_start(yT[:, 4 * l:4 * l + 2, :], A["p_2"][l, 0].rearrange("(a p) n -> p a n", p=P))\
                    .then_inc(S("p_in"), 16)
            assert n_par == {"params": N_PARAMS, "late_params": N_LATE}, n_par

            def load_jobs(name):
                for j in span[name] if isinstance(name, str) else name:
                    jb = jobs[j]
                    if j in ADA_JOB:
                        load_ada([ADA_FIRST + ADA_JOB.index(j)])
                    if jb["new"]:
                        load(jb["slot"], slot_view(jb["slot"], jb["k"], jb["cols"]),
                             jb["W"].rearrange("(k p) n -> p k n", p=P))

            def load_experts1(m):
                n0 = slot_moe[m]
                gate = A["moe_w_gate"].rearrange("l e (p k) n -> l e p (k n)", p=P)
                up = A["moe_w_up"].rearrange("l e (p k) n -> l e p (k n)", p=P)
                down = A["moe_w_down"].rearrange("l e (p k) n -> l e p (k n)", p=P)
                sp.wait_ge(S("ids_ready"), m + 1)
                with sp.Fori(0, E1_GROUPS) as i:
                    e = [sp.value_load(ids[0:1, 0, bass.ds(i + E1_GROUPS * j, 1)], min_val=0, max_val=E1 - 1) for j in range(4)]
                    on = [sp.value_load(ids[0:1, 1, bass.ds(i + E1_GROUPS * j, 1)], min_val=0, max_val=1) for j in range(4)]
                    order = [(w, j) for w in (gate, up, down) for j in range(4)]
                    for s, (w, j) in enumerate(order):
                        sp.wait_ge(S("slot_used"), 12 * i + (n0 + s - RING + 1))
                        sp.dma_start(ring[:, (n0 + s) % RING, :], w[m, e[j]], cond=on[j] > 0)\
                            .then_inc(S(f"slot{(n0 + s) % RING}"), 16)

            def load_experts2(l, part):
                n0, groups = slot_part[2 + l, part], E2_PARTS[part]
                w1 = A["w1_2"].rearrange("l e (p k) n -> l e p (k n)", p=P)
                w3 = A["w3_2"].rearrange("l e (p k) n -> l e p (k n)", p=P)
                w2 = A["w2_2"].rearrange("l e (p k) n -> l e p (k n)", p=P)
                with sp.Fori(0, len(groups)) as i:
                    order = [(w, j, kk) for kk in range(4) for w in (w1, w3) for j in range(4)]
                    order += [(w2, j, kk) for kk in range(4) for j in range(4)]
                    for s, (w, j, kk) in enumerate(order):
                        sp.wait_ge(S("slot_used"), 48 * i + (n0 + s - RING + 1))
                        sp.dma_start(ring[:, (n0 + s) % RING, :], w[l, 4 * i + (4 * groups[0] + j)][:, SLOT * kk:SLOT * kk + SLOT])\
                            .then_inc(S(f"slot{(n0 + s) % RING}"), 16)

            load_jobs("diff")
            load_ada(range(ADA_FIRST + len(ADA_JOB), 12))
            load_jobs("diff_out")
            load_experts1(0)
            load_jobs("nsa")
            load_jobs("nsa_out")
            load_experts1(1)
            load_jobs("even")
            load_jobs("even_out")
            load_jobs("value0")
            load_experts2(0, 0)
            load_jobs(gate_jobs(0, 0))
            load_experts2(0, 1)
            load_jobs(gate_jobs(0, 1))
            load_experts2(0, 2)
            load_jobs("odd")
            load_jobs("odd_out")
            load_jobs("value1")
            load_experts2(1, 0)
            load_jobs(gate_jobs(1, 0))
            load_experts2(1, 1)
            load_jobs(gate_jobs(1, 1))
            load_experts2(1, 2)
            for tt in range(TT):
                sp.wait_ge(S("out_ready"), tt + 1)
                sp.dma_start(out[0, P * tt:P * tt + P, :], h_tok[:, tt, :]).then_inc(S("stored"), 16)
            sp.wait_ge(S("stored"), 16 * TT)

        @block.tensor
        def _(pe):
            mmul = nc.tensor.matmul

            def slot_in(n):
                pe.wait_ge(S(f"slot{n % RING}"), 16 * (n // RING + 1))

            def tr(dst, src, k=P):
                return nc.tensor.transpose(dst, src, ident[0:k, 0:k])

            def project(js):
                for j in js:
                    jb = jobs[j]
                    if j in ADA_JOB:
                        ada_other(ADA_JOB.index(j))
                    chunked = jb["need"] and jb["need"][0] == "h_ready"
                    if isinstance(jb["need"], tuple) and not chunked:
                        pe.wait_ge(S(jb["need"][0]), jb["need"][1])
                    if jb["new"]:
                        slot_in(jb["slot"])
                    if j >= 2:
                        await_need(pe, ("job", j - 2))
                    for x, grp in enumerate(jb["mm"](slot_view(jb["slot"], jb["k"], jb["cols"]), j % 2)):
                        for i, (o, l, r, *flags) in enumerate(grp):
                            if chunked and x == 0:
                                pe.wait_ge(S("h_ready"), C * (jb["need"][1] - 1) + i + 1)
                            start, stop = flags or (i == 0, i == len(grp) - 1)
                            last = mmul(o, l, r, start=start, stop=stop)
                    last.then_inc(S(finished(j)[0]), 1)
                    after(j)

            rope_next = [0]

            def rope(i):
                buf, n, r0, rows, rot, _, _, need = ropes[i]
                await_need(pe, need)
                if i >= 2:
                    pe.wait_ge(S("rope_done"), i - 1)
                rr = slice(r0, r0 + rows)
                mmul(ps[rr, 2 + i % 2, 0:n * T], rot[rr, rr], buf[rr, :], start=True, stop=True)\
                    .then_inc(S("rope_mm"), 1)

            def after(j):
                while rope_next[0] < r_end and ropes[rope_next[0]][7][0] == "job" and \
                        ropes[rope_next[0]][7][1] < j and rope_next[0] < rope_limit[0]:
                    rope(rope_next[0])
                    rope_next[0] += 1

            rope_limit = [0]

            def ropes_until(end):
                while rope_next[0] < end:
                    rope(rope_next[0])
                    rope_next[0] += 1

            def pn_sums(b):
                for i in pn_batch[b]:
                    srcs, heads = pns[i][0], pns[i][1]
                    pe.wait_ge(S("pn_sq"), i + 1)
                    n = srcs[0].shape[-1]
                    for c in range(n // T):
                        for tt in range(TT):
                            for a in range(len(srcs)):
                                at = 512 * (i % 2) + n * a + T * c + P * tt
                                last = mmul(ps[:, 7, pn_columns(i, c, tt)], sqb[:, at:at + P], heads,
                                            start=(a == 0), stop=(a == len(srcs) - 1))
                    last.then_inc(S("pn_mm"), 1)

            def pn_spread(i):
                n, w = pns[i][0][0].shape[-1], pns[i][1].shape[-1]
                pe.wait_ge(S("pn_inv"), [i in b for b in pn_batch].index(True) + 1)
                if i >= 2:
                    pe.wait_ge(S("pn_done"), i - 1)
                for c in range(n // T):
                    for tt in range(TT):
                        for h in range(w):
                            at, m = pn_columns(i, c, tt).start + h, P // w
                            last = mmul(ps[m * h:m * h + m, 5 + i % 2, T * c + P * tt:T * c + P * tt + P],
                                        pn[:, at:at + 1].to_broadcast([P, m]), ident, start=True, stop=True)
                last.then_inc(S("pn_sp"), 1)

            def partition_norms(b):
                pn_sums(b)
                for i in pn_batch[b]:
                    pn_spread(i)

            def norm(n):
                if n >= 5:
                    pe.wait_ge(S("x_ready"), n + 1)
                    for c in range(C):
                        last = mmul(ps[:, 3, 0:T], K("ones"), xT[:, c, :], start=(c == 0), stop=(c == C - 1))
                    last.then_inc(S("mean_mm"), 1)
                for c in range(C):
                    if c % 2 == 0:
                        pe.wait_ge(S("sq_ready"), 4 * n + c // 2 + 1)
                    last = mmul(ps[:, 2, 0:T], K("ones"), sq[:, T * c:T * c + T], start=(c == 0), stop=(c == C - 1))
                last.then_inc(S("sq_mm"), 1)

            def ada_part(p, dst):
                for k in range(C):
                    for j in range(4):
                        n = ada_slot(p, j)
                        if k == 0:
                            slot_in(n)
                        last = mmul(dst[32 * j:32 * j + 32, :], cpad[:, k, :], slot_view(n, 8, 256)[:, k, :],
                                    start=(k == 0), stop=(k == C - 1))
                        if k == C - 1:
                            last.then_inc(S("slot_used"), 1)

            def ada_other(x):
                if x >= 2:
                    pe.wait_ge(S("ada_evac"), 1 + x - 1)
                ada_part(ADA_FIRST + x, ps[:, ada_bank(x), 0:T])

            def attention(name, ada=False):
                us = list(u_span[name])

                def scores(u):
                    un = units[u]
                    if un["cmp"] is not None:
                        return
                    b = 4 + s_no[u] % 2
                    if s_no[u] > 2:
                        pe.wait_ge(S("exp_done"), s_no[u] - 2)
                    q, k = un["q"], un["k"]
                    if un["causal"]:
                        mmul(ps[:, b, 0:P], q[:, 0:P], k[:, 0:P], start=True, stop=False, skip_group_check=True)
                        mmul(ps[:, b, 0:P], identb[:, :], trib[:, :], start=False, stop=True, skip_group_check=True)
                        mmul(ps[:, b, P:P + T], q[:, P:T], k, start=True, stop=False, skip_group_check=True)
                        last = mmul(ps[:, b, T:T + P], identb[:, :], trib[:, :], start=False, stop=True,
                                    skip_group_check=True)
                    else:
                        mmul(ps[:, b, 0:T], q[:, 0:P], k, start=True, stop=True)
                        last = mmul(ps[:, b, T:2 * T], q[:, P:T], k, start=True, stop=True)
                    last.then_inc(S("s_done"), 1)

                def transposes(u):
                    un = units[u]
                    b = 6 + u % 2
                    if u - 2 >= us[0]:
                        pe.wait_ge(S("pt_ready"), u - 1)
                    if un["cmp"] is not None:
                        for tt in range(TT):
                            last = tr(ps[0:NCMP, b, P * tt:P * tt + P], PC[:, tt, un["cmp"], :])
                    else:
                        pe.wait_ge(S("p_ready"), s_no[u])
                        p = pb[:, s_no[u] % 2, :]
                        order = [0, 1, 2] if un["causal"] else [0, 2, 1, 3]
                        for i, blk_ in enumerate(order):
                            last = tr(ps[:, b, P * i:P * i + P], p[:, P * blk_:P * blk_ + P])
                    last.then_inc(S("t_done"), 1)

                def values(u):
                    un = units[u]
                    b = 2 + un["o"] % 2
                    pe.wait_ge(S("pt_ready"), u + 1)
                    if un["start"] and un["o"] >= 2:
                        pe.wait_ge(S("o_evac"), un["o"] - 1)
                    o, pt, v = ps[un["rows"], b, 0:T], ptb[:, u % 2, :], un["v"]
                    if un["cmp"] is not None:
                        last = mmul(o, v, pt[0:NCMP, 0:T], start=False, stop=True, skip_group_check=True)
                    elif un["causal"]:
                        mmul(o, v[0], pt[:, 0:T], start=un["start"], stop=False, skip_group_check=True)
                        last = mmul(ps[un["rows"], b, P:T], v[1], pt[:, T:T + P], start=False, stop=un["stop"],
                                    skip_group_check=True)
                    else:
                        mmul(o, v[0], pt[:, 0:T], start=True, stop=False)
                        last = mmul(o, v[1], pt[:, T:2 * T], start=False, stop=True)
                    last.then_inc(S("v_done"), 1)

                pe.wait_ge(S("att_go"), {"diff": 1, "nsa": 2, "mla": 3, "gqa": 4}[name])
                scores(us[0])
                for i, u in enumerate(us):
                    if u in soft and s_no[u] < len(soft) and soft[s_no[u]] in us:
                        scores(soft[s_no[u]])
                    if i >= 1:
                        transposes(u - 1)
                    if i >= 2:
                        values(u - 2)
                    if ada and i in ADA_STEP:
                        ada_other(len(ADA_JOB) + ADA_STEP.index(i))
                transposes(us[-1])
                values(us[-2])
                values(us[-1])

            def to_tokens(src, count):
                for tt in range(TT):
                    for c in range(C):
                        last = tr(ps[:, 2 * tt + c // 4, P * (c % 4):P * (c % 4) + P], src[:, c, P * tt:P * tt + P])
                last.then_inc(S("tok_mm"), 1)

            def rank_of(sel, n, m):
                pe.wait_ge(S("sel_ready"), m + 1)
                mmul(ps[:, 5, 0:n], K("before"), sel[:, 0, :], start=True, stop=True)
                mmul(ps[:, 5, 64:64 + n], K("ones"), sel[:, 0, :], start=True, stop=False)
                return mmul(ps[:, 5, 64:64 + n], K("before"), sel[:, 1, :], start=False, stop=True)

            def router(m, src, n):
                for tt in range(TT):
                    for k in range(C):
                        if tt == 0:
                            pe.wait_ge(S("h_ready"), C * (2 * m + 1) + k + 1)
                        last = mmul(ps[:, 4, 64 * tt:64 * tt + n], src[:, k, P * tt:P * tt + P], wr[m][:, k, 0:n],
                                    start=(k == 0), stop=(k == C - 1 and m >= 2))
                    if m < 2:
                        last = mmul(ps[:, 4, 64 * tt:64 * tt + n], K("ones", 1), rows1[0:1, RB0 + 36 * m:RB0 + 36 * m + n],
                                    start=False, stop=True)
                last.then_inc(S("logits"), 1)

            def route1(m):
                router(m, hT, 36)
                to_tokens(hT, m)
                sel = rt_sel(E1)
                rank_of(sel, E1, m)
                mmul(ps[0:32, 5, 128:129], sel[:, 0, :], K("ones")[:, 0:1], start=True, stop=False)
                mmul(ps[0:32, 5, 128:129], sel[:, 1, :], K("ones")[:, 0:1], start=False, stop=True)\
                    .then_inc(S("rank_mm"), 1)
                pe.wait_ge(S("nblk_ready"), m + 1)
                mmul(ps[:, 5, 192:224], rt_nblkB, K("before")[0:32, 0:32], start=True, stop=True)
                mmul(ps[:, 5, 224:225], rt_nblkB, K("ones")[0:32, 0:1], start=True, stop=True)
                mmul(ps[0:32, 5, 226:227], K("before")[0:32, 0:32], rt_nblk, start=True, stop=True)\
                    .then_inc(S("base_mm"), 1)
                pe.wait_ge(S("cmp_ready"), m + 1)
                mmul(ps[0:1, 6, 0:E1_BLOCKS], K("ones")[0:32, 0:1], rt_cmp, start=True, stop=True)\
                    .then_inc(S("count_mm"), 1)

            def route2(m):
                values = list(span[f"value{m - 2}"])
                await_need(pe, ("job", values[0] - 1))
                router(m, xT, 16)
                to_tokens(xT, m)
                pe.wait_ge(S("tok_ready"), m + 1)
                project(values[:1])
                pe.wait_ge(S("aff_ready"), m - 1)
                for tt in range(TT):
                    last = tr(ps[0:E2, 6, P * tt:P * tt + P], affL[:, 0, tt, 0:E2])
                last.then_inc(S("affT_mm"), 1)
                project(values[1:3])
                pe.wait_ge(S("selT_ready"), m - 1)
                for tt in range(TT):
                    last = tr(ps[:, 6, 256 + 16 * tt:272 + 16 * tt], rt_selT[:, P * tt:P * tt + P], k=E2)
                last.then_inc(S("sel_mm"), 1)
                project(values[3:])
                rank_of(rt_sel(E2), E2, m).then_inc(S("rank_mm"), 1)

            def gather(chunks):
                for k in chunks:
                    for tt in range(TT):
                        last = mmul(ps[:, 4 + k // 4, P * (k % 4):P * (k % 4) + P], h_tok[:, tt, k::C],
                                    Dg[:, tt, :], start=(tt == 0), stop=(tt == 1))
                return last

            def experts1(m):
                n0, g0, x0, ff, per = slot_moe[m], moe_g0[m], gather_g0[m], E1_FF, 12
                nch = ff // P

                pe.wait_ge(S("tok_ready"), m + 1)
                pe.wait_ge(S("D_ready"), x0 + 1)
                gather(range(C)).then_inc(S("xg_mm"), 1)
                with pe.Fori(0, E1_GROUPS) as i:
                    def slot_in_group(s):
                        n = n0 + s
                        pe.wait_ge(S(f"slot{n % RING}"), 16 * i + 16 * (n // RING + 1))
                        return ring[:, n % RING, :]
                    for tt in range(TT):
                        last = tr(ps[:, 6, P * tt:P * tt + P], DAg[:, tt, :])
                    last.then_inc(S("C_mm"), 1)
                    pe.wait_ge(S("xg_ready"), i + (x0 + 1))
                    for a in range(2):
                        w = [slot_in_group(4 * a + j) for j in range(4)]
                        for k in range(C):
                            for j in range(4):
                                last = mmul(ps[32 * j:32 * j + 32, a, 0:ff], xg[:, k, 32 * j:32 * j + 32],
                                            w[j][:, ff * k:ff * k + ff], start=(k == 0), stop=(k == C - 1))
                                if k == C - 1:
                                    last.then_inc(S("slot_used"), 1)
                    pe.wait_ge(S("D_ready"), i + (x0 + 2))
                    pe.wait_ge(S("y_added"), i + (g0 + m + 1))
                    gather(range(C - 2))
                    pe.wait_ge(S("hid_ready"), i + (g0 + 1))
                    for c in range(nch):
                        last = tr(ps[:, 7, P * c:P * c + P], hid[:, c:ff:nch])
                    last.then_inc(S("hT_mm"), 1)
                    gather(range(C - 2, C)).then_inc(S("xg_mm"), 1)
                    pe.wait_ge(S("hidT_ready"), i + (g0 + 1))
                    pe.wait_ge(S("C_ready"), i + (g0 + 1))
                    w = [slot_in_group(8 + j) for j in range(4)]
                    for c in range(nch):
                        for h in range(2):
                            for j in range(4):
                                last = mmul(ps[32 * j:32 * j + 32, 6 + h, :], hidT[:, c, 32 * j:32 * j + 32],
                                            w[j][:, D * c + 512 * h:D * c + 512 * h + 512],
                                            start=(c == 0), stop=(c == nch - 1))
                                if c == nch - 1 and h == 1:
                                    last.then_inc(S("slot_used"), 1)
                    pe.wait_ge(S("xg_ready"), i + (x0 + 2))
                    for h in range(2):
                        pe.wait_ge(S(f"Y_ready{h}"), i + (g0 + 1))
                        for c in range(4 * h, 4 * h + 4):
                            last = mmul(ps[:, 2 + c // 2, T * (c % 2):T * (c % 2) + T], Yg[:, P * c:P * c + P],
                                        Cg[:, :], start=True, stop=True)
                    last.then_inc(S("y_mm"), 1)

            def experts2(m, part):
                first, groups, ff = E2_PARTS[part][0], len(E2_PARTS[part]), E2_FF
                kpack = SLOT // ff
                halves = max(1, ff // 512)
                width = min(ff, 512)
                nup, ndn = 8 // kpack, ff // 256
                per = 12 * (ff // 256)
                n0, g0, x0 = slot_part[m, part], moe_g0[m] + first, gather_g0[m] + first
                if part == 0:
                    pe.wait_ge(S("tok_ready"), m + 1)
                    pe.wait_ge(S("D_ready"), x0 + 1)
                    gather(range(C)).then_inc(S("xg_mm"), 1)
                before = gate_jobs(m - 2, part - 1) if part else span[f"value{m - 2}"]
                await_need(pe, ("job", before[-1]))
                with pe.Fori(0, groups) as i:
                    def slot_in_group(s):
                        n = n0 + s
                        pe.wait_ge(S(f"slot{n % RING}"), 16 * (per // RING) * i + 16 * (n // RING + 1))
                        return ring[:, n % RING, :]
                    for tt in range(TT):
                        last = tr(ps[:, 6, P * tt:P * tt + P], DAg[:, tt, :])
                    last.then_inc(S("C_mm"), 1)
                    pe.wait_ge(S("xg_ready"), i + (x0 + 1))
                    pe.wait_ge(S("y_added"), i + (g0 + m + 1))
                    s = 0
                    for kk in range(nup):
                        for a in range(2):
                            w = [slot_in_group(s + j) for j in range(4)]
                            for k2 in range(kpack):
                                k = kpack * kk + k2
                                for h in range(halves):
                                    for j in range(4):
                                        last = mmul(ps[32 * j:32 * j + 32, 2 * a + h, 0:width],
                                                    xg[:, k, 32 * j:32 * j + 32],
                                                    w[j][:, ff * k2 + width * h:ff * k2 + width * h + width],
                                                    start=(k == 0), stop=(k == C - 1))
                                        if k2 == kpack - 1 and h == halves - 1:
                                            last.then_inc(S("slot_used"), 1)
                            s += 4
                    pe.wait_ge(S("hid_ready"), i + (g0 + 1))
                    nch = ff // P
                    for c in range(nch):
                        last = tr(ps[:, 4 + c // 4, P * (c % 4):P * (c % 4) + P], hid[:, c:ff:nch])
                    last.then_inc(S("hT_mm"), 1)
                    pe.wait_ge(S("hidT_ready"), i + (g0 + 1))
                    pe.wait_ge(S("D_ready"), i + (x0 + 2))
                    gather(range(C)).then_inc(S("xg_mm"), 1)
                    pe.wait_ge(S("C_ready"), i + (g0 + 1))
                    for kk in range(ndn):
                        w = [slot_in_group(s + j) for j in range(4)]
                        for c2 in range(2):
                            c = 2 * kk + c2
                            for h in range(2):
                                for j in range(4):
                                    last = mmul(ps[32 * j:32 * j + 32, 6 + h, :], hidT[:, c, 32 * j:32 * j + 32],
                                                w[j][:, D * c2 + 512 * h:D * c2 + 512 * h + 512],
                                                start=(c == 0), stop=(c == nch - 1))
                                    if c2 == 1 and h == 1:
                                        last.then_inc(S("slot_used"), 1)
                        s += 4
                    for c in range(C):
                        if c % 4 == 0:
                            pe.wait_ge(S(f"Y_ready{c // 4}"), i + (g0 + 1))
                        last = mmul(ps[:, c // 2, T * (c % 2):T * (c % 2) + T], Yg[:, P * c:P * c + P], Cg[:, :],
                                    start=True, stop=True)
                    last.then_inc(S("y_mm"), 1)

            def gla_stage():
                pe.wait_ge(S("proj_evac"), acts_before[ev_lr] + 1)
                pe.wait_ge(S("o_evac"), o_after["mla"])
                for d in range(2):
                    for tt in range(TT):
                        mmul(ps[:, 4 + d, T * tt:T * tt + T], lrT[:, d, P * tt:P * tt + P], gw[:, d, :],
                             start=True, stop=False)
                        last = mmul(ps[:, 4 + d, T * tt:T * tt + T], K("ones", 1), rows1[0:1, GB0 + T * d:GB0 + T * d + T],
                                    start=False, stop=True)
                last.then_inc(S("gl_mm"), 1)
                for d in range(2):
                    pe.wait_ge(S("la_ready"), d + 1)
                    for c in range(2):
                        for tt in range(TT):
                            last = mmul(ps[:, 6 + d, T * c + P * tt:T * c + P * tt + P],
                                        la[d][:, tt, P * c:P * c + P], K("tri_f" if d == 0 else "tri_b"),
                                        start=True, stop=True)
                    last.then_inc(S("cum_mm"), 1)
                for d in range(2):
                    pe.wait_ge(S("qk_ready"), d + 1)
                    for h in range(4):
                        r = slice(64 * (h % 2), 64 * (h % 2) + 64)
                        for tt in range(TT):
                            tk = slice(P * tt, P * tt + P)
                            last = mmul(ps[:, 4 + 2 * d + h % 2, T * (h // 2) + P * tt:T * (h // 2) + P * tt + P],
                                        kg[d][r, h // 2, tk], qg[d][r, h // 2, tk], start=True, stop=True)
                    for c in range(2):
                        for tt in range(TT):
                            last = tr(ps[:, 2 + d, T * tt + P * c:T * tt + P * c + P], kd[d][:, c, P * tt:P * tt + P])
                    last.then_inc(S("at_mm"), 1)
                for d in range(2):
                    pe.wait_ge(S("at_ready"), d + 1)
                    for h in range(4):
                        c, half = h // 2, h % 2
                        for n in range(4):
                            tk = slice(64 * (n % 2), 64 * (n % 2) + 64)
                            last = mmul(ps[64 * half:64 * half + 64, 4 * d + n % 2,
                                           T * c + P * (n // 2):T * c + P * (n // 2) + P],
                                        kdt[d][tk, n // 2, 64 * h:64 * h + 64], gv[tk, n // 2, P * h:P * h + P],
                                        start=True, stop=True)
                    last.then_inc(S("u_mm"), 1)
                pe.wait_ge(S("st_ready"), 2)
                for h in range(4):
                    r, c = slice(64 * (h % 2), 64 * (h % 2) + 64), h // 2
                    for tt in range(TT):
                        o0 = T * (h // 2) + P * tt
                        for d in range(2):
                            mmul(ps[:, 6 + h % 2, o0:o0 + P], gv[:, tt, P * h:P * h + P],
                                 at[d][:, 4 * (h % 2) + 2 * (h // 2) + tt, :], start=(d == 0), stop=False,
                                 skip_group_check=True)
                        inter = [(d, n) for n in (2 * tt, 2 * tt + 1) for d in range(2)
                                 if not (d == 0 and n == 0) and not (d == 1 and n == 3)]
                        for x, (d, n) in enumerate(inter):
                            last = mmul(ps[:, 6 + h % 2, o0 + 64 * (n % 2):o0 + 64 * (n % 2) + 64],
                                        stt_[d][r, c, n, :], qg[d][r, c, 64 * n:64 * n + 64],
                                        start=False, stop=(x == len(inter) - 1), skip_group_check=True)
                    if h >= 2:
                        last.then_inc(S("go_mm"), 1)

            pe.wait_ge(S("consts"), 16)
            pe.wait_ge(S("x_in"), 16 * TT)
            for c in range(C):
                for tt in range(TT):
                    last = tr(ps[:, c // 2, T * (c % 2) + P * tt:T * (c % 2) + P * tt + P],
                              sq[:, 1024 * tt + P * c:1024 * tt + P * c + P])
            last.then_inc(S("xT_mm"), 1)
            pe.wait_ge(S("params"), 16 * N_PARAMS)
            for a in range(3):
                last = tr(ps[:, 4, P * a:P * a + P], rowsA[:, a, :])
            last.then_inc(S("cols_mm"), 1)
            pe.wait_ge(S("lam_ready"), 1)
            mmul(ps[:, 7, 0:1], K("ones", 1), misc[0:1, 8:9], start=True, stop=True).then_inc(S("lam_mm"), 1)
            norm(0)
            pe.wait_ge(S("cpad_ready"), 1)
            pe.wait_ge(S("x_ready"), 1)
            for p in range(ADA_FIRST):
                ada_part(p, ps[:, 0, T * p:T * p + T])
            pe.wait_ge(S("ada_evac"), 1)
            for b in range(2 * ADA_FIRST):
                last = tr(ps[:, 3, P * b:P * b + P], ada_rows01[:, P * b:P * b + P])
            last.then_inc(S("modT_mm"), 1)
            pe.wait_ge(S("p_in"), 32)
            for l in range(2):
                for k in range(2):
                    for tt in range(TT):
                        last = tr(ps[:, 5 + l, T * k + P * tt:T * k + P * tt + P],
                                  yT[:, 4 * l + tt, P * k:P * k + P])
            last.then_inc(S("p_mm"), 1)
            rope_limit[0] = r_nsa
            project(span["diff"])
            ropes_until(r_nsa)
            attention("diff", ada=True)
            pe.wait_ge(S("ada_evac"), 1 + len(ada_rows))
            pe.wait_ge(S("o_evac"), o_after["diff"])
            for x, rows in enumerate(ada_rows):
                for h in range(2):
                    last = tr(ps[:, (2, 3, 0, 1, 4)[x // 2], T * (x % 2) + P * h:T * (x % 2) + P * h + P],
                              rows[:, P * h:P * h + P])
            last.then_inc(S("modT_mm"), 1)
            partition_norms(0)
            pe.wait_ge(S("pn_done"), 4)
            pe.wait_ge(S("mod_ready"), 2)
            project(span["diff_out"])
            norm(1)
            pe.wait_ge(S("late_params"), 16 * N_LATE)
            route1(0)
            experts1(0)
            norm(2)
            rope_limit[0] = r_even
            project(range(ph["nsa"], nsa_w2))
            pe.wait_ge(S("proj_evac"), acts_before[nsa_w2])
            for t in range(2):
                for m in range(2):
                    for half in range(2):
                        last = mmul(ps[:, 6, 32 * (2 * t + m):32 * (2 * t + m) + 30], hpart[:, t, half, P * m:P * m + P],
                                    K("fold"), start=(half == 0), stop=(half == 1))
            last.then_inc(S("hsum_mm"), 1)
            project(range(nsa_w2, ph["nsa_out"]))
            ropes_until(r_even)
            pe.wait_ge(S("rope_done"), r_even)
            for i in range(2):
                for tt in range(TT):
                    last = tr(ps[:, 7, 256 * i + P * tt:256 * i + P * tt + P], kT[:, 4 + i, P * tt:P * tt + P])
            last.then_inc(S("vt_mm"), 1)
            pe.wait_ge(S("proj_evac"), acts_before[nsa_src["cmp"]] + 1)
            for tt in range(TT):
                for c in range(C):
                    o0 = 2 * NCMP * (C * tt + c)
                    last = mmul(ps[:, 4, o0:o0 + 2 * NCMP], qT[:, c, P * tt:P * tt + P],
                                kcmp[:, c // 4, :, :].rearrange("p e n -> p (e n)"), start=True, stop=True)
            last.then_inc(S("sc_mm"), 1)
            attention("nsa")
            pe.wait_ge(S("o_evac"), o_after["nsa"])
            project(span["nsa_out"])
            norm(3)
            route1(1)
            experts1(1)
            norm(4)
            rope_limit[0] = r_even
            project(range(ph["even"], ev_uq))
            partition_norms(1)
            rope_limit[0] = r_odd
            project(range(ev_uq, ph["even_out"]))
            ropes_until(r_odd)
            attention("mla")
            gla_stage()
            partition_norms(2)
            pe.wait_ge(S("pn_done"), 8)
            project(span["even_out"])
            norm(5)
            route2(2)
            for part in range(len(E2_PARTS)):
                experts2(2, part)
                if part < len(GATE_PARTS):
                    pe.wait_ge(S("y_added"), moe_g0[2] + E2_PARTS[part][-1] + 2 + 2)
                    project(gate_jobs(0, part))
            norm(6)
            rope_limit[0] = r_odd
            project(span["odd"])
            pn_sums(3)
            for s in range(6):
                pn_spread(8 + s)
                if s:
                    ropes_until(r_odd + s)
            ropes_until(r_end)
            attention("gqa")
            pe.wait_ge(S("o_evac"), o_after["gqa"])
            project(span["odd_out"])
            norm(7)
            route2(3)
            for part in range(len(E2_PARTS)):
                experts2(3, part)
                if part < len(GATE_PARTS):
                    pe.wait_ge(S("y_added"), moe_g0[3] + E2_PARTS[part][-1] + 3 + 2)
                    project(gate_jobs(1, part))
            norm(8)
            pe.wait_ge(S("h_ready"), 9 * C)
            to_tokens(xT, 4)

        @block.scalar
        def _(act):
            func = nc.scalar.activation
            chain = [0]

            def link(ins):
                chain[0] += 1
                ins.then_inc(S("act_chain"), 1)
                act.wait_ge(S("act_chain"), chain[0])

            def ada_row(x):
                act.wait_ge(S("slot_used"), ada_slot(ADA_FIRST + x, 3) + 1)
                func(ada_rows[x], ps[:, ada_bank(x), 0:T], ACT.Copy).then_inc(S("ada_evac"), 1)

            def evacuate(js):
                for j in js:
                    if j in ADA_JOB:
                        ada_row(ADA_JOB.index(j))
                    if jobs[j]["eng"] == "act":
                        act.wait_ge(S(finished(j)[0]), finished(j)[1])
                        jobs[j]["evac"](j % 2).then_inc(S("proj_evac"), 1)

            def roots(n):
                for a in range(4):
                    if n >= 5:
                        act.wait_ge(S("xc_ready"), 4 * (n - 5) + a + 1)
                    elif a == 0:
                        act.wait_ge(S("x_ready"), n + 1)
                    func(sq[:, 512 * a:512 * a + 512], pair_dst(xT, a), ACT.Square).then_inc(S("sq_ready"), 1)
                act.wait_ge(S("sq_mm"), n + 1)
                func(st[:, :], ps[:, 2, 0:T], ACT.Sqrt, bias=eps_col, scale=1.0 / D).then_inc(S("std_ready"), 1)

            def gain(n):
                if n < 2:
                    act.wait_ge(S("gain_ready"), n + 1)
                dst = hT if n < 4 else xT
                for c in range(C):
                    if c % 2 == 0:
                        act.wait_ge(S("xn_ready"), 4 * n + c // 2 + 1)
                    if n < 4:
                        l, a = n // 2, n % 2
                        last = func(dst[:, c, :], dst[:, c, :], ACT.Identity, scale=modA[:, n, c:c + 1],
                                    bias=mod[:, l, 24 * a + c:24 * a + c + 1])
                    elif n == 4:
                        last = func(dst[:, c, :], dst[:, c, :], ACT.Copy, scale=col("final_g", c))
                    else:
                        l, which = (n - 5) // 2, "ln1" if n % 2 else "ln2"
                        last = func(dst[:, c, :], dst[:, c, :], ACT.Identity, scale=col(which + "_g_2", 8 * l + c),
                                    bias=col(which + "_b_2", 8 * l + c))
                    last.then_inc(S("h_ready"), 1)

            def norm(n):
                roots(n)
                gain(n)

            def partition_norms(b):
                for i in pn_batch[b]:
                    srcs, need = pns[i][0], pns[i][4]
                    await_need(act, need)
                    if i >= 2:
                        act.wait_ge(S("pn_mm"), i - 1)
                    for a, s in enumerate(srcs):
                        n = s.shape[-1]
                        last = func(sqb[:, 512 * (i % 2) + n * a:512 * (i % 2) + n * a + n], s, ACT.Square)
                    last.then_inc(S("pn_sq"), 1)
                act.wait_ge(S("pn_mm"), pn_batch[b][-1] + 1)
                for size in sorted({pns[i][2] for i in pn_batch[b]}):
                    same = [i for i in pn_batch[b] if pns[i][2] == size]
                    cols = slice(pn_columns(same[0], 0, 0).start,
                                 pn_columns(same[-1], pns[same[-1]][0][0].shape[-1] // T - 1, TT - 1).stop)
                    last = func(pn[:, cols], ps[:, 7, cols], ACT.Sqrt, bias=eps_col, scale=1.0 / size)
                last.then_inc(S("pn_std"), 1)

            def attention(name, ada=False):
                us = list(u_span[name])

                def exps(u):
                    un = units[u]
                    if un["cmp"] is None:
                        act.wait_ge(S("nm_ready"), s_no[u])
                        if s_no[u] > 2:
                            act.wait_ge(S("t_done"), soft[s_no[u] - 3] + 1)
                        n0 = P if un["causal"] else T
                        b, p, m = 4 + s_no[u] % 2, pb[:, s_no[u] % 2, :], mx[:, s_no[u] % 2, :]
                        func(p[:, 0:n0], ps[:, b, 0:n0], ACT.Exp, bias=m[:, 2:3], scale=un["scale"],
                             accum_out=m[:, 4:5])
                        func(p[:, n0:n0 + T], ps[:, b, n0:n0 + T], ACT.Exp, bias=m[:, 3:4], scale=un["scale"],
                             accum_out=m[:, 5:6]).then_inc(S("exp_done"), 1)

                def move(u):
                    un = units[u]
                    act.wait_ge(S("t_done"), u + 1)
                    if u - 2 >= us[0]:
                        act.wait_ge(S("v_done"), u - 1)
                    if un["cmp"] is not None:
                        src, dst = ps[0:NCMP, 6 + u % 2, 0:T], ptb[0:NCMP, u % 2, 0:T]
                    else:
                        n = 384 if un["causal"] else 512
                        src, dst = ps[:, 6 + u % 2, 0:n], ptb[:, u % 2, 0:n]
                    func(dst, src, ACT.Copy).then_inc(S("pt_ready"), 1)

                moved = us[0]
                for i, u in enumerate(us):
                    if u not in soft:
                        continue
                    exps(u)
                    for x in range(moved, u):
                        move(x)
                    moved = u
                    if ada and i - 1 in ADA_STEP:
                        ada_row(len(ADA_JOB) + ADA_STEP.index(i - 1))
                for x in range(moved, us[-1] + 1):
                    move(x)

            def route1(m):
                act.wait_ge(S("gmax_ready"), m + 1)
                for tt in range(TT):
                    last = func(rt_e[:, 4 * tt:4 * tt + 4], rt_lg[:, tt, 0:4], ACT.Exp, bias=rt_c[:, tt:tt + 1],
                                accum_out=rt_c[:, 2 + tt:3 + tt])
                last.then_inc(S("gsum_ready"), 1)
                act.wait_ge(S("v10_ready"), m + 1)
                func(rt_c[:, 6:8], rt_c[:, 4:6], ACT.Exp).then_inc(S("e1_ready"), 1)

            def tokens(m):
                act.wait_ge(S("tok_mm"), m + 1)
                func(h_tok[:, :, :].rearrange("p a d -> p (a d)"), psf(0, 4), ACT.Copy).then_inc(S("tok_ready"), 1)

            def route2(m):
                act.wait_ge(S("amax_ready"), m - 1)
                for tt in range(TT):
                    last = func(affL[:, 0, tt, 0:E2], ps[:, 4, 64 * tt:64 * tt + E2], ACT.Exp, bias=rt_c[:, tt:tt + 1],
                                accum_out=rt_c[:, 2 + tt:3 + tt])
                last.then_inc(S("asum_ready"), 1)

            def outputs(h, last_slot):
                act.wait_ge(S("slot_used"), last_slot)
                func(Yg[:, 512 * h:512 * h + 512], ps[:, 6 + h, :], ACT.Copy).then_inc(S(f"Y_ready{h}"), 1)

            def experts1(m):
                g0, x0, n0, ff, per = moe_g0[m], gather_g0[m], slot_moe[m], E1_FF, 12
                xf = xg[:, :, :].rearrange("p k s -> p (k s)")
                act.wait_ge(S("xg_mm"), x0 + 1)
                func(xf, psf(4, 2), ACT.Copy).then_inc(S("xg_ready"), 1)
                with act.Fori(0, E1_GROUPS) as i:
                    act.wait_ge(S("C_mm"), i + (g0 + 1))
                    func(Cg[:, :], ps[:, 6, 0:T], ACT.Copy).then_inc(S("C_ready"), 1)
                    act.wait_ge(S("slot_used"), per * i + (n0 + 4))
                    func(sg[:, 0:ff], ps[:, 0, 0:ff], ACT.Silu).then_inc(S("sg_ready"), 1)
                    act.wait_ge(S("xg_mm"), i + (x0 + 2))
                    func(xf, psf(4, 2), ACT.Copy).then_inc(S("xg_ready"), 1)
                    for h in range(2):
                        outputs(h, per * i + (n0 + per))

            def experts2(m, part):
                first, groups, ff = E2_PARTS[part][0], len(E2_PARTS[part]), E2_FF
                g0, x0, n0, per = moe_g0[m] + first, gather_g0[m] + first, slot_part[m, part], 12 * (ff // 256)
                xf = xg[:, :, :].rearrange("p k s -> p (k s)")
                if part == 0:
                    act.wait_ge(S("xg_mm"), x0 + 1)
                    func(xf, psf(4, 2), ACT.Copy).then_inc(S("xg_ready"), 1)
                with act.Fori(0, groups) as i:
                    act.wait_ge(S("C_mm"), i + (g0 + 1))
                    func(Cg[:, :], ps[:, 6, 0:T], ACT.Copy).then_inc(S("C_ready"), 1)
                    act.wait_ge(S("slot_used"), per * i + (n0 + 2 * per // 3))
                    func(sg[:, :], psf(0, 2), ACT.Silu).then_inc(S("sg_ready"), 1)
                    act.wait_ge(S("xg_mm"), i + (x0 + 2))
                    func(xf, psf(4, 2), ACT.Copy).then_inc(S("xg_ready"), 1)
                    for h in range(2):
                        outputs(h, per * i + (n0 + per))

            def gla_stage():
                act.wait_ge(S("gl_mm"), 1)
                func(lnb[0], psf(4), ACT.Abs)
                link(func(lnb[1], psf(5), ACT.Abs))
                func(lnb[0], lnb[0], ACT.Exp, scale=-1.0)
                link(func(lnb[1], lnb[1], ACT.Exp, scale=-1.0))
                for d in range(2):
                    func(lnb[d], lnb[d], ACT.Ln, bias=1.0).then_inc(S("ln_ready"), 1)
                for d in range(2):
                    act.wait_ge(S("cum_mm"), d + 1)
                    func(gE[d][0], ps[:, 6 + d, :], ACT.Exp, scale=1.0 / 16.0)
                    func(gE[d][1], ps[:, 6 + d, :], ACT.Exp, scale=-1.0 / 16.0).then_inc(S("e_ready"), 1)
                for d in range(2):
                    act.wait_ge(S("diff_ready"), d + 1)
                    func(gE[d][2], gE[d][2], ACT.Exp, scale=1.0 / 16.0).then_inc(S("el_ready"), 1)

            act.wait_ge(S("xT_mm"), 1)
            func(xT[:, :, :].rearrange("p c t -> p (c t)"), psf(0, 4), ACT.Copy).then_inc(S("x_ready"), 1)
            act.wait_ge(S("cols_mm"), 1)
            func(colsA[:, :, :].rearrange("p a n -> p (a n)"), ps[:, 4, 0:384], ACT.Copy).then_inc(S("cols_ready"), 1)
            act.wait_ge(S("cols_ready"), 1)
            act.wait_ge(S("cpad_zero"), 1)
            func(cpad[:, :, 0], colsA[:, 1, 0:8], ACT.Silu).then_inc(S("cpad_ready"), 1)
            act.wait_ge(S("lam_sum"), 1)
            func(misc[0:1, 4:6], misc[0:1, 2:4], ACT.Exp).then_inc(S("lam_exp"), 1)
            act.wait_ge(S("ang_ready"), 1)
            func(cosd[:, :, :].rearrange("p a t -> p (a t)"), cosd[:, :, :].rearrange("p a t -> p (a t)"), ACT.Sin)\
                .then_inc(S("cos_ready"), 1)
            roots(0)
            act.wait_ge(S("slot_used"), 4 * ADA_FIRST)
            func(ada_rows01, ps[:, 0, :], ACT.Copy).then_inc(S("ada_evac"), 1)
            gain(0)
            act.wait_ge(S("p_mm"), 1)
            func(pTall[:, :, :, :].rearrange("p l k t -> p (l k t)"), psf(5, 2), ACT.Copy).then_inc(S("pT_ready"), 1)
            evacuate(span["diff"])
            attention("diff", ada=True)
            partition_norms(0)
            norm(1)
            tokens(0)
            route1(0)
            experts1(0)
            norm(2)
            evacuate(range(ph["nsa"], nsa_w2))
            act.wait_ge(S("hsum_mm"), 1)
            act.wait_ge(S("kcmp_zero"), 1)
            for t in range(2):
                for m in range(2):
                    last = func(gh[:, t, m, :], ps[:, 6, 32 * (2 * t + m):32 * (2 * t + m) + 30], ACT.Gelu_apprx_tanh,
                                bias=col("nsa_cmp_b1", 2 * t + m))
            last.then_inc(S("gelu"), 1)
            evacuate(range(nsa_w2, ph["nsa_out"]))
            act.wait_ge(S("vt_mm"), 1)
            func(vt[:, 0:512], ps[:, 7, :], ACT.Copy).then_inc(S("vt_ready"), 1)
            act.wait_ge(S("sc_sub"), 1)
            for tt in range(TT):
                last = func(PC[:, tt, :, :], PC[:, tt, :, :], ACT.Exp, scale=0.125)
            last.then_inc(S("sc_exp"), 1)
            attention("nsa")
            norm(3)
            tokens(1)
            route1(1)
            experts1(1)
            norm(4)
            evacuate(range(ph["even"], ev_uq))
            partition_norms(1)
            evacuate(range(ev_uq, ph["even_out"]))
            attention("mla")
            gla_stage()
            partition_norms(2)
            norm(5)
            tokens(2)
            route2(2)
            evacuate(span["value0"])
            for part in range(len(E2_PARTS)):
                experts2(2, part)
                if part < len(GATE_PARTS):
                    evacuate(gate_jobs(0, part))
            norm(6)
            evacuate(span["odd"])
            partition_norms(3)
            attention("gqa")
            norm(7)
            tokens(3)
            route2(3)
            evacuate(span["value1"])
            for part in range(len(E2_PARTS)):
                experts2(3, part)
                if part < len(GATE_PARTS):
                    evacuate(gate_jobs(1, part))
            norm(8)
            act.wait_ge(S("tok_mm"), 5)
            for tt in range(TT):
                func(h_tok[:, tt, :], psf(2 * tt, 2), ACT.Copy).then_inc(S("out_ready"), 1)

        @block.vector
        def _(dve):
            V = nc.vector
            chain = [0]

            def link(ins):
                chain[0] += 1
                ins.then_inc(S("dve_chain"), 1)
                dve.wait_ge(S("dve_chain"), chain[0])

            def scale(n):
                def pairs(dst, op):
                    for a in range(4):
                        b = st[:, :].rearrange("p (o t) -> p o t", o=1).to_broadcast([P, 2, T])
                        yield V.tensor_tensor(dst[:, 2 * a:2 * a + 2, :], xT[:, 2 * a:2 * a + 2, :], b, op)

                if n >= 5:
                    dve.wait_ge(S("mean_mm"), n - 4)
                    link(V.tensor_scalar(st[:, :], ps[:, 3, 0:T], 1.0 / D, None, ALU.mult))
                    for ins in pairs(xT, ALU.subtract):
                        ins.then_inc(S("xc_ready"), 1)
                dve.wait_ge(S("std_ready"), n + 1)
                link(V.reciprocal(st[:, :], st[:, :]))
                for ins in pairs(hT if n < 4 else xT, ALU.mult):
                    ins.then_inc(S("xn_ready"), 1)

            def norm(n):
                scale(n)
                dve.wait_ge(S("h_ready"), C * (n + 1))

            rope_at = [0]

            def ropes_until(end):
                while rope_at[0] < end:
                    i = rope_at[0]
                    buf, n, r0, rows, _, cos, sin, _ = ropes[i]
                    rr = slice(r0, r0 + rows)
                    b3 = buf[rr, :].rearrange("p (c t) -> p c t", c=n)
                    t3 = rtmp[rr, 0:n * T].rearrange("p (c t) -> p c t", c=n)
                    p3 = ps[rr, 2 + i % 2, 0:n * T].rearrange("p (c t) -> p c t", c=n)
                    cb = cos[rr, :].rearrange("p (o t) -> p o t", o=1).to_broadcast([rows, n, T])
                    sb_ = sin[rr, :].rearrange("p (o t) -> p o t", o=1).to_broadcast([rows, n, T])
                    dve.wait_ge(S("rope_mm"), i + 1)
                    V.tensor_tensor(t3, p3, sb_, ALU.mult)
                    link(V.tensor_tensor(b3, b3, cb, ALU.mult))
                    V.tensor_tensor(b3, b3, t3, ALU.add).then_inc(S("rope_done"), 1)
                    dve.wait_ge(S("rope_done"), i + 1)
                    rope_at[0] += 1

            def pn_inverse(b):
                dve.wait_ge(S("pn_std"), b + 1)
                r = pn[:, 0:pn_width(pn_batch[b])]
                V.reciprocal(r, r).then_inc(S("pn_inv"), 1)

            def partition_norm(i):
                srcs, _, _, apply, _ = pns[i]
                n = srcs[0].shape[-1]
                dve.wait_ge(S("pn_sp"), i + 1)
                for src, c, dst, times in apply:
                    last = V.scalar_tensor_tensor(dst, src, c, ps[:, 5 + i % 2, 0:n], ALU.mult, ALU.mult)
                    if times is not None:
                        link(last)
                        last = V.tensor_tensor(dst, dst, times, ALU.mult)
                last.then_inc(S("pn_done"), 1)
                dve.wait_ge(S("pn_done"), i + 1)

            def partition_norms(b):
                pn_inverse(b)
                for i in pn_batch[b]:
                    partition_norm(i)

            def attention(name):
                us = list(u_span[name])

                def neg_max(u):
                    un = units[u]
                    if un["cmp"] is not None:
                        return
                    dve.wait_ge(S("s_done"), s_no[u])
                    b, m = 4 + s_no[u] % 2, mx[:, s_no[u] % 2, :]
                    if un["causal"]:
                        V.tensor_reduce(m[:, 0:1], ps[:, b, 0:P], AX, ALU.max)
                        link(V.tensor_reduce(m[:, 1:2], ps[:, b, P:P + T], AX, ALU.max))
                    else:
                        link(V.tensor_reduce(m[:, 0:2], ps[:, b, :].rearrange("p (a n) -> p a n", a=2), AX, ALU.max))
                    V.tensor_scalar(m[:, 2:4], m[:, 0:2], -un["scale"], None, ALU.mult).then_inc(S("nm_ready"), 1)

                def normalise(u):
                    un = units[u]
                    if un["cmp"] is not None:
                        return
                    dve.wait_ge(S("exp_done"), s_no[u])
                    m, p, n0 = mx[:, s_no[u] % 2, :], pb[:, s_no[u] % 2, :], P if un["causal"] else T
                    link(V.reciprocal(m[:, 6:8], m[:, 4:6]))
                    if un["coef"] is not None:
                        link(V.tensor_tensor(m[:, 6:8], m[:, 6:8], un["coef"], ALU.mult))
                    V.tensor_scalar(p[:, 0:n0], p[:, 0:n0], m[:, 6:7], None, ALU.mult)
                    V.tensor_scalar(p[:, n0:n0 + T], p[:, n0:n0 + T], m[:, 7:8], None, ALU.mult)\
                        .then_inc(S("p_ready"), 1)

                def outputs(u):
                    un = units[u]
                    if un["last"]:
                        dve.wait_ge(S("v_done"), u + 1)
                        V.tensor_copy(obanks[un["o"]], ps[:, 2 + un["o"] % 2, 0:T]).then_inc(S("o_evac"), 1)

                mine = [u for u in us if u in soft]
                left = us[0]
                for i, u in enumerate(mine):
                    neg_max(u)
                    if i >= 1:
                        normalise(mine[i - 1])
                    for x in range(left, u - 2):
                        outputs(x)
                    left = max(left, u - 2)
                normalise(mine[-1])
                for x in range(left, us[-1] + 1):
                    outputs(x)
                dve.wait_ge(S("o_evac"), o_after[name])

            def residual(name, gate=None):
                for j in span[name]:
                    s, r = jobs[j]["evac"], res_no[j]
                    dve.wait_ge(S(finished(j)[0]), finished(j)[1])
                    if gate is not None:
                        for a in range(2):
                            c = 2 * s + a
                            last = V.scalar_tensor_tensor(xT[:, c, :], ps[:, j % 2, T * a:T * a + T],
                                                          mod[:, gate, 16 + c:17 + c], xT[:, c, :], ALU.mult, ALU.add)
                    else:
                        last = V.scalar_tensor_tensor(pair_dst(xT, s), pair_dst(xT, s), ALPHA, ps[:, j % 2, :],
                                                      ALU.mult, ALU.add)
                    last.then_inc(S("res_evac"), 1)
                dve.wait_ge(S("res_evac"), r + 1)
                V.memset(misc[:, 60:61], 0.0).then_inc(S("x_ready"), 1)

            def route1(m):
                for_sel = rt_sel(E1)
                dve.wait_ge(S("logits"), m + 1)
                for tt in range(TT):
                    V.tensor_copy(rt_lg[:, tt, :], ps[:, 4, 64 * tt:64 * tt + 36])
                link(V.memset(rt_g8[:, :, :], -NEG))
                for tt in range(TT):
                    last = V.tensor_copy(rt_g8[:, tt, 0:4], rt_lg[:, tt, 0:4])
                link(last)
                for tt in range(TT):
                    link(V.max(rt_m8[:, tt, :], rt_g8[:, tt, :]))
                    last = V.max_index(i8[:, 0, tt, :], rt_m8[:, tt, :], rt_g8[:, tt, :])
                link(last)
                V.tensor_scalar(rt_c[:, 0:2], rt_m8[:, :, 0], -1.0, None, ALU.mult).then_inc(S("gmax_ready"), 1)
                link(V.tensor_copy(rt_c[:, 8:10], i8[:, 0, :, 0]))
                for tt in range(TT):
                    link(V.tensor_scalar(rt_oh4[:, tt, :], iota[:, 0:4], rt_c[:, 8 + tt:9 + tt], None, ALU.is_equal))
                    msk = rt_oh4[:, tt, :].rearrange("p (g o) -> p g o", o=1).to_broadcast([P, 4, 8])
                    le = rt_lg[:, tt, 4:36].rearrange("p (g e) -> p g e", g=4)
                    lm = rt_le[:, tt, :].rearrange("p (g e) -> p g e", g=4)
                    link(V.tensor_tensor(lm, le, msk, ALU.mult))
                    link(V.tensor_scalar(rt_oh4[:, tt, :], rt_oh4[:, tt, :], NEG, -NEG, ALU.mult, ALU.add))
                    link(V.tensor_tensor(lm, lm, msk, ALU.add))
                    link(V.max(rt_m8[:, tt, :], rt_le[:, tt, :]))
                    last = V.max_index(i8[:, 1, tt, :], rt_m8[:, tt, :], rt_le[:, tt, :])
                link(last)
                V.tensor_tensor(rt_c[:, 4:6], rt_m8[:, :, 1], rt_m8[:, :, 0], ALU.subtract).then_inc(S("v10_ready"), 1)
                V.tensor_copy(rt_c[:, 10:12], i8[:, 1, :, 0])
                link(V.tensor_copy(rt_c[:, 12:14], i8[:, 1, :, 1]))
                for tt in range(TT):
                    for a in range(2):
                        link(V.tensor_scalar(rt_oh[:, a, tt, :], iota[:, 0:E1], rt_c[:, 10 + 2 * a + tt:11 + 2 * a + tt],
                                             None, ALU.is_equal))
                V.tensor_tensor(for_sel, rt_oh[:, 0, :, :], rt_oh[:, 1, :, :], ALU.add).then_inc(S("sel_ready"), 1)
                dve.wait_ge(S("gsum_ready"), m + 1)
                dve.wait_ge(S("e1_ready"), m + 1)
                link(V.tensor_scalar(rt_c[:, 14:16], rt_c[:, 6:8], 1.0, None, ALU.add))
                link(V.tensor_tensor(rt_c[:, 14:16], rt_c[:, 14:16], rt_c[:, 2:4], ALU.mult))
                link(V.reciprocal(Lw[:, 2, :], rt_c[:, 14:16]))
                link(V.tensor_tensor(Lw[:, 3, :], Lw[:, 2, :], rt_c[:, 6:8], ALU.mult))
                dve.wait_ge(S("rank_mm"), m + 1)
                link(V.tensor_copy(rt_c[0:32, 16:17], ps[0:32, 5, 128:129]))
                link(V.tensor_scalar(rt_t8, iota[0:32, 0:8], float(BLK), rt_c[0:32, 16:17], ALU.mult, ALU.is_lt))
                link(V.tensor_reduce(rt_nblk, rt_t8, AX, ALU.add))
                V.tensor_scalar(rt_nblkB, K("ones")[0:32, :], rt_nblk, None, ALU.mult).then_inc(S("nblk_ready"), 1)
                dve.wait_ge(S("base_mm"), m + 1)
                link(V.tensor_copy(rt_base, ps[:, 5, 192:227]))
                V.tensor_scalar(rt_cmp, iota[0:32, 0:E1_BLOCKS], rt_base[0:32, 34:35], None, ALU.is_ge)\
                    .then_inc(S("cmp_ready"), 1)
                dve.wait_ge(S("count_mm"), m + 1)
                V.tensor_scalar(ids[0:1, 0, :], ps[0:1, 6, 0:E1_BLOCKS], -1.0, None, ALU.add)
                link(V.tensor_copy(rt_count, ps[0:1, 6, 0:E1_BLOCKS]))
                link(V.tensor_tensor(rt_new[:, 1:E1_BLOCKS], rt_count[:, 1:E1_BLOCKS], rt_count[:, 0:E1_BLOCKS - 1],
                                     ALU.not_equal))
                link(V.memset(rt_new[:, 0:E1_BLOCKS:E1_GROUPS], 1.0))
                V.scalar_tensor_tensor(ids[0:1, 1, :], iota[0:1, 0:E1_BLOCKS], rt_base[0:1, 32:33], rt_new,
                                       ALU.is_lt, ALU.mult).then_inc(S("ids_ready"), 1)
                for tt in range(TT):
                    link(V.scalar_tensor_tensor(rt_L[:, tt, :], rt_base[:, 0:E1], float(BLK), ps[:, 5, 64 * tt:64 * tt + E1],
                                                ALU.mult, ALU.add))
                for a in range(2):
                    link(V.tensor_tensor(rt_oh[:, a, :, :], rt_oh[:, a, :, :], rt_L[:, :, :], ALU.mult))
                    link(V.tensor_reduce(Lw[:, a, :], rt_oh[:, a, :, :], AX, ALU.add))
                V.memset(yT[:, :, :], 0.0).then_inc(S("y_added"), 1)
                link(V.tensor_copy(iog[:, :], K("slots")))

            def route2(m):
                V.memset(yT[:, :, :], 0.0).then_inc(S("y_added"), 1)
                dve.wait_ge(S("logits"), m + 1)
                lg = ps[:, 4, 0:128].rearrange("p (a n) -> p a n", a=TT)[:, :, 0:E2]
                link(V.tensor_reduce(rt_c[:, 4:6], lg, AX, ALU.max))
                V.tensor_scalar(rt_c[:, 0:2], rt_c[:, 4:6], -1.0, None, ALU.mult).then_inc(S("amax_ready"), 1)
                dve.wait_ge(S("asum_ready"), m - 1)
                link(V.reciprocal(rt_c[:, 4:6], rt_c[:, 2:4]))
                for tt in range(TT):
                    last = V.tensor_scalar(affL[:, 0, tt, 0:E2], affL[:, 0, tt, 0:E2], rt_c[:, 4 + tt:5 + tt], None, ALU.mult)
                last.then_inc(S("aff_ready"), 1)
                dve.wait_ge(S("affT_mm"), m - 1)
                link(V.tensor_copy(rt_selT, ps[0:E2, 6, 0:T]))
                for r in range(2 * T // E2 // 8):
                    link(V.max(rt_m8e, rt_selT))
                    link(V.match_replace(rt_selT, rt_m8e, rt_selT, -1.0))
                V.tensor_scalar(rt_selT, rt_selT, 0.0, None, ALU.is_lt).then_inc(S("selT_ready"), 1)
                dve.wait_ge(S("sel_mm"), m - 1)
                sel = rt_sel(E2)
                V.tensor_copy(sel, ps[:, 6, 256:288].rearrange("p (a n) -> p a n", a=TT)).then_inc(S("sel_ready"), 1)
                dve.wait_ge(S("sel_ready"), m + 1)
                dve.wait_ge(S("rank_mm"), m + 1)
                rk = ps[:, 5, 0:128].rearrange("p (a n) -> p a n", a=TT)[:, :, 0:E2]
                link(V.scalar_tensor_tensor(affL[:, 1, :, 0:E2], rk, 1.0, sel, ALU.add, ALU.mult))
                link(V.tensor_scalar(affL[:, 1, :, 0:E2], affL[:, 1, :, 0:E2], -1.0, None, ALU.add))

            def dispatch(link):
                for tt in range(TT):
                    link(V.tensor_scalar(Dg[:, tt, :], iog[:, :], Lw[:, 0, tt:tt + 1], None, ALU.is_equal))
                    V.scalar_tensor_tensor(Dg[:, tt, :], iog[:, :], Lw[:, 1, tt:tt + 1], Dg[:, tt, :],
                                           ALU.is_equal, ALU.add)
                    V.tensor_scalar(DAg[:, tt, :], iog[:, :], Lw[:, 0, tt:tt + 1], Lw[:, 2, tt:tt + 1],
                                    ALU.is_equal, ALU.mult)
                    link(V.tensor_scalar(rtmp[:, 0:P], iog[:, :], Lw[:, 1, tt:tt + 1], Lw[:, 3, tt:tt + 1],
                                         ALU.is_equal, ALU.mult))
                    link(V.tensor_tensor(DAg[:, tt, :], DAg[:, tt, :], rtmp[:, 0:P], ALU.add))
                V.tensor_scalar(iog[:, :], iog[:, :], float(BLK), None, ALU.add).then_inc(S("D_ready"), 1)

            def experts1(m):
                g0, x0, ff = moe_g0[m], gather_g0[m], E1_FF
                dispatch(link)
                base, n_links = chain[0], 3 * TT
                with dve.Fori(0, E1_GROUPS) as i:
                    at_link = [0]

                    def llink(ins):
                        at_link[0] += 1
                        ins.then_inc(S("dve_chain"), 1)
                        dve.wait_ge(S("dve_chain"), n_links * i + (base + at_link[0]))

                    dve.wait_ge(S("D_ready"), i + (x0 + 1))
                    dve.wait_ge(S("xg_mm"), i + (x0 + 1))
                    dve.wait_ge(S("C_mm"), i + (g0 + 1))
                    dispatch(llink)
                    assert at_link[0] == n_links, at_link[0]
                    dve.wait_ge(S("sg_ready"), i + (g0 + 1))
                    dve.wait_ge(S("slot_used"), 12 * i + (slot_moe[m] + 8))
                    V.tensor_tensor(hid[:, 0:ff], sg[:, 0:ff], ps[:, 1, 0:ff], ALU.mult).then_inc(S("hid_ready"), 1)
                    dve.wait_ge(S("hT_mm"), i + (g0 + 1))
                    V.tensor_copy(hidT[:, 0:ff // P, :].rearrange("p c s -> p (c s)"), ps[:, 7, 0:ff])\
                        .then_inc(S("hidT_ready"), 1)
                    dve.wait_ge(S("y_mm"), i + (g0 + 1))
                    dve.wait_ge(S("y_added"), i + (g0 + m + 1))
                    V.tensor_tensor(yT[:, :, :].rearrange("p c t -> p (c t)"), yT[:, :, :].rearrange("p c t -> p (c t)"),
                                    psf(2, 4), ALU.add).then_inc(S("y_added"), 1)
                chain[0] += n_links * E1_GROUPS
                dve.wait_ge(S("y_added"), g0 + E1_GROUPS + m + 1)
                for c in range(C):
                    last = V.scalar_tensor_tensor(xT[:, c, :], yT[:, c, :], mod[:, m, 40 + c:41 + c], xT[:, c, :],
                                                  ALU.mult, ALU.add)
                last.then_inc(S("x_ready"), 1)
                dve.wait_ge(S("x_ready"), 2 * m + 3)

            def dispatch2(e, link):
                for tt in range(TT):
                    d3 = Dg[:, tt, :].rearrange("p (j s) -> p j s", j=4)
                    io = iota[:, 0:32].rearrange("p (o s) -> p o s", o=1).to_broadcast([P, 4, 32])
                    lp, af = [affL[:, a, tt, bass.ds(e, 4)].rearrange("p (j o) -> p j o", o=1).to_broadcast([P, 4, 32])
                              for a in (1, 0)]
                    link(V.tensor_tensor(d3, io, lp, ALU.is_equal))
                    last = V.tensor_tensor(DAg[:, tt, :].rearrange("p (j s) -> p j s", j=4), d3, af, ALU.mult)
                last.then_inc(S("D_ready"), 1)

            def experts2(m, part):
                first, groups, ff = E2_PARTS[part][0], len(E2_PARTS[part]), E2_FF
                g0, x0 = moe_g0[m] + first, gather_g0[m] + first
                if part == 0:
                    dispatch2(0, link)
                base = [chain[0]]

                with dve.Fori(0, groups) as i:
                    n_links = 2
                    at_link = [0]

                    def llink(ins):
                        at_link[0] += 1
                        ins.then_inc(S("dve_chain"), 1)
                        dve.wait_ge(S("dve_chain"), n_links * i + (base[0] + at_link[0]))

                    dve.wait_ge(S("D_ready"), i + (x0 + 1))
                    dve.wait_ge(S("xg_mm"), i + (x0 + 1))
                    dve.wait_ge(S("C_mm"), i + (g0 + 1))
                    dispatch2(4 * i + 4 * (first + 1), llink)
                    dve.wait_ge(S("sg_ready"), i + (g0 + 1))
                    V.tensor_tensor(hid, sg[:, :], psf(2, 2), ALU.mult).then_inc(S("hid_ready"), 1)
                    dve.wait_ge(S("hT_mm"), i + (g0 + 1))
                    V.tensor_copy(hidT[:, 0:ff // P, :].rearrange("p c s -> p (c s)"),
                                  psf(4, 2)[:, 0:ff]).then_inc(S("hidT_ready"), 1)
                    dve.wait_ge(S("y_mm"), i + (g0 + 1))
                    dve.wait_ge(S("y_added"), i + (g0 + m + 1))
                    V.tensor_tensor(yT[:, :, :].rearrange("p c t -> p (c t)"), yT[:, :, :].rearrange("p c t -> p (c t)"),
                                    psf(0, 4), ALU.add).then_inc(S("y_added"), 1)
                assert at_link[0] == n_links, at_link[0]
                chain[0] += n_links * groups
                dve.wait_ge(S("y_added"), g0 + groups + m + 1)

            def embedding(m, part):
                for a in GATE_PARTS[part]:
                    dve.wait_ge(S("proj_evac"), acts_before[ph[f"gate{m - 2}"] + a] + 1)
                    link(V.tensor_tensor(pair_dst(kT, a), pair_dst(kT, a), pair_dst(hT, a), ALU.mult))
                    last = V.tensor_tensor(pair_dst(yT, a), pair_dst(yT, a), pair_dst(kT, a), ALU.add)
                link(last)

            def second_sum(m):
                V.scalar_tensor_tensor(xT[:, :, :], xT[:, :, :], ALPHA, yT[:, :, :], ALU.mult, ALU.add)\
                    .then_inc(S("x_ready"), 1)
                dve.wait_ge(S("x_ready"), 2 * m + 3)

            def gla_stage():
                for d in range(2):
                    dve.wait_ge(S("ln_ready"), d + 1)
                    V.scalar_tensor_tensor(la[d].rearrange("p a n -> p (a n)"), psf(4 + d), 0.0, lnb[d],
                                           ALU.min, ALU.subtract).then_inc(S("la_ready"), 1)
                for d in range(2):
                    dve.wait_ge(S("e_ready"), d + 1)
                    last_tok = 63 if d == 0 else 0
                    cum = ps[:, 6 + d, :].rearrange("p (n l) -> p n l", l=64)
                    link(V.tensor_copy(gdec[d][:, 0, :], cum[:, :, last_tok]))
                    lb = gdec[d][:, 0, :].rearrange("p (n o) -> p n o", o=1).to_broadcast([P, 8, 64])
                    V.tensor_copy(gdec[d][:, 1, :], gE[d][0].rearrange("p (n l) -> p n l", l=64)[:, :, last_tok])
                    V.tensor_tensor(gE[d][2].rearrange("p (n l) -> p n l", l=64), lb, cum, ALU.subtract)\
                        .then_inc(S("diff_ready"), 1)
                    qf, kf = gqT.rearrange("p c t -> p (c t)"), gkT.rearrange("p c t -> p (c t)")
                    V.scalar_tensor_tensor(qg[d].rearrange("p c t -> p (c t)"), qf, 0.125, gE[d][0], ALU.mult, ALU.mult)
                    V.tensor_tensor(kg[d].rearrange("p c t -> p (c t)"), kf, gE[d][1], ALU.mult)
                    dve.wait_ge(S("el_ready"), d + 1)
                    V.tensor_tensor(kd[d].rearrange("p c t -> p (c t)"), kf, gE[d][2], ALU.mult)\
                        .then_inc(S("qk_ready"), 1)
                for d in range(2):
                    dve.wait_ge(S("at_mm"), d + 1)
                    V.tensor_copy(kdt[d].rearrange("p a n -> p (a n)"), ps[:, 2 + d, :])
                    tri = K("tri_f" if d == 0 else "tri_b").rearrange("p (o n) -> p o n", o=1).to_broadcast([P, 8, P])
                    V.tensor_tensor(at[d], psf(4 + 2 * d, 2).rearrange("p (a n) -> p a n", a=8), tri, ALU.mult)\
                        .then_inc(S("at_ready"), 1)
                for d in range(2):
                    dve.wait_ge(S("u_mm"), d + 1)
                    order = [1, 2, 3] if d == 0 else [2, 1, 0]
                    for x, n in enumerate(order):
                        prev = n - 1 if d == 0 else n + 1
                        for c in range(2):
                            u0 = T * c + P * (prev // 2)
                            u = ps[:, 4 * d + prev % 2, u0:u0 + P]
                            if x == 0:
                                last = V.tensor_copy(stt_[d][:, c, n, :], u)
                            else:
                                last = V.scalar_tensor_tensor(stt_[d][:, c, n, :], stt_[d][:, c, prev, :],
                                                              gdec[d][:, 1, 4 * c + prev:4 * c + prev + 1], u,
                                                              ALU.mult, ALU.add)
                        if x < 2:
                            link(last)
                    last.then_inc(S("st_ready"), 1)
                for s in range(2):
                    dve.wait_ge(S("go_mm"), s + 1)
                    V.tensor_copy(oT[:, 4 + s:8:2, :], ps[:, 6 + s, :].rearrange("p (c t) -> p c t", c=2))\
                        .then_inc(S("gla_evac"), 1)
                dve.wait_ge(S("gla_evac"), 2)

            def ada_vectors(l, i0, n, src, count):
                dve.wait_ge(S("modT_mm"), count)
                for h in range(2):
                    v = src.rearrange("p (i h x) -> p i h x", h=2, x=P)[:, :, h, 0:P:32]
                    dst = mod[:, l, 8 * i0:8 * i0 + 8 * n].rearrange("p (i j h) -> p i j h", i=n, h=2)[:, :, :, h]
                    b_ = colsA[:, 0, 48 * l + 8 * i0:48 * l + 8 * i0 + 8 * n]\
                        .rearrange("p (i j h) -> p i j h", i=n, h=2)[:, :, :, h]
                    last = V.tensor_tensor(dst, v, b_, ALU.add)
                ada_calls[0] += 1
                last.then_inc(S("ada_add"), 1)
                dve.wait_ge(S("ada_add"), ada_calls[0])
                if ada_calls[0] in (1, 4):
                    V.memset(misc[:, 56:57], 0.0).then_inc(S("mod_ready"), 1)

            ada_calls = [0]

            def modulation(n):
                l, a = n // 2, n % 2
                link(V.scalar_tensor_tensor(modA[:, n, :], mod[:, l, 24 * a + 8:24 * a + 16], 1.0,
                                            colsA[:, 0, 96 + 8 * n:104 + 8 * n], ALU.add, ALU.mult))

            V.memset(affL[:, :, :, E2:E2 + 4], -1.0)
            V.memset(eps_col, EPS)
            V.memset(cpad[:, :, :], 0.0).then_inc(S("cpad_zero"), 1)
            dve.wait_ge(S("consts"), 16)
            V.tensor_copy(identb[:, :], ident)
            V.tensor_copy(trib[:, :], K("tri_neg"))
            dve.wait_ge(S("params"), 16 * N_PARAMS)
            pos = cosd[:, 1, :]
            link(V.tensor_copy(pos, posi))
            link(V.tensor_scalar(pos, pos, K("inv_freq"), None, ALU.mult))
            two_pi = 2.0 * math.pi
            hi = 6.28125
            lo = two_pi - hi
            magic = 1.5 * 2.0 ** 23
            for a, (shift, add) in enumerate(((0.25, math.pi / 2), (0.0, 0.0))):
                n, r = pn[:, 0:T], cosd[:, a, :]
                link(V.tensor_scalar(n, pos, 1.0 / two_pi, shift, ALU.mult, ALU.add))
                link(V.tensor_scalar(n, n, magic, None, ALU.add))
                link(V.tensor_scalar(n, n, -magic, None, ALU.add))
                link(V.scalar_tensor_tensor(r, n, -hi, pos, ALU.mult, ALU.add))
                link(V.scalar_tensor_tensor(r, n, -lo, r, ALU.mult, ALU.add))
                link(V.tensor_scalar(r, r, add, 3.1415925, ALU.add, ALU.min))
                link(V.tensor_scalar(r, r, -3.1415925, None, ALU.max))
            V.memset(misc[:, 59:60], 0.0).then_inc(S("ang_ready"), 1)
            lam = rows1[0:1, LAM0:LAM0 + 256].rearrange("p (a b d) -> p a b d", a=2, b=2)
            pr = rows1[0:1, 840:968].rearrange("p (a d) -> p a d", a=2)
            link(V.tensor_tensor(pr, lam[:, :, 0, :], lam[:, :, 1, :], ALU.mult))
            V.tensor_reduce(misc[0:1, 2:4], pr, AX, ALU.add).then_inc(S("lam_sum"), 1)
            dve.wait_ge(S("lam_exp"), 1)
            link(V.tensor_tensor(misc[0:1, 8:9], misc[0:1, 5:6], misc[0:1, 4:5], ALU.subtract))
            V.tensor_scalar(misc[0:1, 8:9], misc[0:1, 8:9], -LAMBDA_INIT, None, ALU.add).then_inc(S("lam_ready"), 1)
            dve.wait_ge(S("lam_mm"), 1)
            V.tensor_copy(coef[:, 0:1], ps[:, 7, 0:1])
            V.tensor_copy(coef[:, 1:2], ps[:, 7, 0:1])
            dve.wait_ge(S("cols_ready"), 1)
            link(V.tensor_scalar(coef[:, 2:3], col("diff_subln_g"), 1.0 - LAMBDA_INIT, None, ALU.mult))
            scale(0)
            ada_vectors(0, 0, ADA_FIRST, ps[:, 3, :], 1)
            modulation(0)
            V.memset(misc[:, 55:56], 0.0).then_inc(S("gain_ready"), 1)
            dve.wait_ge(S("cos_ready"), 1)
            dve.wait_ge(S("h_ready"), C)
            ropes_until(r_nsa)
            dve.wait_ge(S("proj_evac"), acts_before[ph["diff_out"]])
            V.memset(misc[:, 58:59], 0.0).then_inc(S("att_go"), 1)
            attention("diff")
            partition_norms(0)
            ada_vectors(0, 2, 4, psf(2, 2), 2)
            ada_vectors(1, 0, 4, psf(0, 2), 2)
            ada_vectors(1, 4, 2, ps[:, 4, :], 2)
            for a in range(1, 4):
                modulation(a)
            V.memset(misc[:, 55:56], 0.0).then_inc(S("gain_ready"), 1)
            residual("diff_out", gate=0)
            norm(1)
            route1(0)
            experts1(0)
            norm(2)
            ropes_until(r_even)
            V.memset(blk[:, :, :, 2 * NCMP:32], 0.0)
            V.memset(kcmp, 0.0).then_inc(S("kcmp_zero"), 1)
            dve.wait_ge(S("proj_evac"), acts_before[nsa_src["c1"]] + 1)
            for t in range(2):
                for g in range(2):
                    kc = kcp[t][:, g, :]
                    win = bass.AP(kc.tensor, kc.offset, [list(kc.ap[0]), [1, 16], [8, NCMP]])
                    last = V.tensor_tensor(blk[:, t, :, NCMP * g:NCMP * g + NCMP], win,
                                           colsA[:, 2, 16 * t:16 * t + 16].rearrange("p (j o) -> p j o", o=1)
                                           .to_broadcast([P, 16, NCMP]), ALU.add)
            last.then_inc(S("blk_ready"), 1)
            link(V.tensor_scalar(rt[:, 400:430], K("cmp_ok"), NEG, -NEG, ALU.mult, ALU.add))
            dve.wait_ge(S("sc_mm"), 1)
            neg = rt[:, 400:430].rearrange("p (a o n) -> p a o n", a=TT, o=1)
            okb = K("cmp_ok").rearrange("p (a o n) -> p a o n", a=TT, o=1)
            for tt in range(TT):
                s = ps[:, 4, 16 * NCMP * tt:16 * NCMP * (tt + 1)].rearrange("p (h n) -> p h n", h=16)
                last = V.tensor_tensor(PC[:, tt, :, :], s, neg[:, tt].to_broadcast([P, 16, NCMP]), ALU.add)
            link(last)
            PCf = PC.rearrange("p a h n -> p (a h) n")
            link(V.tensor_reduce(rt[:, 440:472], PCf, AX, ALU.max))
            V.tensor_tensor(PCf, PCf, rt[:, 440:472].rearrange("p (h o) -> p h o", o=1).to_broadcast([P, 32, NCMP]),
                            ALU.subtract).then_inc(S("sc_sub"), 1)
            dve.wait_ge(S("sc_exp"), 1)
            for tt in range(TT):
                last = V.tensor_tensor(PC[:, tt, :, :], PC[:, tt, :, :], okb[:, tt].to_broadcast([P, 16, NCMP]), ALU.mult)
            link(last)
            link(V.tensor_reduce(rt[:, 440:472], PCf, AX, ALU.add))
            link(V.tensor_scalar(rt[:, 440:472], rt[:, 440:472], 1e-30, None, ALU.max))
            link(V.reciprocal(rt[:, 480:512], rt[:, 440:472]))
            link(V.tensor_tensor(rt[:, 480:512].rearrange("p (a h) -> p a h", a=TT),
                                 rt[:, 480:512].rearrange("p (a h) -> p a h", a=TT), gates[:, :, 0:48:3], ALU.mult))
            link(V.tensor_tensor(PCf, PCf, rt[:, 480:512].rearrange("p (h o) -> p h o", o=1)
                                 .to_broadcast([P, 32, NCMP]), ALU.mult))
            dve.wait_ge(S("vt_ready"), 1)
            V.memset(misc[:, 58:59], 0.0).then_inc(S("att_go"), 1)
            attention("nsa")
            residual("nsa_out", gate=1)
            norm(3)
            route1(1)
            experts1(1)
            norm(4)
            partition_norms(1)
            ropes_until(r_odd)
            dve.wait_ge(S("proj_evac"), acts_before[ph["even_out"]])
            V.tensor_copy(kT[64:96, :, :], kpe[64:96, :].rearrange("p (o t) -> p o t", o=1).to_broadcast([32, C, T]))\
                .then_inc(S("att_go"), 1)
            attention("mla")
            gla_stage()
            partition_norms(2)
            residual("even_out")
            norm(5)
            route2(2)
            for part in range(len(E2_PARTS)):
                experts2(2, part)
                if part < len(GATE_PARTS):
                    embedding(2, part)
            second_sum(2)
            norm(6)
            pn_inverse(3)
            for s in range(6):
                partition_norm(8 + s)
                if s:
                    ropes_until(r_odd + s)
            ropes_until(r_end)
            dve.wait_ge(S("proj_evac"), acts_before[ph["odd_out"]])
            V.memset(misc[:, 58:59], 0.0).then_inc(S("att_go"), 1)
            attention("gqa")
            residual("odd_out")
            norm(7)
            route2(3)
            for part in range(len(E2_PARTS)):
                experts2(3, part)
                if part < len(GATE_PARTS):
                    embedding(3, part)
            second_sum(3)
            norm(8)

        @block.gpsimd
        def _(pool):
            nc.gpsimd.memset(rowsA[:, :, :], 0.0).then_inc(S("rows_zero"), 1)


_INS = ["x", "c", "positions", "ada_w", "ada_b", "norm_g", "final_g", "diff_w_in", "diff_w_out", "diff_lambda",
        "diff_subln_g", "nsa_w_in", "nsa_w_out", "nsa_cmp_pos", "nsa_cmp_w1", "nsa_cmp_b1", "nsa_cmp_w2",
        "moe_w_group", "moe_b_group", "moe_w_expert", "moe_b_expert", "moe_w_gate", "moe_w_up", "moe_w_down",
        "p_2", "w_in_even_2", "mla_q_norm_2", "w_uq_2", "mla_kv_norm_2", "w_ukv_2", "gla_gate_w_fwd_2",
        "gla_gate_b_fwd_2", "gla_gate_w_bwd_2", "gla_gate_b_bwd_2", "gla_norm_2", "w_in_odd_2", "gqa_q_norm_2",
        "gqa_k_norm_2", "w_o_2", "ln1_g_2", "ln1_b_2", "router_w_2", "w1_2", "w3_2", "w2_2", "ple_gate_w_2",
        "ple_gate_b_2", "ple_w_2", "ln2_g_2", "ln2_b_2"]


def kernel(**inputs):
    import concourse.bacc as _bacc
    from concourse.bass_utils import run_bass_kernel_spmd as _run

    nc = _bacc.Bacc("TRN2", target_bir_lowering=False, num_devices=1)
    arrays, args = {}, {}
    for name in _INS + ["consts"]:
        a = np.ascontiguousarray(inputs[name] if name != "consts" else shape_constants())
        arrays[f"in_{name}"] = a
        args[name] = nc.dram_tensor(f"in_{name}", a.shape, mybir.dt.from_np(a.dtype), kind="ExternalInput").ap()
    out = nc.dram_tensor("out_0", (1, T, D), F32, kind="ExternalOutput").ap()
    program(nc, args, out)
    r = _run(nc, [arrays], core_ids=[0])
    return r.results[0]["out_0"]
```
